# Optimizing a Trainium2 kernel written in Bass

```python
import jax, jax.numpy as jnp
from jax import lax
import numpy as np

D_MODEL = 1024
BATCH = 1
SEQ = 256
DEPTH = 1
DEC_BATCH = 8
DEC_SEQ = 8
PAST_LEN = 2048
PAGE_SIZE = 128

N_BRANCH = 4
BRANCH_W = D_MODEL // 4
POOL_WINDOWS = (2, 4, 8, 16)
POOL_GROUPS = len(POOL_WINDOWS)
POOL_GW = BRANCH_W // POOL_GROUPS
POOL_HIST = max(POOL_WINDOWS) - 1
CONF_WIDTH = 31
CONF_HIST = CONF_WIDTH - 1
SCONV_WIDTH = 3
SCONV_HIST = SCONV_WIDTH - 1
CHUNK = 128
SGU_HEADS = 4
SGU_HW = BRANCH_W // SGU_HEADS
N_GROUPS = 4
EXPERTS_PER_GROUP = 8
N_EXPERTS = N_GROUPS * EXPERTS_PER_GROUP
TOP_K = 2
D_EXPERT = D_MODEL // 4
RMS_EPS = 1e-6
LN_EPS = 1e-5
COLS = (BRANCH_W, 2 * BRANCH_W, 3 * BRANCH_W, 2 * BRANCH_W, N_BRANCH * D_MODEL)
IN_COLS = sum(COLS)
SPLITS = [sum(COLS[:i + 1]) for i in range(len(COLS) - 1)]

kernel_name = 'hybrid_pool_conv_sgu_hmoe_step'

def rmsnorm(x, g):
    xf = x.astype(jnp.float32)
    y = xf * lax.rsqrt(jnp.mean(xf * xf, axis=-1, keepdims=True) + RMS_EPS)
    return (y * g.astype(jnp.float32)).astype(x.dtype)

def layernorm(x, g, b):
    xf = x.astype(jnp.float32)
    mu = jnp.mean(xf, axis=-1, keepdims=True)
    xc = xf - mu
    y = xc * lax.rsqrt(jnp.mean(xc * xc, axis=-1, keepdims=True) + LN_EPS)
    return (y * g.astype(jnp.float32) + b.astype(jnp.float32)).astype(x.dtype)

def causal_dwconv(ext, w):
    c = ext.shape[-1]
    return lax.conv_general_dilated(ext, w.astype(ext.dtype)[:, None, :], window_strides=(1,), padding='VALID', dimension_numbers=('NWC', 'WIO', 'NWC'), feature_group_count=c)

def pool_mixer(a, prev, start_pos, pool_w, pool_scale):
    bsz, t, c = a.shape
    ext = jnp.concatenate([prev.astype(a.dtype), a], axis=1)
    cs = jnp.concatenate([jnp.zeros((bsz, 1, c), jnp.float32), jnp.cumsum(ext.astype(jnp.float32), axis=1)], axis=1)
    end = cs[:, POOL_HIST + 1:]
    pos = start_pos + jnp.arange(t)
    means = []
    for gi, w in enumerate(POOL_WINDOWS):
        sl = slice(gi * POOL_GW, (gi + 1) * POOL_GW)
        begin = cs[:, POOL_HIST + 1 - w:POOL_HIST + 1 - w + t, sl]
        cnt = jnp.minimum(pos + 1, w).astype(jnp.float32)[None, :, None]
        means.append((end[..., sl] - begin) / cnt)
    pooled = (jnp.concatenate(means, axis=-1) - a.astype(jnp.float32)).astype(a.dtype)
    pooled = pooled.reshape(bsz, t, POOL_GROUPS, POOL_GW)
    mixed = jnp.einsum('btgc,gcd->btgd', pooled, pool_w).reshape(bsz, t, c)
    return mixed * pool_scale, ext[:, -POOL_HIST:]

def chunk_spatial_mix(v, ws, b):
    bsz, t, c = v.shape
    L = min(t, CHUNK)
    n = -(-t // L)
    vp = jnp.pad(v, ((0, 0), (0, n * L - t), (0, 0))).reshape(bsz, n, L, SGU_HEADS, SGU_HW)
    mask = jnp.tril(jnp.ones((L, L), dtype=bool))
    w = jnp.where(mask[None], ws[:, :L, :L], 0)
    s = jnp.einsum('hts,bnshc->bnthc', w, vp) + jnp.transpose(b[:, :L])[None, None, :, :, None]
    return s.reshape(bsz, n * L, c)[:, :t]

def token_mixer(xn, pool_prev, conv_prev, sconv_prev, start_pos, w_in, pool_w, pool_scale, conf_dw, conf_dw_b, conf_ln_g, conf_ln_b, sconv_w, sgu_ln_g, sgu_ln_b, sgu_ws, sgu_b, w_branch, w_out):
    proj = jnp.einsum('btd,df->btf', xn, w_in)
    a_pool, a_conf, a_sc, a_sgu, a_gate = jnp.split(proj, SPLITS, axis=-1)
    br_a, pool_new = pool_mixer(a_pool, pool_prev, start_pos, pool_w, pool_scale)
    g_lin, g_gate = jnp.split(a_conf, 2, axis=-1)
    glu = g_lin * jax.nn.sigmoid(g_gate)
    ext_b = jnp.concatenate([conv_prev.astype(glu.dtype), glu], axis=1)
    cb = causal_dwconv(ext_b, conf_dw) + conf_dw_b
    br_b = jax.nn.silu(layernorm(cb, conf_ln_g, conf_ln_b))
    b_gate, c_gate, h_in = jnp.split(a_sc, 3, axis=-1)
    z = c_gate * h_in
    ext_c = jnp.concatenate([sconv_prev.astype(z.dtype), z], axis=1)
    br_c = b_gate * causal_dwconv(ext_c, sconv_w)
    u, v = jnp.split(jax.nn.gelu(a_sgu), 2, axis=-1)
    v = layernorm(v, sgu_ln_g, sgu_ln_b)
    br_d = u * chunk_spatial_mix(v, sgu_ws, sgu_b)
    t = v.shape[1]
    v_new = v[:, ((t - 1) // CHUNK) * CHUNK:]
    merged = None
    for i, br in enumerate((br_a, br_b, br_c, br_d)):
        gate = jax.nn.sigmoid(a_gate[..., i * D_MODEL:(i + 1) * D_MODEL])
        term = gate * jnp.einsum('btc,cd->btd', br, w_branch[i])
        merged = term if merged is None else merged + term
    out = jnp.einsum('btd,de->bte', merged, w_out)
    return out, pool_new, ext_b[:, -CONF_HIST:], ext_c[:, -SCONV_HIST:], v_new

def hier_moe(xn, router_g, router_g_b, router_e, router_e_b, w_gate, w_up, w_down):
    bsz, t, d = xn.shape
    x2 = xn.reshape(-1, d)
    xf = x2.astype(jnp.float32)
    lg = xf @ router_g.astype(jnp.float32) + router_g_b.astype(jnp.float32)
    pg = jax.nn.softmax(lg, axis=-1)
    gsel = jnp.argmax(lg, axis=-1)
    pg_sel = jnp.take_along_axis(pg, gsel[:, None], axis=1)[:, 0]
    le = (xf @ router_e.astype(jnp.float32) + router_e_b.astype(jnp.float32)).reshape(-1, N_GROUPS, EXPERTS_PER_GROUP)
    le_g = jnp.take_along_axis(le, gsel[:, None, None], axis=1)[:, 0]
    tv, ti = lax.top_k(le_g, TOP_K)
    tw = jax.nn.softmax(tv, axis=-1) * pg_sel[:, None]
    eidx = gsel[:, None] * EXPERTS_PER_GROUP + ti
    cw = jnp.sum(jax.nn.one_hot(eidx, N_EXPERTS, dtype=jnp.float32) * tw[..., None], axis=1)
    cw = cw.astype(xn.dtype).reshape(-1, N_GROUPS, EXPERTS_PER_GROUP)
    out = jnp.zeros_like(x2)
    for g in range(N_GROUPS):
        sl = slice(g * EXPERTS_PER_GROUP, (g + 1) * EXPERTS_PER_GROUP)
        ha = jnp.einsum('nd,edf->nef', x2, w_gate[sl])
        hb = jnp.einsum('nd,edf->nef', x2, w_up[sl])
        hh = jax.nn.silu(ha) * hb * cw[:, g, :, None]
        out = out + jnp.einsum('nef,efd->nd', hh, w_down[sl])
    return out.reshape(bsz, t, d)

def trunk(x, pool_prev, conv_prev, sconv_prev, start_pos, p):
    h = x
    pools, convs, sconvs, vs = [], [], [], []
    for l in range(DEPTH):
        xn = rmsnorm(h, p['norm1_g'][l])
        mix, pn, cn, sn, vn = token_mixer(xn, pool_prev[l], conv_prev[l], sconv_prev[l], start_pos, p['w_in'][l], p['pool_w'][l], p['pool_scale'][l], p['conf_dw'][l], p['conf_dw_b'][l], p['conf_ln_g'][l], p['conf_ln_b'][l], p['sconv_w'][l], p['sgu_ln_g'][l], p['sgu_ln_b'][l], p['sgu_ws'][l], p['sgu_b'][l], p['w_branch'][l], p['w_out'][l])
        h = h + mix
        h = h + hier_moe(rmsnorm(h, p['norm2_g'][l]), p['router_g'][l], p['router_g_b'][l], p['router_e'][l], p['router_e_b'][l], p['w_gate'][l], p['w_up'][l], p['w_down'][l])
        pools.append(pn); convs.append(cn); sconvs.append(sn); vs.append(vn)
    y = rmsnorm(h, p['final_g'])
    return y, jnp.stack(pools), jnp.stack(convs), jnp.stack(sconvs), jnp.stack(vs)

def setup_inputs(seed: int = 0) -> dict:
    key = jax.random.key(seed)
    ks = jax.random.split(key, 32)
    f32 = jnp.float32

    def nrm(k, shape, s):
        return jax.random.normal(k, shape, f32) * s

    return {
        'x_prompt': nrm(ks[0], (BATCH, SEQ, D_MODEL), 1.0),
        'x_sample': nrm(ks[1], (DEC_BATCH, DEC_SEQ, D_MODEL), 1.0),
        'state_pool': nrm(ks[2], (DEPTH, DEC_BATCH, POOL_HIST, BRANCH_W), 1.0),
        'state_conv': nrm(ks[3], (DEPTH, DEC_BATCH, CONF_HIST, BRANCH_W), 0.5),
        'state_sconv': nrm(ks[4], (DEPTH, DEC_BATCH, SCONV_HIST, BRANCH_W), 0.5),
        'norm1_g': 1.0 + nrm(ks[5], (DEPTH, D_MODEL), 0.02),
        'w_in': nrm(ks[6], (DEPTH, D_MODEL, IN_COLS), D_MODEL ** -0.5),
        'pool_w': nrm(ks[7], (DEPTH, POOL_GROUPS, POOL_GW, POOL_GW), POOL_GW ** -0.5),
        'pool_scale': 1.0 + nrm(ks[8], (DEPTH, BRANCH_W), 0.02),
        'conf_dw': nrm(ks[9], (DEPTH, CONF_WIDTH, BRANCH_W), CONF_WIDTH ** -0.5),
        'conf_dw_b': nrm(ks[10], (DEPTH, BRANCH_W), 0.02),
        'conf_ln_g': 1.0 + nrm(ks[11], (DEPTH, BRANCH_W), 0.02),
        'conf_ln_b': nrm(ks[12], (DEPTH, BRANCH_W), 0.02),
        'sconv_w': nrm(ks[13], (DEPTH, SCONV_WIDTH, BRANCH_W), SCONV_WIDTH ** -0.5),
        'sgu_ln_g': 1.0 + nrm(ks[14], (DEPTH, BRANCH_W), 0.02),
        'sgu_ln_b': nrm(ks[15], (DEPTH, BRANCH_W), 0.02),
        'sgu_ws': nrm(ks[16], (DEPTH, SGU_HEADS, CHUNK, CHUNK), CHUNK ** -0.5),
        'sgu_b': 1.0 + nrm(ks[17], (DEPTH, SGU_HEADS, CHUNK), 0.02),
        'w_branch': nrm(ks[18], (DEPTH, N_BRANCH, BRANCH_W, D_MODEL), BRANCH_W ** -0.5),
        'w_out': nrm(ks[19], (DEPTH, D_MODEL, D_MODEL), D_MODEL ** -0.5),
        'norm2_g': 1.0 + nrm(ks[20], (DEPTH, D_MODEL), 0.02),
        'router_g': nrm(ks[21], (DEPTH, D_MODEL, N_GROUPS), D_MODEL ** -0.5),
        'router_g_b': nrm(ks[22], (DEPTH, N_GROUPS), 0.01),
        'router_e': nrm(ks[23], (DEPTH, D_MODEL, N_EXPERTS), D_MODEL ** -0.5),
        'router_e_b': nrm(ks[24], (DEPTH, N_EXPERTS), 0.01),
        'w_gate': nrm(ks[25], (DEPTH, N_EXPERTS, D_MODEL, D_EXPERT), D_MODEL ** -0.5),
        'w_up': nrm(ks[26], (DEPTH, N_EXPERTS, D_MODEL, D_EXPERT), D_MODEL ** -0.5),
        'w_down': nrm(ks[27], (DEPTH, N_EXPERTS, D_EXPERT, D_MODEL), D_EXPERT ** -0.5),
        'final_g': 1.0 + nrm(ks[28], (D_MODEL,), 0.02),
    }

def reference(x_prompt, x_sample, state_pool, state_conv, state_sconv, norm1_g, w_in, pool_w, pool_scale, conf_dw, conf_dw_b, conf_ln_g, conf_ln_b, sconv_w, sgu_ln_g, sgu_ln_b, sgu_ws, sgu_b, w_branch, w_out, norm2_g, router_g, router_g_b, router_e, router_e_b, w_gate, w_up, w_down, final_g):
    p = dict(norm1_g=norm1_g, w_in=w_in, pool_w=pool_w, pool_scale=pool_scale, conf_dw=conf_dw, conf_dw_b=conf_dw_b, conf_ln_g=conf_ln_g, conf_ln_b=conf_ln_b, sconv_w=sconv_w, sgu_ln_g=sgu_ln_g, sgu_ln_b=sgu_ln_b, sgu_ws=sgu_ws, sgu_b=sgu_b, w_branch=w_branch, w_out=w_out, norm2_g=norm2_g, router_g=router_g, router_g_b=router_g_b, router_e=router_e, router_e_b=router_e_b, w_gate=w_gate, w_up=w_up, w_down=w_down, final_g=final_g)
    bp = x_prompt.shape[0]
    zp = jnp.zeros((DEPTH, bp, POOL_HIST, BRANCH_W), x_prompt.dtype)
    zc = jnp.zeros((DEPTH, bp, CONF_HIST, BRANCH_W), x_prompt.dtype)
    zs = jnp.zeros((DEPTH, bp, SCONV_HIST, BRANCH_W), x_prompt.dtype)
    y_prompt, pool_p, conv_p, sconv_p, sguv_p = trunk(x_prompt, zp, zc, zs, 0, p)
    y_sample, pool_s, conv_s, sconv_s, sguv_s = trunk(x_sample, state_pool, state_conv, state_sconv, PAST_LEN, p)
    return (y_prompt, y_sample, pool_p, conv_p, sconv_p, sguv_p, pool_s, conv_s, sconv_s, sguv_s)


_drawn_inputs = setup_inputs


def setup_inputs(seed=0):
    import zlib

    import numpy as np

    out = dict(_drawn_inputs(seed))
    spreads = {}
    factors = {'pool_scale': 15.051,
     'conf_dw_b': 3.316,
     'conf_ln_g': 17.544,
     'conf_ln_b': 20.642,
     'sgu_ln_g': 24.609,
     'sgu_ln_b': 25.663,
     'sgu_b': 21.979,
     'router_g_b': 14.148,
     'router_e_b': 23.484,
     'final_g': 20.255,
     'norm2_g': 5.073,
     'state_sconv': 4.581}
    for name, (base, spread) in spreads.items():
        noise = np.random.default_rng([zlib.crc32(name.encode()), seed]).standard_normal(out[name].shape)
        drawn = base * np.exp(spread * noise) if base else spread * noise
        out[name] = __import__('jax').numpy.asarray(drawn.astype(out[name].dtype))
    for name, factor in factors.items():
        out[name] = (out[name] * factor).astype(out[name].dtype)
    return out
```

```python
from contextlib import ExitStack

import concourse.bass as bass
from concourse import mybir

F32 = mybir.dt.float32
F32R = mybir.dt.float32r
I32 = mybir.dt.int32
ALU = mybir.AluOpType
ACT = mybir.ActivationFunctionType
AX_X = mybir.AxisListType.X

P = 128
D = 1024
KT = D // P
NPR, NB, NS = 256, 8, 8
NSM = NB * NS
T = NPR + NSM
TILES = ((0, 128), (128, 128), (256, 64))
NT = len(TILES)
BW = 256
CT = BW // P
NBR = 4
HP, HC, HS = 15, 30, 2
CW, SW = 31, 3
WINDOWS = (2, 4, 8, 16)
NG, EG = 4, 8
NE = NG * EG
PAIRS = NE // 2
F = 256
FK = F // P
CAP = 64
CH = 256
N_PROJ = 2048 // CH
N_GATE = NBR * D // CH
N_OUT = D // CH
TAIL = 96
BIG = 1.0e6
RMS_EPS, LN_EPS = 1e-6, 1e-5
LP = HP + NPR
LC = HC + NPR
LS = HS + NPR
EP, EC, ES = LP + NB * (HP + NS), LC + NB * (HC + NS), LS + NB * (HS + NS)
PRM = dict(dw=0, dwb=31, lng=32, lnb=33, sw=34, vg=37, vb=38, ps=39)
NPRM = 40


def build(nc, a, o):
    ctx = ExitStack()
    sems = {}

    def sb(name, shape, dt=F32, stack=ctx):
        return stack.enter_context(nc.sbuf_tensor(name, shape, dt))

    def sem(name):
        if name not in sems:
            sems[name] = ctx.enter_context(nc.semaphore(name))
        return sems[name]

    class Steps:

        def __init__(self, eng, name):
            self.eng, self.sem, self.n = eng, sem(name), 0

        def step(self, ins):
            self.n += 1
            ins.then_inc(self.sem, 1)

        def last(self):
            self.eng.wait_ge(self.sem, self.n)

    xn2_dram = nc.dram_tensor("xn2_rows", (T, D), F32).ap()
    rec_dram = nc.dram_tensor("slot_records", (NE * CAP, 4), F32).ap()
    y_dram = nc.dram_tensor("expert_rows", (2 * T, D), F32).ap()
    tail_dram = nc.dram_tensor("state_tail_rows", (3, NSM, BW), F32).ap()

    x_tok = sb("x_tok", [P, NT, D])
    ident = sb("ident", [P, P])
    before = sb("before", [P, P])
    ones = sb("ones", [P, P])
    mean_w = sb("mean_w", [P, P])
    g2b = sb("g2b", [P, D])
    gfb = sb("gfb", [P, D])
    rg = sb("rg", [P, KT, NG])
    re = sb("re", [P, KT, NE])
    rw = sb("rw", [P, KT, NG + NE])
    rb = sb("rb", [P, NG + NE])
    ss = sb("ss", [P, NT])
    ms = sb("ms", [P, NT])
    root = sb("root", [P, NT])
    rstd = sb("rstd", [P, NT])
    epsb = sb("epsb", [P, 1])
    banks = [ctx.enter_context(nc.psum_tensor(f"bank{i}", [P, 512], F32)) for i in range(8)]

    mixer = ExitStack()

    def pa(name, shape, dt=F32):
        return sb(name, shape, dt, mixer)

    xh = pa("xh", [P, KT, T], F32R)
    xl = pa("xl", [P, KT, T], F32R)
    proj = pa("proj", [P, 16, T])
    brh = pa("brh", [P, NBR * CT, T], F32R)
    brl = pa("brl", [P, NBR * CT, T], F32R)
    merged = pa("merged", [P, KT, T])
    raw = [pa(f"raw{q}", [P, KT + CT, CH]) for q in range(2)]
    wh = [pa(f"wh{q}", [P, KT + CT, CH], F32R) for q in range(2)]
    wl = [pa(f"wl{q}", [P, KT + CT, CH], F32R) for q in range(2)]
    sig = [pa(f"sig{q}", [P, T]) for q in range(2)]
    prod = [pa(f"prod{q}", [P, T]) for q in range(2)]
    g1b = pa("g1b", [P, D])
    zrow = pa("zrow", [P, 512])
    prm_rows = pa("prm_rows", [NPRM, BW])
    prm = pa("prm", [P, CT, NPRM])
    pool_rows = pa("pool_rows", [NB * HP, BW])
    conv_rows = pa("conv_rows", [NB * HC // 2, 2, BW])
    sconv_rows = pa("sconv_rows", [NB * HS, BW])
    ws_rows = pa("ws_rows", [P, 4, P])
    wsT = pa("wsT", [P, 4, P])
    wsS = pa("wsS", [NSM, 4, NSM])
    bS = pa("bS", [P, CT, P])
    pw = pa("pw", [P, CT, P])
    pext = pa("pext", [P, CT, EP])
    cext = pa("cext", [P, CT, EC])
    zext = pa("zext", [P, CT, ES])
    invc = pa("invc", [P, CT, NPR])
    cacc = pa("cacc", [P, CT, T])
    vn = pa("vn", [P, CT, T])
    sqb = pa("sqb", [P, CT, T])
    lnr = pa("lnr", [P, T])
    v_tok = pa("v_tok", [P, NT, BW])
    tail_sb = pa("tail_sb", [TAIL, 3, BW])
    proj_flat = proj[:, :, :].rearrange("p k t -> p (k t)")
    xs = proj_flat[:, 0:NT * D].rearrange("p (t d) -> p t d", t=NT)
    junk = proj_flat[:, 4 * D:5 * D]
    merged_flat = merged[:, :, :].rearrange("p k t -> p (k t)")
    sum2 = merged_flat[:, 0:CT * EP].rearrange("p (c e) -> p c e", c=CT)
    sum4 = merged_flat[:, CT * EP:2 * CT * EP].rearrange("p (c e) -> p c e", c=CT)
    sum8 = merged_flat[:, 2 * CT * EP:2 * CT * EP + EP]
    sum16 = sum2[:, 1, :]
    mixer.close()

    moe = ExitStack()

    def pb(name, shape, dt=F32):
        return sb(name, shape, dt, moe)

    wgu = [[pb(f"wgu{s}{j}", [P, 2, KT, F]) for j in range(2)] for s in range(2)]
    wd = [[pb(f"wd{s}{j}", [P, FK, D]) for j in range(2)] for s in range(2)]
    xn2 = pb("xn2", [P, NT, D])
    xn2T = pb("xn2T", [P, KT, T])
    xg = [pb(f"xg{s}", [P, D]) for s in range(2)]
    xgT = [pb(f"xgT{s}", [P, KT, P]) for s in range(2)]
    sg = [pb(f"sg{s}", [P, F]) for s in range(2)]
    hh = [pb(f"hh{s}", [P, F]) for s in range(2)]
    hhT = [pb(f"hhT{s}", [P, FK, P]) for s in range(2)]
    yy = [pb(f"yy{s}", [P, D]) for s in range(2)]
    junk2 = xgT[0][:, :, :].rearrange("p k t -> p (k t)")
    lgt = pb("lgt", [P, NT, NG + NE])
    iog = pb("iog", [P, NT, NG])
    ioe = pb("ioe", [P, NT, NE])
    gsh = pb("gsh", [P, NT, NG])
    geq = pb("geq", [P, NT, NG])
    gex = pb("gex", [P, NT, NG])
    gmax = pb("gmax", [P, NT])
    gidx = pb("gidx", [P, NT])
    psel = pb("psel", [P, NT])
    lem = pb("lem", [P, NT, NE])
    eqm = pb("eqm", [P, NT, NE])
    oh = [pb(f"oh{w}", [P, NT, NE]) for w in range(2)]
    topv = [pb(f"topv{w}", [P, NT]) for w in range(2)]
    tidx = pb("tidx", [P, NT])
    tw = [pb(f"tw{w}", [P, NT]) for w in range(2)]
    both = pb("both", [P, NT, NE])
    posx = pb("posx", [P, NT, NE])
    over = pb("over", [P, NT, NE])
    ebase = pb("ebase", [P, NT, NE])
    cwo = pb("cwo", [P, NT, NE])
    rtmp = pb("rtmp", [P, NT, NE])
    slotf = [pb(f"slotf{w}", [P, NT]) for w in range(2)]
    sloti = [pb(f"sloti{w}", [P, NT], I32) for w in range(2)]
    rec = pb("rec", [P, NT, 2, 4])
    recz = pb("recz", [P, PAIRS, 4])
    recs = pb("recs", [P, PAIRS, 4])
    tok_i = pb("tok_i", [P, PAIRS], I32)
    row_i = pb("row_i", [P, PAIRS], I32)
    ovs = pb("ovs", [P, 1])
    flag_i = pb("flag_i", [P, 1], I32)
    ov_cw = pb("ov_cw", [P, NT])
    ytk = [wgu[t // 2][t % 2][:, :, :, :].rearrange("p w k f -> p (w k f)")[:, 0:2 * D] for t in range(NT)]
    ex = pb("ex", [P, NT])
    moe.close()

    w_in3 = a["w_in"][0].rearrange("(k p) n -> p k n", p=P)
    w_out3 = a["w_out"][0].rearrange("(k p) n -> p k n", p=P)
    w_br3 = a["w_branch"][0].rearrange("b (k p) n -> p (b k) n", p=P)
    x_rows = [a["x_prompt"][0, 0:128, :], a["x_prompt"][0, 128:256, :],
              a["x_sample"].rearrange("b s d -> (b s) d")]
    y_rows = [o["y_prompt"][0, 0:128, :], o["y_prompt"][0, 128:256, :],
              o["y_sample"].rearrange("b s d -> (b s) d")]
    w_gate4 = a["w_gate"][0].rearrange("e (p k) f -> e p k f", k=KT)
    w_up4 = a["w_up"][0].rearrange("e (p k) f -> e p k f", k=KT)
    w_down4 = a["w_down"][0].rearrange("e (p k) d -> e p k d", k=FK)

    def seg(ext, base, hist):
        return ext[:, :, base:base + NB * (hist + NS)].rearrange("p c (b s) -> p c b s", b=NB)

    def smp(ap):
        return ap[:, :, NPR:T].rearrange("p c (b s) -> p c b s", b=NB)

    N_SMALL = 8 + 3 + 1 + 4
    N_SMALL2 = 6
    raw_in = [sem("raw_in0"), sem("raw_in1")]
    wbr_in = [sem("wbr_in0"), sem("wbr_in1")]
    x_in = [sem(f"x_in{t}") for t in range(NT)]
    FIRST_OUT = N_PROJ + N_GATE

    block = ctx.enter_context(nc.Block())

    @block.sync
    def _(sp):
        for t, (_, n) in enumerate(TILES):
            sp.dma_start(x_tok[0:n, t, :], x_rows[t]).then_inc(x_in[t], 16)
        sp.dma_start(g1b[:, :], a["norm1_g"][0:1, :].to_broadcast([P, D])).then_inc(sem("g1_in"), 16)

        def load_plain(c):
            src, n0 = (w_in3, c * CH) if c < N_PROJ else (w_out3, (c - FIRST_OUT) * CH)
            sp.dma_start(raw[c % 2][:, 0:KT, :], src[:, :, n0:n0 + CH]).then_inc(raw_in[c % 2], 16)

        load_plain(0)
        load_plain(1)
        small = sem("small_in")
        sp.dma_start(prm_rows[0:31, :], a["conf_dw"][0]).then_inc(small, 16)
        sp.dma_start(prm_rows[31:32, :], a["conf_dw_b"]).then_inc(small, 16)
        sp.dma_start(prm_rows[32:33, :], a["conf_ln_g"]).then_inc(small, 16)
        sp.dma_start(prm_rows[33:34, :], a["conf_ln_b"]).then_inc(small, 16)
        sp.dma_start(prm_rows[34:37, :], a["sconv_w"][0]).then_inc(small, 16)
        sp.dma_start(prm_rows[37:38, :], a["sgu_ln_g"]).then_inc(small, 16)
        sp.dma_start(prm_rows[38:39, :], a["sgu_ln_b"]).then_inc(small, 16)
        sp.dma_start(prm_rows[39:40, :], a["pool_scale"]).then_inc(small, 16)
        sp.dma_start(pool_rows[:, :], a["state_pool"][0].rearrange("b r c -> (b r) c")).then_inc(small, 16)
        sp.dma_start(conv_rows[:, :, :],
                     a["state_conv"][0].rearrange("(h b) r c -> (b r) h c", h=2)).then_inc(small, 16)
        sp.dma_start(sconv_rows[:, :], a["state_sconv"][0].rearrange("b r c -> (b r) c")).then_inc(small, 16)
        sp.dma_start(ws_rows[:, :, :], a["sgu_ws"][0].rearrange("h t s -> t h s")).then_inc(small, 16)
        for h in range(4):
            q = 64 * (h % 2)
            sp.dma_start(bS[q:q + 64, h // 2, :],
                         a["sgu_b"][0, h:h + 1, :].to_broadcast([64, P])).then_inc(small, 16)
        sp.wait_ge(sem("const_done"), 3)
        for g in range(4):
            q = 64 * (g % 2)
            sp.dma_start(pw[q:q + 64, g // 2, q:q + 64], a["pool_w"][0, g]).then_inc(sem("pw_in"), 16)

        for c in range(2, N_PROJ):
            sp.wait_ge(sem("lo_done"), c - 1)
            load_plain(c)
            if c == 3:
                s2 = sem("small2_in")
                sp.dma_start(g2b[:, :], a["norm2_g"][0:1, :].to_broadcast([P, D])).then_inc(s2, 16)
                sp.dma_start(gfb[:, :], a["final_g"].rearrange("(u d) -> u d", u=1).to_broadcast([P, D])).then_inc(s2, 16)
                sp.dma_start(rg[:, :, :], a["router_g"][0].rearrange("(p k) g -> p k g", k=KT)).then_inc(s2, 16)
                sp.dma_start(re[:, :, :], a["router_e"][0].rearrange("(p k) g -> p k g", k=KT)).then_inc(s2, 16)
                sp.dma_start(rb[:, 0:NG], a["router_g_b"][0:1, :].to_broadcast([P, NG])).then_inc(s2, 16)
                sp.dma_start(rb[:, NG:NG + NE], a["router_e_b"][0:1, :].to_broadcast([P, NE])).then_inc(s2, 16)
                sp.dma_start(o["pool_s"][0, :, 0:HP - NS, :],
                             a["state_pool"][0, :, NS:HP, :]).then_inc(sem("out_dma"), 16)
                sp.dma_start(o["conv_s"][0, :, 0:HC - NS, :],
                             a["state_conv"][0, :, NS:HC, :]).then_inc(sem("out_dma"), 16)
            if c == 5:
                sp.wait_ge(sem("const_done"), 6)
                for r in range(5):
                    sp.dma_start(y_dram[r * P:(r + 1) * P, :].rearrange("p (h d) -> p h d", h=2),
                                 zrow[:, :].unsqueeze(1).to_broadcast([P, 2, 512])).then_inc(sem("zero_out"), 16)
        with sp.Fori(0, NBR) as i:
            for m in range(4):
                q = m % 2
                sp.wait_ge(sem("lo_done"), i * 4 + (N_PROJ + m - 1))
                sp.dma_start(raw[q][:, 0:KT, :],
                             w_in3[:, :, bass.ds(i * D + (N_PROJ + m) * CH, CH)]).then_inc(raw_in[q], 16)
                sp.dma_start(raw[q][:, KT:KT + CT, :],
                             w_br3[:, bass.ds(i * CT, CT), m * CH:(m + 1) * CH]).then_inc(wbr_in[q], 16)
        for c in range(FIRST_OUT, FIRST_OUT + N_OUT):
            sp.wait_ge(sem("lo_done"), c - 1)
            load_plain(c)
            if c == FIRST_OUT + 1:
                sp.wait_ge(sem("v_tok_done"), 2)
                sp.dma_start(o["sguv_p"][0, 0], v_tok[:, 1, :]).then_inc(sem("out_dma"), 16)
                sp.dma_start(o["sguv_s"][0].rearrange("b s c -> (b s) c"),
                             v_tok[0:NSM, 2, :]).then_inc(sem("out_dma"), 16)
                sp.wait_ge(sem("tail_done"), 2)
                sp.dma_start(o["pool_p"][0, 0], tail_sb[32 - HP:32, 0, :]).then_inc(sem("out_dma"), 16)
                sp.dma_start(o["conv_p"][0, 0], tail_sb[32 - HC:32, 1, :]).then_inc(sem("out_dma"), 16)
                sp.dma_start(o["sconv_p"][0, 0], tail_sb[32 - HS:32, 2, :]).then_inc(sem("out_dma"), 16)
                sp.dma_start(tail_dram.rearrange("x r c -> r x c"),
                             tail_sb[32:TAIL, :, :]).then_inc(sem("tail_out"), 16)

        sp.wait_ge(sem("wo_mm"), NT * N_OUT)
        sp.wait_ge(sem("out_dma"), 16 * 7)
        sp.wait_ge(sem("tail_out"), 16)
        sp.wait_ge(sem("zero_out"), 16 * 5)
        sp.wait_ge(sem("wsS_in"), 16 * NB)

        def load_pair(p, s):
            for j in range(2):
                e = p * 2 + j
                sp.dma_start(wgu[s][j][:, 0, :, :], w_gate4[e]).then_inc(sem(f"wgu_in{s}"), 16)
                sp.dma_start(wgu[s][j][:, 1, :, :], w_up4[e]).then_inc(sem(f"wgu_in{s}"), 16)

        def load_down(p, s):
            for j in range(2):
                sp.dma_start(wd[s][j][:, :, :], w_down4[p * 2 + j]).then_inc(sem(f"wd_in{s}"), 16)

        for p in range(2):
            load_pair(p, p)
            load_down(p, p)
            if p == 0:
                sp.dma_start(o["pool_s"][0, :, HP - NS:HP, :],
                             tail_dram[0].rearrange("(b s) c -> b s c", b=NB)).then_inc(sem("out_dma"), 16)
                sp.dma_start(o["conv_s"][0, :, HC - NS:HC, :],
                             tail_dram[1].rearrange("(b s) c -> b s c", b=NB)).then_inc(sem("out_dma"), 16)
                sp.dma_start(o["sconv_s"][0],
                             tail_dram[2].rearrange("(b s) c -> b s c", b=NB)[:, NS - HS:NS, :]).then_inc(sem("out_dma"), 16)
        with sp.Fori(1, PAIRS // 2) as i:
            for s in range(2):
                sp.wait_ge(sem("gu_mm"), i * 2 + (s - 1))
                for j in range(2):
                    sp.dma_start(wgu[s][j][:, 0, :, :], w_gate4[i * 4 + (2 * s + j)]).then_inc(sem(f"wgu_in{s}"), 16)
                    sp.dma_start(wgu[s][j][:, 1, :, :], w_up4[i * 4 + (2 * s + j)]).then_inc(sem(f"wgu_in{s}"), 16)
                sp.wait_ge(sem("dn_mm"), i * 2 + (s - 1))
                for j in range(2):
                    sp.dma_start(wd[s][j][:, :, :], w_down4[i * 4 + (2 * s + j)]).then_inc(sem(f"wd_in{s}"), 16)

        sp.wait_ge(sem("flag_ready"), 1)
        flag = sp.value_load(flag_i[0:1, 0:1], min_val=0, max_val=2 * T)
        with sp.If(flag > 0):
            with sp.Fori(0, NE) as e:
                sp.wait_ge(sem("ov_free"), e + 1)
                sp.dma_start(wgu[0][0][:, 0, :, :], w_gate4[e]).then_inc(sem("ov_in"), 16)
                sp.dma_start(wgu[0][0][:, 1, :, :], w_up4[e]).then_inc(sem("ov_in"), 16)
                sp.dma_start(wd[0][0][:, :, :], w_down4[e]).then_inc(sem("ov_in"), 16)
            sp.wait_ge(sem("ov_free"), NE + 1)

        for s in range(2):
            sp.wait_ge(sem(f"y_out{s}"), 16 * PAIRS // 2)
        for t, (t0, n) in enumerate(TILES):
            sp.dma_start(ytk[t][0:n, :],
                         y_dram[2 * t0:2 * (t0 + n), :].rearrange("(t w) d -> t (w d)", w=2)).then_inc(sem(f"yt_in{t}"), 16)
        for t, (_, n) in enumerate(TILES):
            sp.wait_ge(sem("y_done"), t + 1)
            sp.dma_start(y_rows[t], ytk[t][0:n, 0:D]).then_inc(sem("out_dma"), 16)
        sp.wait_ge(sem("out_dma"), 16 * (7 + 3 + NT))

    @block.gpsimd
    def _(pool):
        g = nc.gpsimd
        const = sem("const_done")
        g.memset(ss[:, :], 1.0)
        g.memset(epsb[:, :], LN_EPS)
        g.memset(pw[:, :, :], 0.0).then_inc(const, 1)
        g.memset(ident[:, :], 0.0).then_inc(const, 1)
        pool.wait_ge(const, 2)
        g.affine_select(out=ident[:, :], in_=ident[:, :], compare_op=ALU.not_equal, fill=1.0, base=0,
                        pattern=[[-1, P]], channel_multiplier=1).then_inc(const, 1)
        g.memset(before[:, :], 1.0).then_inc(const, 1)
        g.iota(invc[:, :, :], pattern=[[0, CT], [1, NPR]], base=1, channel_multiplier=0,
               allow_small_or_imprecise_dtypes=True)
        pool.wait_ge(const, 4)
        g.affine_select(out=before[:, :], in_=before[:, :], compare_op=ALU.is_gt, fill=0.0, base=0,
                        pattern=[[1, P]], channel_multiplier=-1).then_inc(const, 1)
        g.memset(ones[:, :], 1.0)
        g.memset(mean_w[:, :], 1.0 / BW)
        g.memset(zrow[:, :], 0.0)
        g.memset(wsS[:, :, :], 0.0)
        g.memset(pext[:, :, 0:HP], 0.0)
        g.memset(cext[:, :, 0:HC], 0.0)
        g.memset(zext[:, :, 0:HS], 0.0).then_inc(const, 1)

        def lo(c, q, kn):
            pool.wait_ge(sem("hi_done"), c + 1)
            g.tensor_tensor(wl[q][:, 0:kn, :], raw[q][:, 0:kn, :], wh[q][:, 0:kn, :].bitcast(F32),
                            ALU.subtract).then_inc(sem("lo_done"), 1)

        lo(0, 0, KT)
        lo(1, 1, KT)
        pool.wait_ge(sem("small_in"), 16 * N_SMALL)
        g.affine_select(out=ws_rows[:, :, :], in_=ws_rows[:, :, :], compare_op=ALU.is_ge, fill=0.0, base=0,
                        pattern=[[0, 4], [-1, P]], channel_multiplier=1).then_inc(sem("ws_masked"), 1)
        with pool.Fori(1, N_PROJ // 2) as i:
            for q in range(2):
                lo(i * 2 + q, q, KT)
        pool.wait_ge(sem("pool_ready"), 1)
        g.memset(merged[:, :, :], 0.0).then_inc(sem("merged_zero"), 1)
        pool.wait_ge(sem("small2_in"), 16 * N_SMALL2)
        g.tensor_copy(rw[:, :, 0:NG], rg[:, :, :])
        g.tensor_copy(rw[:, :, NG:NG + NE], re[:, :, :]).then_inc(sem("rw_done"), 1)
        with pool.Fori(0, N_GATE // 2) as i:
            for q in range(2):
                lo(i * 2 + (N_PROJ + q), q, KT + CT)
        with pool.Fori(0, N_OUT // 2) as i:
            for q in range(2):
                lo(i * 2 + (FIRST_OUT + q), q, KT)

        pool.wait_ge(sem("wo_mm"), NT * N_OUT)
        pool.wait_ge(sem("out_dma"), 16 * 7)
        pool.wait_ge(sem("tail_out"), 16)
        g.iota(iog[:, :, :], pattern=[[0, NT], [1, NG]], base=-NG, channel_multiplier=0,
               allow_small_or_imprecise_dtypes=True)
        g.iota(ioe[:, :, :], pattern=[[0, NT], [1, NE]], base=-NE, channel_multiplier=0,
               allow_small_or_imprecise_dtypes=True)
        g.iota(ebase[:, :, :], pattern=[[0, NT], [1, PAIRS], [CAP * PAIRS, 2]], base=0, channel_multiplier=0,
               allow_small_or_imprecise_dtypes=True)
        for w in range(2):
            g.iota(rec[:, :, w, 0], pattern=[[2 * P, NT]], base=w, channel_multiplier=2,
                   allow_small_or_imprecise_dtypes=True)
            g.iota(rec[:, :, w, 2], pattern=[[P, NT]], base=0, channel_multiplier=1,
                   allow_small_or_imprecise_dtypes=True)
        g.memset(rec[:, :, :, 3], 0.0)
        g.memset(recz[:, :, 0:1], BIG)
        g.memset(recz[:, :, 1:2], 0.0)
        g.memset(recz[:, :, 2:3], BIG)
        g.memset(recz[:, :, 3:4], 0.0)
        g.memset(lgt[:, :, :], 0.0)
        g.memset(xg[0][:, :], 0.0)
        g.memset(xg[1][:, :], 0.0).then_inc(sem("moe_const"), 1)
        pool.wait_ge(sem("moe_const"), 1)
        pool.dma_start(rec_dram.rearrange("(p r) c -> p r c", p=P), recz[:, :, :]).then_inc(sem("rec_init"), 16)
        pool.wait_ge(sem("rec_init"), 16)
        pool.wait_ge(sem("rec_ready"), 1)
        for w in range(2):
            for t, (_, n) in enumerate(TILES):
                pool.indirect_dma_start(
                    out=rec_dram, out_offset=bass.IndirectOffsetOnAxis(ap=sloti[w][0:n, t:t + 1], axis=0),
                    in_=rec[0:n, t, w, :], in_offset=None, bounds_check=NE * CAP - 1,
                    oob_is_err=False).then_inc(sem("rec_out"), 16)
        pool.wait_ge(sem("rec_out"), 16 * 2 * NT)
        pool.dma_start(recs[:, :, :], rec_dram.rearrange("(p r) c -> p r c", p=P)).then_inc(sem("rec_in"), 16)
        pool.wait_ge(sem("rec_in"), 16)
        g.tensor_copy(tok_i[:, :], recs[:, :, 2])
        g.tensor_copy(row_i[:, :], recs[:, :, 0]).then_inc(sem("idx_ready"), 1)
        pool.wait_ge(sem("idx_ready"), 1)
        pool.wait_ge(sem("xn2_out"), 16 * NT)
        pool.wait_ge(sem("zero_out"), 16 * 5)

        def gather(p):
            if p >= 2:
                pool.wait_ge(sem("xt_mm"), p - 1)
            pool.indirect_dma_start(
                out=xg[p % 2][:, :], out_offset=None, in_=xn2_dram,
                in_offset=bass.IndirectOffsetOnAxis(ap=tok_i[:, p:p + 1], axis=0),
                bounds_check=T - 1, oob_is_err=False).then_inc(sem(f"xg_in{p % 2}"), 16)

        def scatter(p):
            pool.wait_ge(sem("ye_act"), p + 1)
            pool.wait_ge(sem("ye_dve"), p + 1)
            pool.indirect_dma_start(
                out=y_dram, out_offset=bass.IndirectOffsetOnAxis(ap=row_i[:, p:p + 1], axis=0),
                in_=yy[p % 2][:, :], in_offset=None, bounds_check=2 * T - 1,
                oob_is_err=False).then_inc(sem(f"y_out{p % 2}"), 16)

        gather(0)
        gather(1)
        for p in range(PAIRS):
            if p + 2 < PAIRS:
                gather(p + 2)
            scatter(p)

    @block.tensor
    def _(pe):
        mm, tr = nc.tensor.matmul, nc.tensor.transpose
        pe.wait_ge(sem("const_done"), 3)
        for u in range(2 * NT):
            t, h = u // 2, u % 2
            n = TILES[t][1]
            pe.wait_ge(sem("xs_done"), t + 1)
            for m in range(4):
                k = 4 * h + m
                last = tr(banks[u][:, m * P:m * P + n], xs[0:n, t, k * P:(k + 1) * P], ident[0:n, 0:n])
            last.then_inc(sem("xT_mm"), 1)

        def prepare():
            pe.wait_ge(sem("small_in"), 16 * N_SMALL)
            pe.wait_ge(sem("ws_masked"), 1)
            for ct in range(CT):
                cs = slice(ct * P, (ct + 1) * P)
                n = NB * HP
                tr(banks[6][:, ct * n:(ct + 1) * n], pool_rows[:, cs], ident[0:n, 0:n])
                tr(banks[6][:, 240 + ct * 16:256 + ct * 16], sconv_rows[:, cs], ident[0:16, 0:16])
                last = tr(banks[6][:, 272 + ct * NPRM:272 + (ct + 1) * NPRM], prm_rows[:, cs], ident[0:NPRM, 0:NPRM])
            last.then_inc(sem("prep_mm"), 1)
            n = NB * HC // 2
            for h in range(2):
                for ct in range(CT):
                    last = tr(banks[7][:, (2 * h + ct) * n:(2 * h + ct + 1) * n],
                              conv_rows[:, h, ct * P:(ct + 1) * P], ident[0:n, 0:n])
            last.then_inc(sem("prep_mm"), 1)
            for h in range(4):
                last = tr(banks[4][:, h * P:(h + 1) * P], ws_rows[:, h, :], ident[:, :])
            last.then_inc(sem("prep_mm"), 1)

        def split_product(out, wq, k0, kn, cols, mh, ml, m0):
            for k in range(kn):
                w_h, w_l = wh[wq][:, k0 + k, cols], wl[wq][:, k0 + k, cols]
                mm(out, w_h, mh(m0 + k), start=(k == 0), stop=False)
                mm(out, w_h, ml(m0 + k), start=False, stop=False)
                last = mm(out, w_l, mh(m0 + k), start=False, stop=(k == kn - 1))
            return last

        def proj_chunk(c, q, par, first):
            pe.wait_ge(sem("lo_done"), c + 1)
            for j in range(2):
                if not first:
                    pe.wait_ge(sem("pj_ev"), c * 2 + (j - 3))
                split_product(banks[2 * par + j][:, 0:T], q, 0, KT, slice(j * P, (j + 1) * P),
                              lambda k: xh[:, k, :], lambda k: xl[:, k, :], 0).then_inc(sem("pj_mm"), 1)

        pe.wait_ge(sem("xT_lo"), 2 * NT)
        proj_chunk(0, 0, 0, True)
        prepare()
        proj_chunk(1, 1, 1, True)
        proj_chunk(2, 0, 0, False)
        proj_chunk(3, 1, 1, False)
        pe.wait_ge(sem("pool_ready"), 1)
        pe.wait_ge(sem("pw_in"), 64)
        pe.wait_ge(sem("prep_done"), 3)
        for ct in range(CT):
            last = mm(banks[6 + ct][:, 0:T], pw[:, ct, :], vn[:, ct, :], start=True, stop=True)
        last.then_inc(sem("map_mm"), 1)
        with pe.Fori(2, N_PROJ // 2) as i:
            for q in range(2):
                proj_chunk(i * 2 + q, q, q, False)

        def channel_mean(bank, src):
            for ct in range(CT):
                last = mm(bank[:, 0:T], mean_w[:, :], src[:, ct, :], start=(ct == 0), stop=(ct == CT - 1))
            last.then_inc(sem("ln_mm"), 1)

        def v_mean():
            pe.wait_ge(sem("gelu_done"), 1)
            pe.wait_ge(sem("br_ready"), 1)
            channel_mean(banks[6], proj[:, 14:16, :])

        def v_var():
            pe.wait_ge(sem("ln_sq"), 1)
            channel_mean(banks[7], sqb)

        def b_mean():
            pe.wait_ge(sem("conv_step"), 4 * CW)
            pe.wait_ge(sem("ln_cent"), 1)
            channel_mean(banks[6], cacc)

        def b_var():
            pe.wait_ge(sem("ln_sq"), 2)
            pe.wait_ge(sem("ln_root"), 1)
            channel_mean(banks[7], sqb)

        def v_rows():
            pe.wait_ge(sem("v_norm"), 1)
            pe.wait_ge(sem("ln_cent"), 2)
            pe.wait_ge(sem("ln_root"), 2)
            for t, (t0, n) in enumerate(TILES):
                for ct in range(CT):
                    out = banks[6 + t // 2][0:n, (t % 2) * BW + ct * P:(t % 2) * BW + (ct + 1) * P]
                    last = tr(out, vn[:, ct, t0:t0 + n], ident[:, :])
            last.then_inc(sem("vT_mm"), 1)

        def v_mix():
            pe.wait_ge(sem("v_tok_done"), 2)
            pe.wait_ge(sem("wsS_in"), 16 * NB)
            for h in range(4):
                q, ct = 64 * (h % 2), h // 2
                hc = slice(h * 64, (h + 1) * 64)
                for n in range(2):
                    mm(banks[6 + ct][q:q + 64, n * P:(n + 1) * P], v_tok[:, n, hc], wsT[:, h, :],
                       start=True, stop=True, tile_position=(0, q))
                last = mm(banks[6 + ct][q:q + 64, NPR:T], v_tok[0:NSM, 2, hc], wsS[:, h, :],
                          start=True, stop=True, tile_position=(0, q))
            last.then_inc(sem("mix_mm"), 1)

        def tails():
            pe.wait_ge(sem("z_done"), 1)
            pe.wait_ge(sem("mix_read"), 2)
            for x, k0 in enumerate((0, 2, 8)):
                for ct in range(CT):
                    out = banks[6 + x // 2][0:TAIL, (x % 2) * BW + ct * P:(x % 2) * BW + (ct + 1) * P]
                    last = tr(out, proj[:, k0 + ct, T - TAIL:T], ident[:, :])
            last.then_inc(sem("tail_mm"), 1)

        def gate_tile(i, j, extra=None):
            q, cols = (j // 2) % 2, slice((j % 2) * P, (j % 2 + 1) * P)
            g = i * 8 + j
            if j % 2 == 0:
                pe.wait_ge(sem("lo_done"), i * 4 + (N_PROJ + j // 2 + 1))
            if isinstance(i, int) and g < 4:
                pe.wait_ge(sem("pj_ev"), 13 + g)
            else:
                pe.wait_ge(sem("gate_sg"), g - 3)
            split_product(banks[j % 4][:, 0:T], q, 0, KT, cols,
                          lambda k: xh[:, k, :], lambda k: xl[:, k, :], 0).then_inc(sem("gate_mm"), 1)
            pe.wait_ge(sem("br_ready"), i + 1)
            if not (isinstance(i, int) and g < 2):
                pe.wait_ge(sem("gp_done"), g - 1)
            out = banks[4 + j % 2][:, 0:T]
            split_product(out, q, KT, CT, cols, lambda k: brh[:, i * CT + k, :],
                          lambda k: brl[:, i * CT + k, :], 0).then_inc(sem("br_mm"), 1)
            if extra:
                extra()

        inserts = [v_mean, v_var, b_mean, b_var, v_rows, v_mix, tails, None]
        for j in range(8):
            gate_tile(0, j, inserts[j])
        with pe.Fori(1, NBR) as i:
            for j in range(8):
                gate_tile(i, j)

        pe.wait_ge(sem("mg_lo"), 4)
        pe.wait_ge(sem("tail_done"), 2)
        for c in range(N_OUT):
            q = c % 2
            pe.wait_ge(sem("lo_done"), FIRST_OUT + c + 1)
            for t, (t0, n) in enumerate(TILES):
                out = banks[3 * q + t][0:n, 0:CH]
                if c >= 2:
                    pe.wait_ge(sem("wo_add"), NT * (c - 2) + t + 1)
                for k in range(KT):
                    mh, ml = brh[:, k, t0:t0 + n], brl[:, k, t0:t0 + n]
                    mm(out, mh, wh[q][:, k, :], start=(k == 0), stop=False)
                    mm(out, mh, wl[q][:, k, :], start=False, stop=False)
                    last = mm(out, ml, wh[q][:, k, :], start=False, stop=(k == KT - 1))
                last.then_inc(sem("wo_mm"), 1)

        for u in range(2 * NT):
            t, h = u // 2, u % 2
            n = TILES[t][1]
            pe.wait_ge(sem("n2_done"), t + 1)
            if u == 0:
                pe.wait_ge(sem("wo_add"), NT * N_OUT)
            for m in range(4):
                k = 4 * h + m
                last = tr(banks[u][:, m * P:m * P + n], xn2[0:n, t, k:D:KT], ident[0:n, 0:n])
            last.then_inc(sem("n2T_mm"), 1)
        pe.wait_ge(sem("n2T_act"), NT)
        pe.wait_ge(sem("n2T_dve"), NT)
        pe.wait_ge(sem("rw_done"), 1)
        for t, (t0, n) in enumerate(TILES):
            for k in range(KT):
                last = mm(banks[6][0:n, t * 64:t * 64 + NG + NE], xn2T[:, k, t0:t0 + n], rw[:, k, :],
                          start=(k == 0), stop=(k == KT - 1))
        last.then_inc(sem("lg_mm"), 1)
        pe.wait_ge(sem("both_done"), 1)
        for t in range(NT):
            for u in range(t + 1):
                last = mm(banks[7][:, t * NE:(t + 1) * NE], (before if u == t else ones)[:, :], both[:, u, :],
                          start=(u == 0), stop=(u == t))
        last.then_inc(sem("cum_mm"), 1)
        pe.wait_ge(sem("ovs_done"), 1)
        mm(banks[7][:, 256:257], ones[:, :], ovs[:, :], start=True, stop=True).then_inc(sem("ovs_mm"), 1)

        psX = banks[0], banks[1]
        psG = banks[2], banks[3]
        psT = banks[4]
        psY = banks[5], banks[6]

        def rows_in(p, s):
            pe.wait_ge(sem(f"xg_in{s}"), xg_target(p, s))
            if not (isinstance(p, int) and p == 0):
                pe.wait_ge(sem("xe_done"), p)
            for k in range(KT):
                last = tr(psX[k // 4][:, (k % 4) * P:(k % 4 + 1) * P], xg[s][:, k:D:KT], ident[:, :])
            last.then_inc(sem("xt_mm"), 1)

        def xg_target(p, s):
            return 16 * (p // 2 + 1) if isinstance(p, int) else p * 8 + (16 - 8 * s)

        def gate_up(p, s):
            pe.wait_ge(sem("xe_done"), p + 1)
            pe.wait_ge(sem(f"wgu_in{s}"), xg_target(p, s) * 4)
            if not (isinstance(p, int) and p < 2):
                pe.wait_ge(sem("h_done"), p - 1)
            for k in range(KT):
                for j in range(2):
                    q = 64 * j
                    last = mm(psG[s][q:q + 64, :].rearrange("p (w f) -> p w f", w=2), xgT[s][:, k, q:q + 64],
                              wgu[s][j][:, :, k, :], start=(k == 0), stop=(k == KT - 1), tile_position=(0, q))
            last.then_inc(sem("gu_mm"), 1)

        def down(p, s):
            pe.wait_ge(sem("h_done"), p + 1)
            if not (isinstance(p, int) and p == 0):
                pe.wait_ge(sem("hte_done"), p)
            for k in range(FK):
                last = tr(psT[:, k * P:(k + 1) * P], hh[s][:, k:F:FK], ident[:, :])
            last.then_inc(sem("ht_mm"), 1)
            pe.wait_ge(sem("hte_done"), p + 1)
            pe.wait_ge(sem(f"wd_in{s}"), xg_target(p, s) * 2)
            if not (isinstance(p, int) and p == 0):
                pe.wait_ge(sem("ye_act"), p)
                pe.wait_ge(sem("ye_dve"), p)
            for half in range(2):
                for k in range(FK):
                    for j in range(2):
                        q = 64 * j
                        last = mm(psY[half][q:q + 64, :], hhT[s][:, k, q:q + 64],
                                  wd[s][j][:, k, half * 512:(half + 1) * 512],
                                  start=(k == 0), stop=(k == FK - 1), tile_position=(0, q))
            last.then_inc(sem("dn_mm"), 1)

        rows_in(0, 0)
        gate_up(0, 0)
        for p in (1, 2):
            rows_in(p, p % 2)
            gate_up(p, p % 2)
            down(p - 1, (p - 1) % 2)
        with pe.Fori(1, PAIRS // 2 - 1) as i:
            for m in (1, 2):
                rows_in(i * 2 + m, m % 2)
                gate_up(i * 2 + m, m % 2)
                down(i * 2 + (m - 1), (m - 1) % 2)
        rows_in(PAIRS - 1, 1)
        gate_up(PAIRS - 1, 1)
        down(PAIRS - 2, 0)
        down(PAIRS - 1, 1)

        pe.wait_ge(sem("flag_ready"), 1)
        flag = pe.value_load(flag_i[0:1, 0:1], min_val=0, max_val=2 * T)
        with pe.If(flag > 0):
            pe.wait_ge(sem("ov_free"), 1)
            with pe.Fori(0, NE) as e:
                pe.wait_ge(sem("ov_in"), e * 48 + 48)
                for t, (t0, n) in enumerate(TILES):
                    pe.wait_ge(sem("ov_acc"), e * NT + (t + 1))
                    for k in range(KT):
                        last = mm(psG[0][0:n, :].rearrange("p (w f) -> p w f", w=2), xn2T[:, k, t0:t0 + n],
                                  wgu[0][0][:, :, k, :], start=(k == 0), stop=(k == KT - 1))
                    last.then_inc(sem("ov_gu"), 1)
                    pe.wait_ge(sem("ov_h"), e * NT + (t + 1))
                    for k in range(FK):
                        last = tr(psT[:, k * P:(k + 1) * P], hh[0][:, k:F:FK], ident[:, :])
                    last.then_inc(sem("ov_ht"), 1)
                    pe.wait_ge(sem("ov_hte"), e * NT + (t + 1))
                    for half in range(2):
                        for k in range(FK):
                            last = mm(psY[half][0:n, :], hhT[0][:, k, 0:n],
                                      wd[0][0][:, k, half * 512:(half + 1) * 512],
                                      start=(k == 0), stop=(k == FK - 1))
                    last.then_inc(sem("ov_dn"), 1)

    @block.scalar
    def _(act):
        f = nc.scalar.activation
        act.wait_ge(sem("const_done"), 1)
        for t, (_, n) in enumerate(TILES):
            act.wait_ge(x_in[t], 16)
            if t:
                act.wait_ge(sem("x_sq"), t)
            f(junk[0:n, :], x_tok[0:n, t, :], ACT.Square, accum_out=ss[0:n, t:t + 1]).then_inc(sem("x_sq"), 1)
        act.wait_ge(sem("x_ms"), 1)
        f(root[:, :], ms[:, :], ACT.Sqrt).then_inc(sem("x_root"), 1)

        def hi(c, q, kn):
            act.wait_ge(raw_in[q], (c - q) // 2 * 16 + 16 if isinstance(c, int) else c * 8 + (16 - 8 * q))
            if kn > KT:
                n = (c - N_PROJ - q) // 2 * 16 + 16 if isinstance(c, int) else c * 8 + (16 - 8 * q - 8 * N_PROJ)
                act.wait_ge(wbr_in[q], n)
            f(wh[q][:, 0:kn, :], raw[q][:, 0:kn, :], ACT.Copy).then_inc(sem("hi_done"), 1)

        hi(0, 0, KT)
        hi(1, 1, KT)
        for u in range(2 * NT):
            t, h = u // 2, u % 2
            t0, n = TILES[t]
            act.wait_ge(sem("xT_mm"), u + 1)
            f(xh[:, 4 * h:4 * h + 4, t0:t0 + n],
              banks[u][:, :].rearrange("p (k c) -> p k c", c=P)[:, :, 0:n], ACT.Copy).then_inc(sem("xT_hi"), 1)
        for c in range(N_PROJ):
            for tl in (2 * c, 2 * c + 1):
                act.wait_ge(sem("pj_mm"), tl + 1)
                f(proj[:, tl, :], banks[tl % 4][:, 0:T], ACT.Copy).then_inc(sem("pj_ev"), 1)
            hi(c + 2, c % 2, KT if c + 2 < N_PROJ else KT + CT)
            if c == 1:
                act.wait_ge(sem("prep_done"), 3)
                act.wait_ge(sem("const_done"), 6)
                for b in range(NB):
                    act.dma_start(wsS[b * NS:(b + 1) * NS, :, b * NS:(b + 1) * NS],
                                  wsT[0:NS, :, 0:NS]).then_inc(sem("wsS_in"), 16)
            if c == 2:
                act.wait_ge(sem("pj_ev"), 6)
                f(proj[:, 4:6, :], proj[:, 4:6, :], ACT.Sigmoid).then_inc(sem("glu_gate"), 1)
            if c == 3:
                act.wait_ge(sem("map_mm"), 1)
                for ct in range(CT):
                    last = f(brh[:, ct, :], banks[6 + ct][:, 0:T], ACT.Copy, scale=prm[:, ct, PRM["ps"]:PRM["ps"] + 1])
                last.then_inc(sem("br_hi"), 1)
        act.wait_ge(sem("pj_ev"), 16)
        f(proj[:, 12:16, :], proj[:, 12:16, :], ACT.Gelu_apprx_tanh).then_inc(sem("gelu_done"), 1)

        def gate(i, j):
            g = i * 8 + j
            act.wait_ge(sem("gate_mm"), g + 1)
            if not (isinstance(i, int) and g < 2):
                act.wait_ge(sem("gp_done"), g - 1)
            f(sig[j % 2][:, :], banks[j % 4][:, 0:T], ACT.Sigmoid).then_inc(sem("gate_sg"), 1)

        def next_hi(i, j, kn=KT + CT):
            act.wait_ge(sem("br_mm"), i * 8 + (j + 1))
            hi(i * 4 + (N_PROJ + j // 2 + 2), (j // 2) % 2, kn)

        def square(n):
            act.wait_ge(sem("ln_cent"), n)
            if n == 2:
                act.wait_ge(sem("ln_mm"), 2)
            f(sqb[:, :, :], (vn if n == 1 else cacc)[:, :, :], ACT.Square).then_inc(sem("ln_sq"), 1)

        def sqrt(n):
            act.wait_ge(sem("ln_mm"), 2 * n)
            if n == 2:
                act.wait_ge(sem("v_norm"), 1)
            f(lnr[:, :], banks[7][:, 0:T], ACT.Sqrt, bias=epsb[:, 0:1]).then_inc(sem("ln_root"), 1)

        def br_high(n, src):
            act.wait_ge(sem("br_val"), n)
            f(brh[:, n * CT:(n + 1) * CT, :], src, ACT.Copy).then_inc(sem("br_hi"), 1)

        gate(0, 0)
        square(1)
        gate(0, 1)
        next_hi(0, 1)
        sqrt(1)
        gate(0, 2)
        square(2)
        gate(0, 3)
        next_hi(0, 3)
        sqrt(2)
        gate(0, 4)
        act.wait_ge(sem("b_norm"), 1)
        f(sqb[:, :, :], cacc[:, :, :], ACT.Sigmoid).then_inc(sem("silu_gate"), 1)
        gate(0, 5)
        next_hi(0, 5)
        br_high(1, cacc[:, :, :])
        gate(0, 6)
        gate(0, 7)
        next_hi(0, 7)
        br_high(2, vn[:, :, :])
        br_high(3, proj[:, 12:14, :])
        with act.Fori(1, NBR - 1) as i:
            for j in range(8):
                gate(i, j)
                if j % 2:
                    next_hi(i, j)
        for j in range(8):
            gate(NBR - 1, j)
            if j % 2:
                next_hi(NBR - 1, j, KT + CT if j < 4 else KT)
        for n in range(4):
            act.wait_ge(sem("mg_add"), 26 + 2 * n)
            f(brh[:, 2 * n:2 * n + 2, :], merged[:, 2 * n:2 * n + 2, :], ACT.Copy).then_inc(sem("mg_hi"), 1)
        for c in (FIRST_OUT + 2, FIRST_OUT + 3):
            act.wait_ge(sem("wo_mm"), NT * (c - FIRST_OUT - 1))
            hi(c, c % 2, KT)

        for t, (_, n) in enumerate(TILES):
            act.wait_ge(sem("wo_add"), NT * (N_OUT - 1) + t + 1)
            if t:
                act.wait_ge(sem("n2_sq"), t)
            else:
                act.wait_ge(sem("wo_mm"), NT * N_OUT)
                act.wait_ge(sem("out_dma"), 16 * 7)
                act.wait_ge(sem("tail_out"), 16)
            f(junk2[0:n, :], x_tok[0:n, t, :], ACT.Square, accum_out=ss[0:n, t:t + 1]).then_inc(sem("n2_sq"), 1)
        act.wait_ge(sem("n2_ms"), 1)
        f(root[:, :], ms[:, :], ACT.Sqrt).then_inc(sem("n2_root"), 1)
        for t, (t0, n) in enumerate(TILES):
            act.wait_ge(sem("n2_done"), t + 1)
            act.dma_start(xn2_dram[t0:t0 + n, :], xn2[0:n, t, :]).then_inc(sem("xn2_out"), 16)
        for t, (t0, n) in enumerate(TILES):
            act.wait_ge(sem("n2T_mm"), 2 * t + 1)
            f(xn2T[:, 0:4, t0:t0 + n], banks[2 * t][:, :].rearrange("p (k c) -> p k c", c=P)[:, :, 0:n],
              ACT.Copy).then_inc(sem("n2T_act"), 1)
        act.wait_ge(sem("gsh_done"), 1)
        f(gex[:, :, :], gsh[:, :, :], ACT.Exp).then_inc(sem("rt_exp"), 1)
        act.wait_ge(sem("tdiff_done"), 1)
        f(ex[:, :], tidx[:, :], ACT.Exp).then_inc(sem("rt_exp"), 1)

        def rows_out(p, s):
            act.wait_ge(sem("xt_mm"), p + 1)
            if not (isinstance(p, int) and p < 2):
                act.wait_ge(sem("gu_mm"), p - 1)
            f(xgT[s][:, 0:4, :], banks[0][:, :].rearrange("p (k c) -> p k c", c=P), ACT.Copy)
            f(xgT[s][:, 4:8, :], banks[1][:, :].rearrange("p (k c) -> p k c", c=P), ACT.Copy).then_inc(sem("xe_done"), 1)

        def silu(p, s):
            act.wait_ge(sem("gu_mm"), p + 1)
            if not (isinstance(p, int) and p < 2):
                act.wait_ge(sem("h_done"), p - 1)
            f(sg[s][:, :], banks[2 + s][:, 0:F], ACT.Silu).then_inc(sem("sg_done"), 1)

        def y_out(p, s):
            act.wait_ge(sem("dn_mm"), p + 1)
            if not (isinstance(p, int) and p < 2):
                act.wait_ge(sem(f"y_out{s}"), p * 8 - 8 * s)
            f(yy[s][:, 0:512], banks[5][:, :], ACT.Copy).then_inc(sem("ye_act"), 1)

        act.wait_ge(sem("n2_root"), 1)
        rows_out(0, 0)
        silu(0, 0)
        for p in range(2):
            rows_out(p + 1, (p + 1) % 2)
            silu(p + 1, (p + 1) % 2)
            y_out(p, p)
        with act.Fori(1, PAIRS // 2 - 1) as i:
            for m in range(2):
                rows_out(i * 2 + (m + 1), (m + 1) % 2)
                silu(i * 2 + (m + 1), (m + 1) % 2)
                y_out(i * 2 + m, m)
        rows_out(PAIRS - 1, 1)
        silu(PAIRS - 1, 1)
        y_out(PAIRS - 2, 0)
        y_out(PAIRS - 1, 1)

        act.wait_ge(sem("flag_ready"), 1)
        flag = act.value_load(flag_i[0:1, 0:1], min_val=0, max_val=2 * T)
        with act.If(flag > 0):
            with act.Fori(0, NE) as e:
                for t, (_, n) in enumerate(TILES):
                    act.wait_ge(sem("ov_gu"), e * NT + (t + 1))
                    f(sg[0][0:n, :], banks[2][0:n, 0:F], ACT.Silu).then_inc(sem("ov_sg"), 1)

        for t, (_, n) in enumerate(TILES):
            act.wait_ge(sem("f_add"), t + 1)
            if t:
                act.wait_ge(sem("f_sq"), t)
            f(junk2[0:n, :], x_tok[0:n, t, :], ACT.Square, accum_out=ss[0:n, t:t + 1]).then_inc(sem("f_sq"), 1)
        act.wait_ge(sem("f_ms"), 1)
        f(root[:, :], ms[:, :], ACT.Sqrt).then_inc(sem("f_root"), 1)

    @block.vector
    def _(dve):
        v = nc.vector
        own = Steps(dve, "dve_step")

        def mean_square(ready, count, done):
            dve.wait_ge(sem(ready), count)
            v.tensor_scalar(ms[:, :], ss[:, :], 1.0 / D, RMS_EPS, ALU.mult, ALU.add).then_inc(sem(done), 1)

        mean_square("x_sq", NT, "x_ms")
        dve.wait_ge(sem("x_root"), 1)
        own.step(v.reciprocal(rstd[:, :], root[:, :]))
        own.last()
        dve.wait_ge(sem("g1_in"), 16)
        for t, (_, n) in enumerate(TILES):
            v.scalar_tensor_tensor(xs[0:n, t, :], x_tok[0:n, t, :], rstd[0:n, t:t + 1], g1b[0:n, :],
                                   ALU.mult, ALU.mult).then_inc(sem("xs_done"), 1)
        for u in range(2 * NT):
            t, h = u // 2, u % 2
            t0, n = TILES[t]
            dve.wait_ge(sem("xT_hi"), u + 1)
            v.tensor_tensor(xl[:, 4 * h:4 * h + 4, t0:t0 + n],
                            banks[u][:, :].rearrange("p (k c) -> p k c", c=P)[:, :, 0:n],
                            xh[:, 4 * h:4 * h + 4, t0:t0 + n].bitcast(F32), ALU.subtract).then_inc(sem("xT_lo"), 1)

        dve.wait_ge(sem("const_done"), 6)
        for n, w in enumerate(WINDOWS):
            q = 64 * (n % 2)
            last = v.tensor_scalar(invc[q:q + 64, n // 2, :], invc[q:q + 64, n // 2, :], float(w), None, ALU.min)
        own.step(last)
        own.last()
        own.step(v.reciprocal(invc[:, :, :], invc[:, :, :]))
        dve.wait_ge(sem("prep_mm"), 1)
        dve.wait_ge(sem("const_done"), 6)
        v.tensor_copy(seg(pext, LP, HP)[:, :, :, 0:HP],
                      banks[6][:, 0:240].rearrange("p (c b r) -> p c b r", c=CT, b=NB))
        v.tensor_copy(seg(zext, LS, HS)[:, :, :, 0:HS],
                      banks[6][:, 240:272].rearrange("p (c b r) -> p c b r", c=CT, b=NB))
        v.tensor_copy(prm[:, :, :], banks[6][:, 272:272 + CT * NPRM].rearrange("p (c r) -> p c r", c=CT)).then_inc(sem("prep_done"), 1)
        dve.wait_ge(sem("prep_mm"), 2)
        for h in range(2):
            last = v.tensor_copy(seg(cext, LC, HC)[:, :, 4 * h:4 * h + 4, 0:HC],
                                 banks[7][:, h * 240:(h + 1) * 240].rearrange("p (c b r) -> p c b r", c=CT, b=4))
        last.then_inc(sem("prep_done"), 1)
        dve.wait_ge(sem("prep_mm"), 3)
        v.tensor_copy(wsT[:, :, :], banks[4][:, :].rearrange("p (h t) -> p h t", h=4)).then_inc(sem("prep_done"), 1)

        dve.wait_ge(sem("pj_ev"), 2)
        v.tensor_copy(pext[:, :, HP:LP], proj[:, 0:2, 0:NPR])
        own.step(v.tensor_copy(seg(pext, LP, HP)[:, :, :, HP:], smp(proj[:, 0:2, :])))
        dve.wait_ge(sem("prep_done"), 1)
        own.last()
        own.step(v.tensor_tensor(sum2[:, :, 1:], pext[:, :, 1:], pext[:, :, :-1], ALU.add))
        own.last()
        own.step(v.tensor_tensor(sum4[:, :, 3:], sum2[:, :, 3:], sum2[:, :, 1:-2], ALU.add))
        own.last()
        own.step(v.tensor_tensor(sum8[:, 7:], sum4[:, 1, 7:], sum4[:, 1, 3:-4], ALU.add))
        own.last()
        own.step(v.tensor_tensor(sum16[64:128, 15:], sum8[64:128, 15:], sum8[64:128, 7:-8], ALU.add))
        own.last()
        for n, (w, sums) in enumerate(zip(WINDOWS, (sum2[:, 0, :], sum4[:, 0, :], sum8, sum16))):
            q, ct = slice(64 * (n % 2), 64 * (n % 2) + 64), n // 2
            v.tensor_tensor(vn[q, ct, 0:NPR], sums[q, HP:LP], invc[q, ct, :], ALU.mult)
            last = v.tensor_scalar(smp(vn[q, ct:ct + 1, :])[:, 0], sums[q, LP:].rearrange("p (b s) -> p b s", b=NB)[:, :, HP:],
                                   1.0 / w, None, ALU.mult)
        own.step(last)
        own.last()
        v.tensor_tensor(vn[:, :, :], vn[:, :, :], proj[:, 0:2, :], ALU.subtract).then_inc(sem("pool_ready"), 1)

        dve.wait_ge(sem("glu_gate"), 1)
        dve.wait_ge(sem("prep_done"), 2)
        own.step(v.tensor_tensor(proj[:, 2:4, :], proj[:, 2:4, :], proj[:, 4:6, :], ALU.mult))
        own.last()
        v.tensor_copy(cext[:, :, HC:LC], proj[:, 2:4, 0:NPR])
        own.step(v.tensor_copy(seg(cext, LC, HC)[:, :, :, HC:], smp(proj[:, 2:4, :])))
        own.last()
        conv_parts = [(ct, part) for ct in range(CT) for part in range(2)]

        def tap_view(ext, base, hist, ct, part, k):
            if part == 0:
                return ext[:, ct, bass.ds(k, NPR)]
            return seg(ext, base, hist)[:, ct, :, bass.ds(k, NS)]

        def acc_view(acc, ct, part):
            return acc[:, ct, 0:NPR] if part == 0 else smp(acc[:, :, :])[:, ct]

        conv = sem("conv_step")
        for ct, part in conv_parts:
            v.tensor_scalar(acc_view(cacc, ct, part), tap_view(cext, LC, HC, ct, part, 0),
                            prm[:, ct, PRM["dw"]:PRM["dw"] + 1], prm[:, ct, PRM["dwb"]:PRM["dwb"] + 1],
                            ALU.mult, ALU.add).then_inc(conv, 1)
        with dve.Fori(1, CW) as k:
            for n, (ct, part) in enumerate(conv_parts):
                dve.wait_ge(conv, k * 4 + (n - 3))
                acc = acc_view(cacc, ct, part)
                v.scalar_tensor_tensor(acc, tap_view(cext, LC, HC, ct, part, k), prm[:, ct, bass.ds(k, 1)], acc,
                                       ALU.mult, ALU.add).then_inc(conv, 1)

        def br_low(n, val):
            dve.wait_ge(sem("br_hi"), n + 1)
            v.tensor_tensor(brl[:, n * CT:(n + 1) * CT, :], val, brh[:, n * CT:(n + 1) * CT, :].bitcast(F32),
                            ALU.subtract).then_inc(sem("br_ready"), 1)

        dve.wait_ge(sem("br_hi"), 1)
        for ct in range(CT):
            last = v.scalar_tensor_tensor(brl[:, ct, :], banks[6 + ct][:, 0:T], prm[:, ct, PRM["ps"]:PRM["ps"] + 1],
                                          brh[:, ct, :].bitcast(F32), ALU.mult, ALU.subtract)
        last.then_inc(sem("br_ready"), 1)

        def merge(i, j):
            g = i * 8 + j
            dve.wait_ge(sem("gate_sg"), g + 1)
            dve.wait_ge(sem("br_mm"), g + 1)
            if not (isinstance(i, int) and g < 2):
                dve.wait_ge(sem("mg_add"), g - 1)
            v.tensor_tensor(prod[j % 2][:, :], sig[j % 2][:, :], banks[4 + j % 2][:, 0:T], ALU.mult).then_inc(sem("gp_done"), 1)
            dve.wait_ge(sem("gp_done"), g + 1)
            if isinstance(i, int) and g == 0:
                dve.wait_ge(sem("merged_zero"), 1)
            v.tensor_tensor(merged[:, j, :], merged[:, j, :], prod[j % 2][:, :], ALU.add).then_inc(sem("mg_add"), 1)

        def center(src, dst):
            mean = banks[6][:, 0:T].unsqueeze(1).to_broadcast([P, CT, T])
            v.tensor_tensor(dst, src, mean, ALU.subtract).then_inc(sem("ln_cent"), 1)

        def normalise(n, x, g, b, done):
            dve.wait_ge(sem("ln_root"), n)
            dve.wait_ge(sem("ln_sq"), n)
            own.step(v.reciprocal(lnr[:, :], lnr[:, :]))
            own.last()
            own.step(v.tensor_tensor(x, x, lnr[:, :].unsqueeze(1).to_broadcast([P, CT, T]), ALU.mult))
            own.last()
            for ct in range(CT):
                last = v.tensor_scalar(x[:, ct, :], x[:, ct, :], prm[:, ct, PRM[g]:PRM[g] + 1],
                                       prm[:, ct, PRM[b]:PRM[b] + 1], ALU.mult, ALU.add)
            last.then_inc(sem(done), 1)

        dve.wait_ge(sem("ln_mm"), 1)
        dve.wait_ge(sem("map_mm"), 1)
        center(proj[:, 14:16, :], vn[:, :, :])
        merge(0, 0)
        merge(0, 1)
        normalise(1, vn[:, :, :], "vg", "vb", "v_norm")
        merge(0, 2)
        dve.wait_ge(sem("ln_mm"), 3)
        center(cacc[:, :, :], cacc[:, :, :])
        merge(0, 3)
        dve.wait_ge(sem("pj_ev"), 12)
        v.tensor_tensor(proj[:, 8:10, :], proj[:, 8:10, :], proj[:, 10:12, :], ALU.mult).then_inc(sem("z_done"), 1)
        dve.wait_ge(sem("z_done"), 1)
        v.tensor_copy(zext[:, :, HS:LS], proj[:, 8:10, 0:NPR])
        own.step(v.tensor_copy(seg(zext, LS, HS)[:, :, :, HS:], smp(proj[:, 8:10, :])))
        normalise(2, cacc[:, :, :], "lng", "lnb", "b_norm")
        merge(0, 4)
        dve.wait_ge(sem("vT_mm"), 1)
        v.tensor_copy(v_tok[:, 0:2, :], banks[6][:, :].rearrange("p (t c) -> p t c", t=2)).then_inc(sem("v_tok_done"), 1)
        v.tensor_copy(v_tok[0:NSM, 2, :], banks[7][0:NSM, 0:BW]).then_inc(sem("v_tok_done"), 1)
        merge(0, 5)
        dve.wait_ge(sem("silu_gate"), 1)
        dve.wait_ge(sem("b_norm"), 1)
        v.tensor_tensor(cacc[:, :, :], cacc[:, :, :], sqb[:, :, :], ALU.mult).then_inc(sem("br_val"), 1)
        dve.wait_ge(sem("br_val"), 1)
        br_low(1, cacc[:, :, :])
        zc = Steps(dve, "sconv_step")
        for k in range(SW):
            for n, (ct, part) in enumerate(conv_parts):
                acc, row = acc_view(vn, ct, part), tap_view(zext, LS, HS, ct, part, k)
                w = prm[:, ct, PRM["sw"] + k:PRM["sw"] + k + 1]
                if k == 0:
                    zc.step(v.tensor_scalar(acc, row, w, None, ALU.mult))
                else:
                    dve.wait_ge(sem("sconv_step"), 4 * k + n - 3)
                    zc.step(v.scalar_tensor_tensor(acc, row, w, acc, ALU.mult, ALU.add))
        zc.last()
        merge(0, 6)
        v.tensor_tensor(vn[:, :, :], vn[:, :, :], proj[:, 6:8, :], ALU.mult).then_inc(sem("br_val"), 1)
        dve.wait_ge(sem("mix_mm"), 1)
        for ct in range(CT):
            v.tensor_tensor(proj[:, 14 + ct, 0:NPR].rearrange("p (n t) -> p n t", n=2),
                            banks[6 + ct][:, 0:NPR].rearrange("p (n t) -> p n t", n=2),
                            bS[:, ct, :].unsqueeze(1).to_broadcast([P, 2, P]), ALU.add)
            v.tensor_tensor(proj[:, 14 + ct, NPR:T].rearrange("p (b s) -> p b s", b=NB),
                            banks[6 + ct][:, NPR:T].rearrange("p (b s) -> p b s", b=NB),
                            bS[:, ct, 0:NS].unsqueeze(1).to_broadcast([P, NB, NS]), ALU.add).then_inc(sem("mix_read"), 1)
        dve.wait_ge(sem("mix_read"), 2)
        v.tensor_tensor(proj[:, 12:14, :], proj[:, 12:14, :], proj[:, 14:16, :], ALU.mult).then_inc(sem("br_val"), 1)
        merge(0, 7)
        br_low(2, vn[:, :, :])
        dve.wait_ge(sem("br_val"), 3)
        br_low(3, proj[:, 12:14, :])
        dve.wait_ge(sem("tail_mm"), 1)
        v.tensor_copy(tail_sb[:, 0:2, :], banks[6][0:TAIL, :].rearrange("p (x c) -> p x c", x=2)).then_inc(sem("tail_done"), 1)
        v.tensor_copy(tail_sb[:, 2, :], banks[7][0:TAIL, 0:BW]).then_inc(sem("tail_done"), 1)
        with dve.Fori(1, NBR) as i:
            for j in range(8):
                merge(i, j)
        for n in range(4):
            dve.wait_ge(sem("mg_hi"), n + 1)
            v.tensor_tensor(brl[:, 2 * n:2 * n + 2, :], merged[:, 2 * n:2 * n + 2, :],
                            brh[:, 2 * n:2 * n + 2, :].bitcast(F32), ALU.subtract).then_inc(sem("mg_lo"), 1)
        for c in range(N_OUT):
            for t, (_, n) in enumerate(TILES):
                dve.wait_ge(sem("wo_mm"), NT * c + t + 1)
                xc = x_tok[0:n, t, c * CH:(c + 1) * CH]
                v.tensor_tensor(xc, xc, banks[3 * (c % 2) + t][0:n, 0:CH], ALU.add).then_inc(sem("wo_add"), 1)

        mean_square("n2_sq", NT, "n2_ms")
        dve.wait_ge(sem("n2_root"), 1)
        own.step(v.reciprocal(rstd[:, :], root[:, :]))
        own.last()
        dve.wait_ge(sem("small2_in"), 16 * N_SMALL2)
        dve.wait_ge(sem("out_dma"), 16 * 7)
        dve.wait_ge(sem("tail_out"), 16)
        for t, (_, n) in enumerate(TILES):
            v.scalar_tensor_tensor(xn2[0:n, t, :], x_tok[0:n, t, :], rstd[0:n, t:t + 1], g2b[0:n, :],
                                   ALU.mult, ALU.mult).then_inc(sem("n2_done"), 1)
        for t, (t0, n) in enumerate(TILES):
            dve.wait_ge(sem("n2T_mm"), 2 * t + 2)
            v.tensor_copy(xn2T[:, 4:8, t0:t0 + n],
                          banks[2 * t + 1][:, :].rearrange("p (k c) -> p k c", c=P)[:, :, 0:n]).then_inc(sem("n2T_dve"), 1)

        def op(ins):
            own.step(ins)
            own.last()

        def wide(x, n):
            return x.unsqueeze(2).to_broadcast([P, NT, n])

        dve.wait_ge(sem("lg_mm"), 1)
        dve.wait_ge(sem("moe_const"), 1)
        logits = banks[6][:, 0:NT * 64].rearrange("p (t c) -> p t c", t=NT)[:, :, 0:NG + NE]
        v.tensor_tensor(lgt[:, 0:2, :], logits[:, 0:2, :], rb[:, :].unsqueeze(1).to_broadcast([P, 2, NG + NE]), ALU.add)
        op(v.tensor_tensor(lgt[0:NSM, 2, :], logits[0:NSM, 2, :], rb[0:NSM, :], ALU.add))
        op(v.tensor_reduce(gmax[:, :], lgt[:, :, 0:NG], axis=AX_X, op=ALU.max))
        v.tensor_tensor(gsh[:, :, :], lgt[:, :, 0:NG], wide(gmax[:, :], NG), ALU.subtract).then_inc(sem("gsh_done"), 1)
        dve.wait_ge(sem("gsh_done"), 1)
        op(v.scalar_tensor_tensor(geq[:, :, :], gsh[:, :, :], 0.0, iog[:, :, :], ALU.is_equal, ALU.mult))
        op(v.tensor_reduce(gidx[:, :], geq[:, :, :], axis=AX_X, op=ALU.min))
        op(v.tensor_tensor(geq[:, :, :], iog[:, :, :], wide(gidx[:, :], NG), ALU.is_equal))
        op(v.tensor_scalar(geq[:, :, :], geq[:, :, :], 1.0, 1.0e30, ALU.subtract, ALU.mult))
        for t in range(NT):
            last = v.tensor_tensor(lem[:, t, :].rearrange("p (g e) -> p g e", g=NG),
                                   lgt[:, t, NG:NG + NE].rearrange("p (g e) -> p g e", g=NG),
                                   geq[:, t, :].unsqueeze(2).to_broadcast([P, NG, EG]), ALU.add)
        op(last)
        for w in range(2):
            op(v.tensor_reduce(topv[w][:, :], lem[:, :, :], axis=AX_X, op=ALU.max))
            op(v.tensor_tensor(eqm[:, :, :], lem[:, :, :], wide(topv[w][:, :], NE), ALU.is_equal))
            op(v.tensor_tensor(eqm[:, :, :], eqm[:, :, :], ioe[:, :, :], ALU.mult))
            op(v.tensor_reduce(tidx[:, :], eqm[:, :, :], axis=AX_X, op=ALU.min))
            op(v.tensor_tensor(oh[w][:, :, :], ioe[:, :, :], wide(tidx[:, :], NE), ALU.is_equal))
            if w == 0:
                op(v.scalar_tensor_tensor(lem[:, :, :], oh[0][:, :, :], -1.0e38, lem[:, :, :], ALU.mult, ALU.add))
        v.memset(oh[0][64:128, 2, :], 0.0)
        op(v.memset(oh[1][64:128, 2, :], 0.0))
        v.tensor_tensor(both[:, :, :], oh[0][:, :, :], oh[1][:, :, :], ALU.add).then_inc(sem("both_done"), 1)
        v.tensor_tensor(tidx[:, :], topv[1][:, :], topv[0][:, :], ALU.subtract).then_inc(sem("tdiff_done"), 1)
        dve.wait_ge(sem("rt_exp"), 2)
        op(v.tensor_reduce(psel[:, :], gex[:, :, :], axis=AX_X, op=ALU.add))
        v.reciprocal(psel[:, :], psel[:, :])
        op(v.tensor_scalar(tw[0][:, :], ex[:, :], 1.0, None, ALU.add))
        op(v.reciprocal(tw[0][:, :], tw[0][:, :]))
        op(v.tensor_tensor(tw[0][:, :], tw[0][:, :], psel[:, :], ALU.mult))
        op(v.tensor_tensor(tw[1][:, :], tw[0][:, :], ex[:, :], ALU.mult))
        for w in range(2):
            v.tensor_copy(rec[:, :, w, 1], tw[w][:, :])
        dve.wait_ge(sem("cum_mm"), 1)
        cum = banks[7][:, 0:NT * NE].rearrange("p (t e) -> p t e", t=NT)
        v.tensor_scalar(over[:, :, :], cum, float(CAP), None, ALU.is_ge)
        op(v.scalar_tensor_tensor(posx[:, :, :], cum, float(PAIRS), ebase[:, :, :], ALU.mult, ALU.add))
        op(v.scalar_tensor_tensor(posx[:, :, :], over[:, :, :], BIG, posx[:, :, :], ALU.mult, ALU.add))
        for w in range(2):
            op(v.tensor_tensor(rtmp[:, :, :], oh[w][:, :, :], posx[:, :, :], ALU.mult))
            op(v.tensor_reduce(slotf[w][:, :], rtmp[:, :, :], axis=AX_X, op=ALU.add))
            last = v.tensor_copy(sloti[w][:, :], slotf[w][:, :])
        last.then_inc(sem("rec_ready"), 1)
        op(v.tensor_tensor(over[:, :, :], over[:, :, :], both[:, :, :], ALU.mult))
        v.tensor_reduce(ovs[:, :], over[:, :, :].rearrange("p t e -> p (t e)"), axis=AX_X, op=ALU.add).then_inc(sem("ovs_done"), 1)
        op(v.tensor_tensor(cwo[:, :, :], oh[0][:, :, :], wide(tw[0][:, :], NE), ALU.mult))
        op(v.tensor_tensor(rtmp[:, :, :], oh[1][:, :, :], wide(tw[1][:, :], NE), ALU.mult))
        op(v.tensor_tensor(cwo[:, :, :], cwo[:, :, :], rtmp[:, :, :], ALU.add))
        op(v.tensor_tensor(cwo[:, :, :], cwo[:, :, :], over[:, :, :], ALU.mult))
        dve.wait_ge(sem("ovs_mm"), 1)
        v.tensor_copy(flag_i[0:1, :], banks[7][0:1, 256:257]).then_inc(sem("flag_ready"), 1)

        def hidden(p, s):
            dve.wait_ge(sem("sg_done"), p + 1)
            if not (isinstance(p, int) and p < 2):
                dve.wait_ge(sem("ht_mm"), p - 1)
            v.scalar_tensor_tensor(hh[s][:, :], sg[s][:, :], recs[:, bass.ds(p, 1), 1].rearrange("p u -> p u"),
                                   banks[2 + s][:, F:2 * F], ALU.mult, ALU.mult).then_inc(sem("h_done"), 1)

        def hidden_T(p, s):
            dve.wait_ge(sem("ht_mm"), p + 1)
            if not (isinstance(p, int) and p < 2):
                dve.wait_ge(sem("dn_mm"), p - 1)
            v.tensor_copy(hhT[s][:, :, :], banks[4][:, 0:FK * P].rearrange("p (k c) -> p k c", k=FK)).then_inc(sem("hte_done"), 1)

        def y_half(p, s):
            dve.wait_ge(sem("dn_mm"), p + 1)
            if not (isinstance(p, int) and p < 2):
                dve.wait_ge(sem(f"y_out{s}"), p * 8 - 8 * s)
            v.tensor_copy(yy[s][:, 512:D], banks[6][:, :]).then_inc(sem("ye_dve"), 1)

        dve.wait_ge(sem("idx_ready"), 1)
        hidden(0, 0)
        for p in range(2):
            hidden_T(p, p)
            y_half(p, p)
            hidden(p + 1, (p + 1) % 2)
        with dve.Fori(1, PAIRS // 2 - 1) as i:
            for m in range(2):
                hidden_T(i * 2 + m, m)
                y_half(i * 2 + m, m)
                hidden(i * 2 + (m + 1), (m + 1) % 2)
        hidden_T(PAIRS - 2, 0)
        y_half(PAIRS - 2, 0)
        hidden(PAIRS - 1, 1)
        hidden_T(PAIRS - 1, 1)
        y_half(PAIRS - 1, 1)

        dve.wait_ge(sem("flag_ready"), 1)
        flag = dve.value_load(flag_i[0:1, 0:1], min_val=0, max_val=2 * T)
        with dve.If(flag > 0):
            v.memset(ovs[:, :], 0.0).then_inc(sem("ov_free"), 1)
            v.memset(ov_cw[:, :], 0.0).then_inc(sem("ov_acc"), 1)
            with dve.Fori(0, NE) as e:
                dve.wait_ge(sem("ov_acc"), e * NT + 1)
                v.tensor_copy(ov_cw[:, :], cwo[:, :, e]).then_inc(sem("ov_cw"), 1)
                dve.wait_ge(sem("ov_cw"), e + 1)
                for t, (_, n) in enumerate(TILES):
                    dve.wait_ge(sem("ov_sg"), e * NT + (t + 1))
                    v.scalar_tensor_tensor(hh[0][0:n, :], sg[0][0:n, :], ov_cw[0:n, t:t + 1],
                                           banks[2][0:n, F:2 * F], ALU.mult, ALU.mult).then_inc(sem("ov_h"), 1)
                    dve.wait_ge(sem("ov_ht"), e * NT + (t + 1))
                    v.tensor_copy(hhT[0][:, :, 0:n],
                                  banks[4][:, 0:FK * P].rearrange("p (k c) -> p k c", k=FK)[:, :, 0:n]).then_inc(sem("ov_hte"), 1)
                    dve.wait_ge(sem("ov_dn"), e * NT + (t + 1))
                    v.tensor_tensor(x_tok[0:n, t, 0:512], x_tok[0:n, t, 0:512], banks[5][0:n, :], ALU.add)
                    v.tensor_tensor(x_tok[0:n, t, 512:D], x_tok[0:n, t, 512:D], banks[6][0:n, :], ALU.add).then_inc(sem("ov_acc"), 1)
                v.memset(ovs[:, :], 0.0).then_inc(sem("ov_free"), 1)

        for t, (_, n) in enumerate(TILES):
            dve.wait_ge(sem(f"yt_in{t}"), 16)
            op(v.tensor_tensor(x_tok[0:n, t, :], x_tok[0:n, t, :], ytk[t][0:n, 0:D], ALU.add))
            v.tensor_tensor(x_tok[0:n, t, :], x_tok[0:n, t, :], ytk[t][0:n, D:2 * D], ALU.add).then_inc(sem("f_add"), 1)
        mean_square("f_sq", NT, "f_ms")
        dve.wait_ge(sem("f_root"), 1)
        op(v.reciprocal(rstd[:, :], root[:, :]))
        for t, (_, n) in enumerate(TILES):
            v.scalar_tensor_tensor(ytk[t][0:n, 0:D], x_tok[0:n, t, :], rstd[0:n, t:t + 1], gfb[0:n, :],
                                   ALU.mult, ALU.mult).then_inc(sem("y_done"), 1)

    ctx.close()


_INS = ['x_prompt', 'x_sample', 'state_pool', 'state_conv', 'state_sconv', 'norm1_g', 'w_in', 'pool_w', 'pool_scale',
        'conf_dw', 'conf_dw_b', 'conf_ln_g', 'conf_ln_b', 'sconv_w', 'sgu_ln_g', 'sgu_ln_b', 'sgu_ws', 'sgu_b',
        'w_branch', 'w_out', 'norm2_g', 'router_g', 'router_g_b', 'router_e', 'router_e_b', 'w_gate', 'w_up',
        'w_down', 'final_g']
_OUTS = [('y_prompt', (1, 256, 1024)), ('y_sample', (8, 8, 1024)), ('pool_p', (1, 1, 15, 256)),
         ('conv_p', (1, 1, 30, 256)), ('sconv_p', (1, 1, 2, 256)), ('sguv_p', (1, 1, 128, 256)),
         ('pool_s', (1, 8, 15, 256)), ('conv_s', (1, 8, 30, 256)), ('sconv_s', (1, 8, 2, 256)),
         ('sguv_s', (1, 8, 8, 256))]


def kernel(**inputs):
    import numpy as _np
    import concourse.bacc as _bacc
    from concourse import mybir as _mybir
    from concourse.bass_utils import run_bass_kernel_spmd as _run

    nc = _bacc.Bacc("TRN2", target_bir_lowering=False, num_devices=1)
    arrays, ins, outs = {}, {}, {}
    for name in _INS:
        x = _np.ascontiguousarray(inputs[name])
        arrays["in_" + name] = x
        ins[name] = nc.dram_tensor("in_" + name, x.shape, _mybir.dt.from_np(x.dtype), kind="ExternalInput").ap()
    for name, shape in _OUTS:
        outs[name] = nc.dram_tensor("out_" + name, shape, _mybir.dt.float32, kind="ExternalOutput").ap()
    build(nc, ins, outs)
    r = _run(nc, [arrays], core_ids=[0])
    return tuple(r.results[0]["out_" + name] for name, _ in _OUTS)
```

```python
from contextlib import ExitStack

import concourse.bass as bass
from concourse import mybir

F32 = mybir.dt.float32
F32R = mybir.dt.float32r
I32 = mybir.dt.int32
ALU = mybir.AluOpType
ACT = mybir.ActivationFunctionType
AX_X = mybir.AxisListType.X

P = 128
D = 1024
KT = D // P
NPR, NB, NS = 256, 8, 8
NSM = NB * NS
T = NPR + NSM
TILES = ((0, 128), (128, 128), (256, 64))
NT = len(TILES)
BW = 256
CT = BW // P
NBR = 4
HP, HC, HS = 15, 30, 2
CW, SW = 31, 3
WINDOWS = (2, 4, 8, 16)
NG, EG = 4, 8
NE = NG * EG
PAIRS = NE // 2
QE = 4
QUADS = NE // QE
F = 256
FK = F // P
CAP = 64
QS = QE * CAP
CH = 256
N_PROJ = 2048 // CH
N_GATE = NBR * D // CH
N_OUT = D // CH
TAIL = 96
RMS_EPS, LN_EPS = 1e-6, 1e-5
LP = HP + NPR
LC = HC + NPR
LS = HS + NPR
EP, EC, ES = LP + NB * (HP + NS), LC + NB * (HC + NS), LS + NB * (HS + NS)
PRM = dict(dw=0, dwb=31, lng=32, lnb=33, sw=34, vg=37, vb=38, ps=39)
NPRM = 40


def build(nc, a, o):
    ctx = ExitStack()
    sems = {}

    def sb(name, shape, dt=F32, stack=ctx):
        return stack.enter_context(nc.sbuf_tensor(name, shape, dt))

    def sem(name):
        if name not in sems:
            sems[name] = ctx.enter_context(nc.semaphore(name))
        return sems[name]

    class Steps:

        def __init__(self, eng, name):
            self.eng, self.sem, self.n = eng, sem(name), 0

        def step(self, ins):
            self.n += 1
            ins.then_inc(self.sem, 1)

        def last(self):
            self.eng.wait_ge(self.sem, self.n)

    tail_dram = nc.dram_tensor("state_tail_rows", (3, NSM, BW), F32).ap()

    x_tok = sb("x_tok", [P, NT, D])
    ident = sb("ident", [P, P])
    before = sb("before", [P, P])
    ones = sb("ones", [P, P])
    mean_w = sb("mean_w", [P, P])
    g2b = sb("g2b", [P, D])
    gfb = sb("gfb", [P, D])
    rg = sb("rg", [P, KT, NG])
    re = sb("re", [P, KT, NE])
    rw = sb("rw", [P, KT, NG + NE])
    rb = sb("rb", [P, NG + NE])
    ss = sb("ss", [P, NT])
    ms = sb("ms", [P, NT])
    root = sb("root", [P, NT])
    rstd = sb("rstd", [P, NT])
    epsb = sb("epsb", [P, 1])
    banks = [ctx.enter_context(nc.psum_tensor(f"bank{i}", [P, 512], F32)) for i in range(8)]

    mixer = ExitStack()

    def pa(name, shape, dt=F32):
        return sb(name, shape, dt, mixer)

    xh = pa("xh", [P, KT, T], F32R)
    xl = pa("xl", [P, KT, T], F32R)
    proj = pa("proj", [P, 16, T])
    brh = pa("brh", [P, NBR * CT, T], F32R)
    brl = pa("brl", [P, NBR * CT, T], F32R)
    merged = pa("merged", [P, KT, T])
    raw = [pa(f"raw{q}", [P, KT + CT, CH]) for q in range(2)]
    wh = [pa(f"wh{q}", [P, KT + CT, CH], F32R) for q in range(2)]
    wl = [pa(f"wl{q}", [P, KT + CT, CH], F32R) for q in range(2)]
    sig = [pa(f"sig{q}", [P, T]) for q in range(2)]
    prod = [pa(f"prod{q}", [P, T]) for q in range(2)]
    g1b = pa("g1b", [P, D])
    prm_rows = pa("prm_rows", [NPRM, BW])
    prm = pa("prm", [P, CT, NPRM])
    pool_rows = pa("pool_rows", [NB * HP, BW])
    conv_rows = pa("conv_rows", [NB * HC // 2, 2, BW])
    sconv_rows = pa("sconv_rows", [NB * HS, BW])
    ws_rows = pa("ws_rows", [P, 4, P])
    wsT = pa("wsT", [P, 4, P])
    wsS = pa("wsS", [NSM, 4, NSM])
    bS = pa("bS", [P, CT, P])
    pw = pa("pw", [P, CT, P])
    pext = pa("pext", [P, CT, EP])
    cext = pa("cext", [P, CT, EC])
    zext = pa("zext", [P, CT, ES])
    invc = pa("invc", [P, CT, NPR])
    cacc = pa("cacc", [P, CT, T])
    vn = pa("vn", [P, CT, T])
    sqb = pa("sqb", [P, CT, T])
    lnr = pa("lnr", [P, T])
    v_tok = pa("v_tok", [P, NT, BW])
    tail_sb = pa("tail_sb", [TAIL, 3, BW])
    proj_flat = proj[:, :, :].rearrange("p k t -> p (k t)")
    xs = proj_flat[:, 0:NT * D].rearrange("p (t d) -> p t d", t=NT)
    junk = proj_flat[:, 4 * D:5 * D]
    merged_flat = merged[:, :, :].rearrange("p k t -> p (k t)")
    sum2 = merged_flat[:, 0:CT * EP].rearrange("p (c e) -> p c e", c=CT)
    sum4 = merged_flat[:, CT * EP:2 * CT * EP].rearrange("p (c e) -> p c e", c=CT)
    sum8 = merged_flat[:, 2 * CT * EP:2 * CT * EP + EP]
    sum16 = sum2[:, 1, :]
    mixer.close()

    moe = ExitStack()

    def pb(name, shape, dt=F32):
        return sb(name, shape, dt, moe)

    wgu = [[pb(f"wgu{s}{j}", [P, 2, KT, F]) for j in range(2)] for s in range(2)]
    wd = [[pb(f"wd{s}{j}", [P, FK, D]) for j in range(2)] for s in range(2)]
    xn2T = pb("xn2T", [P, KT, T])
    xnh = pb("xnh", [P, NT, D], F32R)
    xnl = pb("xnl", [P, NT, D], F32R)
    xgT = pb("xgT", [P, KT, QS])
    onehot = pb("onehot", [P, NT, QE, CAP], F32R)
    onehot_s = pb("onehot_s", [P, NT, QE, CAP], F32R)
    slot_tok = pb("slot_tok", [P, 2, T], F32R)
    slot_w = pb("slot_w", [P, 2])
    yl = pb("yl", [P, 2, D], F32R)
    sg = [pb(f"sg{s}", [P, F]) for s in range(2)]
    hh = [pb(f"hh{s}", [P, F]) for s in range(2)]
    hhT = [pb(f"hhT{s}", [P, FK, P]) for s in range(2)]
    junk2 = xgT[:, :, :].rearrange("p k t -> p (k t)")[:, 0:D]
    lgt = pb("lgt", [P, NT, NG + NE])
    iog = pb("iog", [P, NT, NG])
    ioe = pb("ioe", [P, NT, NE])
    gsh = pb("gsh", [P, NT, NG])
    geq = pb("geq", [P, NT, NG])
    gex = pb("gex", [P, NT, NG])
    gmax = pb("gmax", [P, NT])
    gidx = pb("gidx", [P, NT])
    psel = pb("psel", [P, NT])
    lem = pb("lem", [P, NT, NE])
    eqm = pb("eqm", [P, NT, NE])
    oh = [pb(f"oh{w}", [P, NT, NE]) for w in range(2)]
    topv = [pb(f"topv{w}", [P, NT]) for w in range(2)]
    tidx = pb("tidx", [P, NT])
    tw = [pb(f"tw{w}", [P, NT]) for w in range(2)]
    both = pb("both", [P, NT, NE])
    pos = pb("pos", [P, NT, NE])
    over = pb("over", [P, NT, NE])
    cwt = pb("cwt", [P, NT, NE])
    cwo = pb("cwo", [P, NT, NE])
    rtmp = pb("rtmp", [P, NT, NE])
    slot_no = pb("slot_no", [P, CAP])
    ovs = pb("ovs", [P, 1])
    flag_i = pb("flag_i", [P, 1], I32)
    ov_cw = pb("ov_cw", [P, NT])
    ex = pb("ex", [P, NT])
    with nc.sbuf_tensor("xn2", [P, NT, D], F32) as xn2:
        pass
    yh = pb("yh", [P, 2, D], F32R)
    moe.close()

    w_in3 = a["w_in"][0].rearrange("(k p) n -> p k n", p=P)
    w_out3 = a["w_out"][0].rearrange("(k p) n -> p k n", p=P)
    w_br3 = a["w_branch"][0].rearrange("b (k p) n -> p (b k) n", p=P)
    x_rows = [a["x_prompt"][0, 0:128, :], a["x_prompt"][0, 128:256, :],
              a["x_sample"].rearrange("b s d -> (b s) d")]
    y_rows = [o["y_prompt"][0, 0:128, :], o["y_prompt"][0, 128:256, :],
              o["y_sample"].rearrange("b s d -> (b s) d")]
    w_gate4 = a["w_gate"][0].rearrange("e (p k) f -> e p k f", k=KT)
    w_up4 = a["w_up"][0].rearrange("e (p k) f -> e p k f", k=KT)
    w_down4 = a["w_down"][0].rearrange("e (p k) d -> e p k d", k=FK)

    def seg(ext, base, hist):
        return ext[:, :, base:base + NB * (hist + NS)].rearrange("p c (b s) -> p c b s", b=NB)

    def smp(ap):
        return ap[:, :, NPR:T].rearrange("p c (b s) -> p c b s", b=NB)

    N_SMALL = 8 + 3 + 1 + 4
    N_SMALL2 = 6
    raw_in = [sem("raw_in0"), sem("raw_in1")]
    wbr_in = [sem("wbr_in0"), sem("wbr_in1")]
    x_in = [sem(f"x_in{t}") for t in range(NT)]
    FIRST_OUT = N_PROJ + N_GATE

    ring = banks[0:3]
    psG = banks[3:5]
    psT = banks[5]
    psY = banks[6:8]
    BACK = [(t, half) for t in range(NT) for half in range(2)]
    IN_BANK = (0, 1, 2, 0)
    BACK_BANK = (1, 2, 0, 1, 2, 0)
    TURN_BANK = (1, 2)

    block = ctx.enter_context(nc.Block())

    @block.sync
    def _(sp):
        for t, (_, n) in enumerate(TILES):
            sp.dma_start(x_tok[0:n, t, :], x_rows[t]).then_inc(x_in[t], 16)
        sp.dma_start(g1b[:, :], a["norm1_g"][0:1, :].to_broadcast([P, D])).then_inc(sem("g1_in"), 16)

        def load_plain(c):
            src, n0 = (w_in3, c * CH) if c < N_PROJ else (w_out3, (c - FIRST_OUT) * CH)
            sp.dma_start(raw[c % 2][:, 0:KT, :], src[:, :, n0:n0 + CH]).then_inc(raw_in[c % 2], 16)

        load_plain(0)
        load_plain(1)
        small = sem("small_in")
        sp.dma_start(prm_rows[0:31, :], a["conf_dw"][0]).then_inc(small, 16)
        sp.dma_start(prm_rows[31:32, :], a["conf_dw_b"]).then_inc(small, 16)
        sp.dma_start(prm_rows[32:33, :], a["conf_ln_g"]).then_inc(small, 16)
        sp.dma_start(prm_rows[33:34, :], a["conf_ln_b"]).then_inc(small, 16)
        sp.dma_start(prm_rows[34:37, :], a["sconv_w"][0]).then_inc(small, 16)
        sp.dma_start(prm_rows[37:38, :], a["sgu_ln_g"]).then_inc(small, 16)
        sp.dma_start(prm_rows[38:39, :], a["sgu_ln_b"]).then_inc(small, 16)
        sp.dma_start(prm_rows[39:40, :], a["pool_scale"]).then_inc(small, 16)
        sp.dma_start(pool_rows[:, :], a["state_pool"][0].rearrange("b r c -> (b r) c")).then_inc(small, 16)
        sp.dma_start(conv_rows[:, :, :],
                     a["state_conv"][0].rearrange("(h b) r c -> (b r) h c", h=2)).then_inc(small, 16)
        sp.dma_start(sconv_rows[:, :], a["state_sconv"][0].rearrange("b r c -> (b r) c")).then_inc(small, 16)
        sp.dma_start(ws_rows[:, :, :], a["sgu_ws"][0].rearrange("h t s -> t h s")).then_inc(small, 16)
        for h in range(4):
            q = 64 * (h % 2)
            sp.dma_start(bS[q:q + 64, h // 2, :],
                         a["sgu_b"][0, h:h + 1, :].to_broadcast([64, P])).then_inc(small, 16)
        sp.wait_ge(sem("const_done"), 3)
        for g in range(4):
            q = 64 * (g % 2)
            sp.dma_start(pw[q:q + 64, g // 2, q:q + 64], a["pool_w"][0, g]).then_inc(sem("pw_in"), 16)

        for c in range(2, N_PROJ):
            sp.wait_ge(sem("lo_done"), c - 1)
            load_plain(c)
            if c == 3:
                s2 = sem("small2_in")
                sp.dma_start(g2b[:, :], a["norm2_g"][0:1, :].to_broadcast([P, D])).then_inc(s2, 16)
                sp.dma_start(gfb[:, :], a["final_g"].rearrange("(u d) -> u d", u=1).to_broadcast([P, D])).then_inc(s2, 16)
                sp.dma_start(rg[:, :, :], a["router_g"][0].rearrange("(p k) g -> p k g", k=KT)).then_inc(s2, 16)
                sp.dma_start(re[:, :, :], a["router_e"][0].rearrange("(p k) g -> p k g", k=KT)).then_inc(s2, 16)
                sp.dma_start(rb[:, 0:NG], a["router_g_b"][0:1, :].to_broadcast([P, NG])).then_inc(s2, 16)
                sp.dma_start(rb[:, NG:NG + NE], a["router_e_b"][0:1, :].to_broadcast([P, NE])).then_inc(s2, 16)
                sp.dma_start(o["pool_s"][0, :, 0:HP - NS, :],
                             a["state_pool"][0, :, NS:HP, :]).then_inc(sem("out_dma"), 16)
                sp.dma_start(o["conv_s"][0, :, 0:HC - NS, :],
                             a["state_conv"][0, :, NS:HC, :]).then_inc(sem("out_dma"), 16)
        with sp.Fori(0, NBR) as i:
            for m in range(4):
                q = m % 2
                sp.wait_ge(sem("lo_done"), i * 4 + (N_PROJ + m - 1))
                sp.dma_start(raw[q][:, 0:KT, :],
                             w_in3[:, :, bass.ds(i * D + (N_PROJ + m) * CH, CH)]).then_inc(raw_in[q], 16)
                sp.dma_start(raw[q][:, KT:KT + CT, :],
                             w_br3[:, bass.ds(i * CT, CT), m * CH:(m + 1) * CH]).then_inc(wbr_in[q], 16)
        for c in range(FIRST_OUT, FIRST_OUT + N_OUT):
            sp.wait_ge(sem("lo_done"), c - 1)
            load_plain(c)
            if c == FIRST_OUT + 1:
                sp.wait_ge(sem("v_tok_done"), 2)
                sp.dma_start(o["sguv_p"][0, 0], v_tok[:, 1, :]).then_inc(sem("out_dma"), 16)
                sp.dma_start(o["sguv_s"][0].rearrange("b s c -> (b s) c"),
                             v_tok[0:NSM, 2, :]).then_inc(sem("out_dma"), 16)
                sp.wait_ge(sem("tail_done"), 2)
                sp.dma_start(o["pool_p"][0, 0], tail_sb[32 - HP:32, 0, :]).then_inc(sem("out_dma"), 16)
                sp.dma_start(o["conv_p"][0, 0], tail_sb[32 - HC:32, 1, :]).then_inc(sem("out_dma"), 16)
                sp.dma_start(o["sconv_p"][0, 0], tail_sb[32 - HS:32, 2, :]).then_inc(sem("out_dma"), 16)
                sp.dma_start(tail_dram.rearrange("x r c -> r x c"),
                             tail_sb[32:TAIL, :, :]).then_inc(sem("tail_out"), 16)

        sp.wait_ge(sem("wo_mm"), NT * N_OUT)
        sp.wait_ge(sem("out_dma"), 16 * 7)
        sp.wait_ge(sem("tail_out"), 16)
        sp.wait_ge(sem("wsS_in"), 16 * NB)

        def load_pair(p, s):
            for j in range(2):
                e = p * 2 + j
                sp.dma_start(wgu[s][j][:, 0, :, :], w_gate4[e]).then_inc(sem(f"wgu_in{s}"), 16)
                sp.dma_start(wgu[s][j][:, 1, :, :], w_up4[e]).then_inc(sem(f"wgu_in{s}"), 16)

        def load_down(p, s):
            for j in range(2):
                sp.dma_start(wd[s][j][:, :, :], w_down4[p * 2 + j]).then_inc(sem(f"wd_in{s}"), 16)

        load_pair(0, 0)
        load_pair(1, 1)
        load_down(0, 0)
        sp.dma_start(o["pool_s"][0, :, HP - NS:HP, :],
                     tail_dram[0].rearrange("(b s) c -> b s c", b=NB)).then_inc(sem("out_dma"), 16)
        sp.dma_start(o["conv_s"][0, :, HC - NS:HC, :],
                     tail_dram[1].rearrange("(b s) c -> b s c", b=NB)).then_inc(sem("out_dma"), 16)
        sp.dma_start(o["sconv_s"][0],
                     tail_dram[2].rearrange("(b s) c -> b s c", b=NB)[:, NS - HS:NS, :]).then_inc(sem("out_dma"), 16)

        def load_quad(i):
            sp.wait_ge(sem("gu_mm"), i * 2 + 1)
            load_pair(i * 2 + 2, 0)
            if not isinstance(i, int):
                sp.wait_ge(sem("dn_mm"), i * 2)
            load_down(i * 2 + 1, 1)
            sp.wait_ge(sem("gu_mm"), i * 2 + 2)
            load_pair(i * 2 + 3, 1)
            sp.wait_ge(sem("dn_mm"), i * 2 + 1)
            load_down(i * 2 + 2, 0)

        load_quad(0)
        with sp.Fori(1, QUADS - 1) as i:
            load_quad(i)
        sp.wait_ge(sem("dn_mm"), PAIRS - 2)
        load_down(PAIRS - 1, 1)

        sp.wait_ge(sem("flag_ready"), 1)
        flag = sp.value_load(flag_i[0:1, 0:1], min_val=0, max_val=2 * T)
        with sp.If(flag > 0):
            with sp.Fori(0, NE) as e:
                sp.wait_ge(sem("ov_free"), e + 1)
                sp.dma_start(wgu[0][0][:, 0, :, :], w_gate4[e]).then_inc(sem("ov_in"), 16)
                sp.dma_start(wgu[0][0][:, 1, :, :], w_up4[e]).then_inc(sem("ov_in"), 16)
                sp.dma_start(wd[0][0][:, :, :], w_down4[e]).then_inc(sem("ov_in"), 16)
            sp.wait_ge(sem("ov_free"), NE + 1)

        for t, (_, n) in enumerate(TILES):
            sp.wait_ge(sem("y_done"), t + 1)
            sp.dma_start(y_rows[t], x_tok[0:n, t, :]).then_inc(sem("out_dma"), 16)
        sp.wait_ge(sem("out_dma"), 16 * (7 + 3 + NT))

    @block.gpsimd
    def _(pool):
        g = nc.gpsimd
        const = sem("const_done")
        g.memset(ss[:, :], 1.0)
        g.memset(epsb[:, :], LN_EPS)
        g.memset(pw[:, :, :], 0.0).then_inc(const, 1)
        g.memset(ident[:, :], 0.0).then_inc(const, 1)
        pool.wait_ge(const, 2)
        g.affine_select(out=ident[:, :], in_=ident[:, :], compare_op=ALU.not_equal, fill=1.0, base=0,
                        pattern=[[-1, P]], channel_multiplier=1).then_inc(const, 1)
        g.memset(before[:, :], 1.0).then_inc(const, 1)
        g.iota(invc[:, :, :], pattern=[[0, CT], [1, NPR]], base=1, channel_multiplier=0,
               allow_small_or_imprecise_dtypes=True)
        pool.wait_ge(const, 4)
        g.affine_select(out=before[:, :], in_=before[:, :], compare_op=ALU.is_gt, fill=0.0, base=0,
                        pattern=[[1, P]], channel_multiplier=-1).then_inc(const, 1)
        g.memset(ones[:, :], 1.0)
        g.memset(mean_w[:, :], 1.0 / BW)
        g.memset(wsS[:, :, :], 0.0)
        g.memset(pext[:, :, 0:HP], 0.0)
        g.memset(cext[:, :, 0:HC], 0.0)
        g.memset(zext[:, :, 0:HS], 0.0).then_inc(const, 1)

        def lo(c, q, kn):
            pool.wait_ge(sem("hi_done"), c + 1)
            g.tensor_tensor(wl[q][:, 0:kn, :], raw[q][:, 0:kn, :], wh[q][:, 0:kn, :].bitcast(F32),
                            ALU.subtract).then_inc(sem("lo_done"), 1)

        lo(0, 0, KT)
        lo(1, 1, KT)
        pool.wait_ge(sem("small_in"), 16 * N_SMALL)
        g.affine_select(out=ws_rows[:, :, :], in_=ws_rows[:, :, :], compare_op=ALU.is_ge, fill=0.0, base=0,
                        pattern=[[0, 4], [-1, P]], channel_multiplier=1).then_inc(sem("ws_masked"), 1)
        with pool.Fori(1, N_PROJ // 2) as i:
            for q in range(2):
                lo(i * 2 + q, q, KT)
        pool.wait_ge(sem("pool_ready"), 1)
        g.memset(merged[:, :, :], 0.0).then_inc(sem("merged_zero"), 1)
        pool.wait_ge(sem("small2_in"), 16 * N_SMALL2)
        g.tensor_copy(rw[:, :, 0:NG], rg[:, :, :])
        g.tensor_copy(rw[:, :, NG:NG + NE], re[:, :, :]).then_inc(sem("rw_done"), 1)
        with pool.Fori(0, N_GATE // 2) as i:
            for q in range(2):
                lo(i * 2 + (N_PROJ + q), q, KT + CT)
        with pool.Fori(0, N_OUT // 2) as i:
            for q in range(2):
                lo(i * 2 + (FIRST_OUT + q), q, KT)

        pool.wait_ge(sem("wo_mm"), NT * N_OUT)
        pool.wait_ge(sem("out_dma"), 16 * 7)
        pool.wait_ge(sem("tail_out"), 16)
        g.iota(iog[:, :, :], pattern=[[0, NT], [1, NG]], base=-NG, channel_multiplier=0,
               allow_small_or_imprecise_dtypes=True)
        g.iota(ioe[:, :, :], pattern=[[0, NT], [1, NE]], base=-NE, channel_multiplier=0,
               allow_small_or_imprecise_dtypes=True)
        g.iota(slot_no[:, :], pattern=[[1, CAP]], base=0, channel_multiplier=0,
               allow_small_or_imprecise_dtypes=True)
        g.memset(lgt[:, :, :], 0.0).then_inc(sem("moe_const"), 1)
        for t, (_, n) in enumerate(TILES):
            pool.wait_ge(sem("xn_hi"), t + 1)
            g.tensor_tensor(xnl[0:n, t, :], xn2[0:n, t, :], xnh[0:n, t, :].bitcast(F32),
                            ALU.subtract).then_inc(sem("xn_lo"), 1)

    @block.tensor
    def _(pe):
        mm, tr = nc.tensor.matmul, nc.tensor.transpose
        pe.wait_ge(sem("const_done"), 3)
        for u in range(2 * NT):
            t, h = u // 2, u % 2
            n = TILES[t][1]
            pe.wait_ge(sem("xs_done"), t + 1)
            for m in range(4):
                k = 4 * h + m
                last = tr(banks[u][:, m * P:m * P + n], xs[0:n, t, k * P:(k + 1) * P], ident[0:n, 0:n])
            last.then_inc(sem("xT_mm"), 1)

        def prepare():
            pe.wait_ge(sem("small_in"), 16 * N_SMALL)
            pe.wait_ge(sem("ws_masked"), 1)
            for ct in range(CT):
                cs = slice(ct * P, (ct + 1) * P)
                n = NB * HP
                tr(banks[6][:, ct * n:(ct + 1) * n], pool_rows[:, cs], ident[0:n, 0:n])
                tr(banks[6][:, 240 + ct * 16:256 + ct * 16], sconv_rows[:, cs], ident[0:16, 0:16])
                last = tr(banks[6][:, 272 + ct * NPRM:272 + (ct + 1) * NPRM], prm_rows[:, cs], ident[0:NPRM, 0:NPRM])
            last.then_inc(sem("prep_mm"), 1)
            n = NB * HC // 2
            for h in range(2):
                for ct in range(CT):
                    last = tr(banks[7][:, (2 * h + ct) * n:(2 * h + ct + 1) * n],
                              conv_rows[:, h, ct * P:(ct + 1) * P], ident[0:n, 0:n])
            last.then_inc(sem("prep_mm"), 1)
            for h in range(4):
                last = tr(banks[4][:, h * P:(h + 1) * P], ws_rows[:, h, :], ident[:, :])
            last.then_inc(sem("prep_mm"), 1)

        def split_product(out, wq, k0, kn, cols, mh, ml, m0):
            for k in range(kn):
                w_h, w_l = wh[wq][:, k0 + k, cols], wl[wq][:, k0 + k, cols]
                mm(out, w_h, mh(m0 + k), start=(k == 0), stop=False)
                mm(out, w_h, ml(m0 + k), start=False, stop=False)
                last = mm(out, w_l, mh(m0 + k), start=False, stop=(k == kn - 1))
            return last

        def proj_chunk(c, q, par, first):
            pe.wait_ge(sem("lo_done"), c + 1)
            for j in range(2):
                if not first:
                    pe.wait_ge(sem("pj_ev"), c * 2 + (j - 3))
                split_product(banks[2 * par + j][:, 0:T], q, 0, KT, slice(j * P, (j + 1) * P),
                              lambda k: xh[:, k, :], lambda k: xl[:, k, :], 0).then_inc(sem("pj_mm"), 1)

        pe.wait_ge(sem("xT_lo"), 2 * NT)
        proj_chunk(0, 0, 0, True)
        prepare()
        proj_chunk(1, 1, 1, True)
        proj_chunk(2, 0, 0, False)
        proj_chunk(3, 1, 1, False)
        pe.wait_ge(sem("pool_ready"), 1)
        pe.wait_ge(sem("pw_in"), 64)
        pe.wait_ge(sem("prep_done"), 3)
        for ct in range(CT):
            last = mm(banks[6 + ct][:, 0:T], pw[:, ct, :], vn[:, ct, :], start=True, stop=True)
        last.then_inc(sem("map_mm"), 1)
        with pe.Fori(2, N_PROJ // 2) as i:
            for q in range(2):
                proj_chunk(i * 2 + q, q, q, False)

        def channel_mean(bank, src):
            for ct in range(CT):
                last = mm(bank[:, 0:T], mean_w[:, :], src[:, ct, :], start=(ct == 0), stop=(ct == CT - 1))
            last.then_inc(sem("ln_mm"), 1)

        def v_mean():
            pe.wait_ge(sem("gelu_done"), 1)
            pe.wait_ge(sem("br_ready"), 1)
            channel_mean(banks[6], proj[:, 14:16, :])

        def v_var():
            pe.wait_ge(sem("ln_sq"), 1)
            channel_mean(banks[7], sqb)

        def b_mean():
            pe.wait_ge(sem("conv_step"), 4 * CW)
            pe.wait_ge(sem("ln_cent"), 1)
            channel_mean(banks[6], cacc)

        def b_var():
            pe.wait_ge(sem("ln_sq"), 2)
            pe.wait_ge(sem("ln_root"), 1)
            channel_mean(banks[7], sqb)

        def v_rows():
            pe.wait_ge(sem("v_norm"), 1)
            pe.wait_ge(sem("ln_cent"), 2)
            pe.wait_ge(sem("ln_root"), 2)
            for t, (t0, n) in enumerate(TILES):
                for ct in range(CT):
                    out = banks[6 + t // 2][0:n, (t % 2) * BW + ct * P:(t % 2) * BW + (ct + 1) * P]
                    last = tr(out, vn[:, ct, t0:t0 + n], ident[:, :])
            last.then_inc(sem("vT_mm"), 1)

        def v_mix():
            pe.wait_ge(sem("v_tok_done"), 2)
            pe.wait_ge(sem("wsS_in"), 16 * NB)
            for h in range(4):
                q, ct = 64 * (h % 2), h // 2
                hc = slice(h * 64, (h + 1) * 64)
                for n in range(2):
                    mm(banks[6 + ct][q:q + 64, n * P:(n + 1) * P], v_tok[:, n, hc], wsT[:, h, :],
                       start=True, stop=True, tile_position=(0, q))
                last = mm(banks[6 + ct][q:q + 64, NPR:T], v_tok[0:NSM, 2, hc], wsS[:, h, :],
                          start=True, stop=True, tile_position=(0, q))
            last.then_inc(sem("mix_mm"), 1)

        def tails():
            pe.wait_ge(sem("z_done"), 1)
            pe.wait_ge(sem("mix_read"), 2)
            for x, k0 in enumerate((0, 2, 8)):
                for ct in range(CT):
                    out = banks[6 + x // 2][0:TAIL, (x % 2) * BW + ct * P:(x % 2) * BW + (ct + 1) * P]
                    last = tr(out, proj[:, k0 + ct, T - TAIL:T], ident[:, :])
            last.then_inc(sem("tail_mm"), 1)

        def gate_tile(i, j, extra=None):
            q, cols = (j // 2) % 2, slice((j % 2) * P, (j % 2 + 1) * P)
            g = i * 8 + j
            if j % 2 == 0:
                pe.wait_ge(sem("lo_done"), i * 4 + (N_PROJ + j // 2 + 1))
            if isinstance(i, int) and g < 4:
                pe.wait_ge(sem("pj_ev"), 13 + g)
            else:
                pe.wait_ge(sem("gate_sg"), g - 3)
            split_product(banks[j % 4][:, 0:T], q, 0, KT, cols,
                          lambda k: xh[:, k, :], lambda k: xl[:, k, :], 0).then_inc(sem("gate_mm"), 1)
            pe.wait_ge(sem("br_ready"), i + 1)
            if not (isinstance(i, int) and g < 2):
                pe.wait_ge(sem("gp_done"), g - 1)
            out = banks[4 + j % 2][:, 0:T]
            split_product(out, q, KT, CT, cols, lambda k: brh[:, i * CT + k, :],
                          lambda k: brl[:, i * CT + k, :], 0).then_inc(sem("br_mm"), 1)
            if extra:
                extra()

        inserts = [v_mean, v_var, b_mean, b_var, v_rows, v_mix, tails, None]
        for j in range(8):
            gate_tile(0, j, inserts[j])
        with pe.Fori(1, NBR) as i:
            for j in range(8):
                gate_tile(i, j)

        pe.wait_ge(sem("mg_lo"), 4)
        pe.wait_ge(sem("tail_done"), 2)
        for c in range(N_OUT):
            q = c % 2
            pe.wait_ge(sem("lo_done"), FIRST_OUT + c + 1)
            for t, (t0, n) in enumerate(TILES):
                out = banks[3 * q + t][0:n, 0:CH]
                if c >= 2:
                    pe.wait_ge(sem("wo_add"), NT * (c - 2) + t + 1)
                for k in range(KT):
                    mh, ml = brh[:, k, t0:t0 + n], brl[:, k, t0:t0 + n]
                    mm(out, mh, wh[q][:, k, :], start=(k == 0), stop=False)
                    mm(out, mh, wl[q][:, k, :], start=False, stop=False)
                    last = mm(out, ml, wh[q][:, k, :], start=False, stop=(k == KT - 1))
                last.then_inc(sem("wo_mm"), 1)

        for u in range(2 * NT):
            t, h = u // 2, u % 2
            n = TILES[t][1]
            pe.wait_ge(sem("n2_done"), t + 1)
            if u == 0:
                pe.wait_ge(sem("wo_add"), NT * N_OUT)
            for m in range(4):
                k = 4 * h + m
                last = tr(banks[u][:, m * P:m * P + n], xn2[0:n, t, k:D:KT], ident[0:n, 0:n])
            last.then_inc(sem("n2T_mm"), 1)
        pe.wait_ge(sem("n2T_act"), NT)
        pe.wait_ge(sem("n2T_dve"), NT)
        pe.wait_ge(sem("rw_done"), 1)
        for t, (t0, n) in enumerate(TILES):
            for k in range(KT):
                last = mm(banks[6][0:n, t * 64:t * 64 + NG + NE], xn2T[:, k, t0:t0 + n], rw[:, k, :],
                          start=(k == 0), stop=(k == KT - 1))
        last.then_inc(sem("lg_mm"), 1)
        pe.wait_ge(sem("both_done"), 1)
        for t in range(NT):
            for u in range(t + 1):
                last = mm(banks[7][:, t * NE:(t + 1) * NE], (before if u == t else ones)[:, :], both[:, u, :],
                          start=(u == 0), stop=(u == t))
        last.then_inc(sem("cum_mm"), 1)
        pe.wait_ge(sem("ovs_done"), 1)
        mm(banks[7][:, 256:257], ones[:, :], ovs[:, :], start=True, stop=True).then_inc(sem("ovs_mm"), 1)

        def rows_in(i):
            pe.wait_ge(sem("g_built"), i + 1)
            for u in range(4):
                if not (isinstance(i, int) and i == 0):
                    if u == 0:
                        pe.wait_ge(sem("xg_done"), i * 4)
                    elif u == 3:
                        pe.wait_ge(sem("xg_done"), i * 4 + 1)
                elif u == 3:
                    pe.wait_ge(sem("xg_done"), 1)
                for j in range(2):
                    k = 2 * u + j
                    out = ring[IN_BANK[u]][:, j * QS:(j + 1) * QS]
                    for t, (_, n) in enumerate(TILES):
                        slots = onehot[0:n, t, :, :].rearrange("p e c -> p (e c)")
                        mm(out, xnh[0:n, t, k:D:KT], slots, start=(t == 0), stop=False)
                        last = mm(out, xnl[0:n, t, k:D:KT], slots, start=False, stop=(t == NT - 1))
                last.then_inc(sem("ga_mm"), 1)

        def weights_in(i):
            pe.wait_ge(sem("cwt_done"), 1)
            for m in range(2):
                for t, (_, n) in enumerate(TILES):
                    slots = onehot[0:n, t, 2 * m:2 * m + 2, :].rearrange("p e c -> p (e c)").bitcast(F32)
                    last = mm(psT[:, 256 + 2 * m:258 + 2 * m], slots, cwt[0:n, t, bass.ds(i * QE + 2 * m, 2)],
                              start=(t == 0), stop=(t == NT - 1))
            last.then_inc(sem("cw_mm"), 1)

        def gate_up(p, s, i):
            pe.wait_ge(sem("xg_done"), i * 4 + 4)
            pe.wait_ge(sem(f"wgu_in{s}"), i * 64 + 64)
            if not (isinstance(p, int) and p < 2):
                pe.wait_ge(sem("h_done"), p - 1)
            for k in range(KT):
                for j in range(2):
                    q = 64 * j
                    last = mm(psG[s][q:q + 64, :].rearrange("p (w f) -> p w f", w=2),
                              xgT[:, k, (2 * s + j) * CAP:(2 * s + j + 1) * CAP],
                              wgu[s][j][:, :, k, :], start=(k == 0), stop=(k == KT - 1), tile_position=(0, q))
            last.then_inc(sem("gu_mm"), 1)

        def turn_hidden(p, s, i):
            pe.wait_ge(sem("h_done"), p + 1)
            pe.wait_ge(sem("cw_ev"), i + 1)
            if not (isinstance(p, int) and p == 0):
                pe.wait_ge(sem("hte_done"), p)
            for k in range(FK):
                last = tr(psT[:, k * P:(k + 1) * P], hh[s][:, k:F:FK], ident[:, :])
            last.then_inc(sem("ht_mm"), 1)

        def down(p, s, i):
            pe.wait_ge(sem("hte_done"), p + 1)
            pe.wait_ge(sem(f"wd_in{s}"), i * 32 + 32)
            if not (isinstance(p, int) and p == 0):
                pe.wait_ge(sem("yl_done"), p * 2)
            for half in range(2):
                for k in range(FK):
                    for j in range(2):
                        q = 64 * j
                        last = mm(psY[half][q:q + 64, :], hhT[s][:, k, q:q + 64],
                                  wd[s][j][:, k, half * 512:(half + 1) * 512],
                                  start=(k == 0), stop=(k == FK - 1), tile_position=(0, q))
            last.then_inc(sem("dn_mm"), 1)

        def back(i, after):
            pe.wait_ge(sem("yl_done"), i * 4 + 4)
            pe.wait_ge(sem("st_ev"), i * 2 + 2)
            for u, (t, half) in enumerate(BACK):
                t0, n = TILES[t]
                if u >= 3:
                    pe.wait_ge(sem("sc_add"), i * 6 + (u - 2))
                elif after == "rows":
                    pe.wait_ge(sem("xg_done"), i * 4 + (10 + u))
                out = ring[BACK_BANK[u]][0:n, :]
                for m in range(2):
                    for y, first in ((yh, True), (yl, False)):
                        last = mm(out, slot_tok[:, m, t0:t0 + n], y[:, m, half * 512:(half + 1) * 512],
                                  start=(m == 0 and first), stop=(m == 1 and not first))
                last.then_inc(sem("sc_mm"), 1)

        def turn_slots(i):
            pe.wait_ge(sem("gs_built"), i + 1)
            for m in range(2):
                if isinstance(i, int) and i == 0:
                    pe.wait_ge(sem("xg_done"), 4 + 2 + m)
                else:
                    pe.wait_ge(sem("sc_add"), i * 6)
                for t, (t0, n) in enumerate(TILES):
                    last = tr(ring[TURN_BANK[m]][:, t0:t0 + n],
                              onehot_s[0:n, t, 2 * m:2 * m + 2, :].rearrange("p e c -> p (e c)").bitcast(F32),
                              ident[0:n, 0:n])
                last.then_inc(sem("st_mm"), 1)

        def quad(i):
            first, end = isinstance(i, int) and i == 0, isinstance(i, int) and i == QUADS - 1
            if not first:
                turn_hidden(i * 2 - 1, 1, i)
            gate_up(i * 2, 0, i)
            if not first:
                down(i * 2 - 1, 1, i - 1)
            gate_up(i * 2 + 1, 1, i)
            turn_hidden(i * 2, 0, i)
            if not end:
                rows_in(i + 1)
                pe.wait_ge(sem("hte_done"), i * 2 + 1)
                weights_in(i + 1)
            if not first:
                back(i - 1, None if end else "rows")
            down(i * 2, 0, i)
            turn_slots(i)

        pe.wait_ge(sem("xn_lo"), NT)
        rows_in(0)
        weights_in(0)
        pe.wait_ge(sem("flag_ready"), 1)
        quad(0)
        with pe.Fori(1, QUADS - 1) as i:
            quad(i)
        quad(QUADS - 1)
        turn_hidden(PAIRS - 1, 1, QUADS - 1)
        down(PAIRS - 1, 1, QUADS - 1)

        flag = pe.value_load(flag_i[0:1, 0:1], min_val=0, max_val=2 * T)
        with pe.If(flag > 0):
            pe.wait_ge(sem("ov_free"), 1)
            with pe.Fori(0, NE) as e:
                pe.wait_ge(sem("ov_in"), e * 48 + 48)
                for t, (t0, n) in enumerate(TILES):
                    pe.wait_ge(sem("ov_acc"), e * NT + (t + 1))
                    for k in range(KT):
                        last = mm(psG[0][0:n, :].rearrange("p (w f) -> p w f", w=2), xn2T[:, k, t0:t0 + n],
                                  wgu[0][0][:, :, k, :], start=(k == 0), stop=(k == KT - 1))
                    last.then_inc(sem("ov_gu"), 1)
                    pe.wait_ge(sem("ov_h"), e * NT + (t + 1))
                    for k in range(FK):
                        last = tr(psT[:, k * P:(k + 1) * P], hh[0][:, k:F:FK], ident[:, :])
                    last.then_inc(sem("ov_ht"), 1)
                    pe.wait_ge(sem("ov_hte"), e * NT + (t + 1))
                    for half in range(2):
                        for k in range(FK):
                            last = mm(psY[half][0:n, :], hhT[0][:, k, 0:n],
                                      wd[0][0][:, k, half * 512:(half + 1) * 512],
                                      start=(k == 0), stop=(k == FK - 1))
                    last.then_inc(sem("ov_dn"), 1)
        back(QUADS - 1, None)

    @block.scalar
    def _(act):
        f = nc.scalar.activation
        act.wait_ge(sem("const_done"), 1)
        for t, (_, n) in enumerate(TILES):
            act.wait_ge(x_in[t], 16)
            if t:
                act.wait_ge(sem("x_sq"), t)
            f(junk[0:n, :], x_tok[0:n, t, :], ACT.Square, accum_out=ss[0:n, t:t + 1]).then_inc(sem("x_sq"), 1)
        act.wait_ge(sem("x_ms"), 1)
        f(root[:, :], ms[:, :], ACT.Sqrt).then_inc(sem("x_root"), 1)

        def hi(c, q, kn):
            act.wait_ge(raw_in[q], (c - q) // 2 * 16 + 16 if isinstance(c, int) else c * 8 + (16 - 8 * q))
            if kn > KT:
                n = (c - N_PROJ - q) // 2 * 16 + 16 if isinstance(c, int) else c * 8 + (16 - 8 * q - 8 * N_PROJ)
                act.wait_ge(wbr_in[q], n)
            f(wh[q][:, 0:kn, :], raw[q][:, 0:kn, :], ACT.Copy).then_inc(sem("hi_done"), 1)

        hi(0, 0, KT)
        hi(1, 1, KT)
        for u in range(2 * NT):
            t, h = u // 2, u % 2
            t0, n = TILES[t]
            act.wait_ge(sem("xT_mm"), u + 1)
            f(xh[:, 4 * h:4 * h + 4, t0:t0 + n],
              banks[u][:, :].rearrange("p (k c) -> p k c", c=P)[:, :, 0:n], ACT.Copy).then_inc(sem("xT_hi"), 1)
        for c in range(N_PROJ):
            for tl in (2 * c, 2 * c + 1):
                act.wait_ge(sem("pj_mm"), tl + 1)
                f(proj[:, tl, :], banks[tl % 4][:, 0:T], ACT.Copy).then_inc(sem("pj_ev"), 1)
            hi(c + 2, c % 2, KT if c + 2 < N_PROJ else KT + CT)
            if c == 1:
                act.wait_ge(sem("prep_done"), 3)
                act.wait_ge(sem("const_done"), 6)
                for b in range(NB):
                    act.dma_start(wsS[b * NS:(b + 1) * NS, :, b * NS:(b + 1) * NS],
                                  wsT[0:NS, :, 0:NS]).then_inc(sem("wsS_in"), 16)
            if c == 2:
                act.wait_ge(sem("pj_ev"), 6)
                f(proj[:, 4:6, :], proj[:, 4:6, :], ACT.Sigmoid).then_inc(sem("glu_gate"), 1)
            if c == 3:
                act.wait_ge(sem("map_mm"), 1)
                for ct in range(CT):
                    last = f(brh[:, ct, :], banks[6 + ct][:, 0:T], ACT.Copy, scale=prm[:, ct, PRM["ps"]:PRM["ps"] + 1])
                last.then_inc(sem("br_hi"), 1)
        act.wait_ge(sem("pj_ev"), 16)
        f(proj[:, 12:16, :], proj[:, 12:16, :], ACT.Gelu_apprx_tanh).then_inc(sem("gelu_done"), 1)

        def gate(i, j):
            g = i * 8 + j
            act.wait_ge(sem("gate_mm"), g + 1)
            if not (isinstance(i, int) and g < 2):
                act.wait_ge(sem("gp_done"), g - 1)
            f(sig[j % 2][:, :], banks[j % 4][:, 0:T], ACT.Sigmoid).then_inc(sem("gate_sg"), 1)

        def next_hi(i, j, kn=KT + CT):
            act.wait_ge(sem("br_mm"), i * 8 + (j + 1))
            hi(i * 4 + (N_PROJ + j // 2 + 2), (j // 2) % 2, kn)

        def square(n):
            act.wait_ge(sem("ln_cent"), n)
            if n == 2:
                act.wait_ge(sem("ln_mm"), 2)
            f(sqb[:, :, :], (vn if n == 1 else cacc)[:, :, :], ACT.Square).then_inc(sem("ln_sq"), 1)

        def sqrt(n):
            act.wait_ge(sem("ln_mm"), 2 * n)
            if n == 2:
                act.wait_ge(sem("v_norm"), 1)
            f(lnr[:, :], banks[7][:, 0:T], ACT.Sqrt, bias=epsb[:, 0:1]).then_inc(sem("ln_root"), 1)

        def br_high(n, src):
            act.wait_ge(sem("br_val"), n)
            f(brh[:, n * CT:(n + 1) * CT, :], src, ACT.Copy).then_inc(sem("br_hi"), 1)

        gate(0, 0)
        square(1)
        gate(0, 1)
        next_hi(0, 1)
        sqrt(1)
        gate(0, 2)
        square(2)
        gate(0, 3)
        next_hi(0, 3)
        sqrt(2)
        gate(0, 4)
        act.wait_ge(sem("b_norm"), 1)
        f(sqb[:, :, :], cacc[:, :, :], ACT.Sigmoid).then_inc(sem("silu_gate"), 1)
        gate(0, 5)
        next_hi(0, 5)
        br_high(1, cacc[:, :, :])
        gate(0, 6)
        gate(0, 7)
        next_hi(0, 7)
        br_high(2, vn[:, :, :])
        br_high(3, proj[:, 12:14, :])
        with act.Fori(1, NBR - 1) as i:
            for j in range(8):
                gate(i, j)
                if j % 2:
                    next_hi(i, j)
        for j in range(8):
            gate(NBR - 1, j)
            if j % 2:
                next_hi(NBR - 1, j, KT + CT if j < 4 else KT)
        for n in range(4):
            act.wait_ge(sem("mg_add"), 26 + 2 * n)
            f(brh[:, 2 * n:2 * n + 2, :], merged[:, 2 * n:2 * n + 2, :], ACT.Copy).then_inc(sem("mg_hi"), 1)
        for c in (FIRST_OUT + 2, FIRST_OUT + 3):
            act.wait_ge(sem("wo_mm"), NT * (c - FIRST_OUT - 1))
            hi(c, c % 2, KT)

        for t, (_, n) in enumerate(TILES):
            act.wait_ge(sem("wo_add"), NT * (N_OUT - 1) + t + 1)
            if t:
                act.wait_ge(sem("n2_sq"), t)
            else:
                act.wait_ge(sem("wo_mm"), NT * N_OUT)
                act.wait_ge(sem("out_dma"), 16 * 7)
                act.wait_ge(sem("tail_out"), 16)
            f(junk2[0:n, :], x_tok[0:n, t, :], ACT.Square, accum_out=ss[0:n, t:t + 1]).then_inc(sem("n2_sq"), 1)
        act.wait_ge(sem("n2_ms"), 1)
        f(root[:, :], ms[:, :], ACT.Sqrt).then_inc(sem("n2_root"), 1)
        for t, (t0, n) in enumerate(TILES):
            act.wait_ge(sem("n2T_mm"), 2 * t + 1)
            f(xn2T[:, 0:4, t0:t0 + n], banks[2 * t][:, :].rearrange("p (k c) -> p k c", c=P)[:, :, 0:n],
              ACT.Copy).then_inc(sem("n2T_act"), 1)
        for t, (_, n) in enumerate(TILES):
            f(xnh[0:n, t, :], xn2[0:n, t, :], ACT.Copy).then_inc(sem("xn_hi"), 1)
        act.wait_ge(sem("gsh_done"), 1)
        f(gex[:, :, :], gsh[:, :, :], ACT.Exp).then_inc(sem("rt_exp"), 1)
        act.wait_ge(sem("tdiff_done"), 1)
        f(ex[:, :], tidx[:, :], ACT.Exp).then_inc(sem("rt_exp"), 1)

        def rows_out(i):
            for u in range(4):
                act.wait_ge(sem("ga_mm"), i * 4 + (u + 1))
                f(xgT[:, 2 * u:2 * u + 2, :], ring[IN_BANK[u]][:, :].rearrange("p (k c) -> p k c", k=2),
                  ACT.Copy).then_inc(sem("xg_done"), 1)

        def silu(p, s):
            act.wait_ge(sem("gu_mm"), p + 1)
            if not (isinstance(p, int) and p < 2):
                act.wait_ge(sem("h_done"), p - 1)
            f(sg[s][:, :], psG[s][:, 0:F], ACT.Silu).then_inc(sem("sg_done"), 1)

        def y_high(p, s):
            act.wait_ge(sem("dn_mm"), p + 1)
            for half in range(2):
                f(yh[:, s, half * 512:(half + 1) * 512], psY[half][:, :], ACT.Copy).then_inc(sem("yh_done"), 1)

        def slots_out(i):
            for m in range(2):
                act.wait_ge(sem("st_mm"), i * 2 + (m + 1))
                f(slot_tok[:, m, :], ring[TURN_BANK[m]][:, 0:T], ACT.Copy).then_inc(sem("st_ev"), 1)

        def quad(i):
            first, end = isinstance(i, int) and i == 0, isinstance(i, int) and i == QUADS - 1
            silu(i * 2, 0)
            if not first:
                y_high(i * 2 - 1, 1)
            silu(i * 2 + 1, 1)
            if not end:
                rows_out(i + 1)
            y_high(i * 2, 0)
            slots_out(i)

        rows_out(0)
        act.wait_ge(sem("xn_lo"), NT)
        quad(0)
        with act.Fori(1, QUADS - 1) as i:
            quad(i)
        quad(QUADS - 1)
        y_high(PAIRS - 1, 1)

        act.wait_ge(sem("flag_ready"), 1)
        flag = act.value_load(flag_i[0:1, 0:1], min_val=0, max_val=2 * T)
        with act.If(flag > 0):
            with act.Fori(0, NE) as e:
                for t, (_, n) in enumerate(TILES):
                    act.wait_ge(sem("ov_gu"), e * NT + (t + 1))
                    f(sg[0][0:n, :], psG[0][0:n, 0:F], ACT.Silu).then_inc(sem("ov_sg"), 1)

        for t, (_, n) in enumerate(TILES):
            act.wait_ge(sem("sc_add"), 6 * (QUADS - 1) + 2 * t + 2)
            if t:
                act.wait_ge(sem("f_sq"), t)
            f(junk2[0:n, :], x_tok[0:n, t, :], ACT.Square, accum_out=ss[0:n, t:t + 1]).then_inc(sem("f_sq"), 1)
        for t in range(NT):
            act.wait_ge(sem("f_ms"), t + 1)
            f(root[:, t:t + 1], ms[:, t:t + 1], ACT.Sqrt).then_inc(sem("f_root"), 1)

    @block.vector
    def _(dve):
        v = nc.vector
        own = Steps(dve, "dve_step")

        def mean_square(ready, count, done):
            dve.wait_ge(sem(ready), count)
            v.tensor_scalar(ms[:, :], ss[:, :], 1.0 / D, RMS_EPS, ALU.mult, ALU.add).then_inc(sem(done), 1)

        mean_square("x_sq", NT, "x_ms")
        dve.wait_ge(sem("x_root"), 1)
        own.step(v.reciprocal(rstd[:, :], root[:, :]))
        own.last()
        dve.wait_ge(sem("g1_in"), 16)
        for t, (_, n) in enumerate(TILES):
            v.scalar_tensor_tensor(xs[0:n, t, :], x_tok[0:n, t, :], rstd[0:n, t:t + 1], g1b[0:n, :],
                                   ALU.mult, ALU.mult).then_inc(sem("xs_done"), 1)
        for u in range(2 * NT):
            t, h = u // 2, u % 2
            t0, n = TILES[t]
            dve.wait_ge(sem("xT_hi"), u + 1)
            v.tensor_tensor(xl[:, 4 * h:4 * h + 4, t0:t0 + n],
                            banks[u][:, :].rearrange("p (k c) -> p k c", c=P)[:, :, 0:n],
                            xh[:, 4 * h:4 * h + 4, t0:t0 + n].bitcast(F32), ALU.subtract).then_inc(sem("xT_lo"), 1)

        dve.wait_ge(sem("const_done"), 6)
        for n, w in enumerate(WINDOWS):
            q = 64 * (n % 2)
            last = v.tensor_scalar(invc[q:q + 64, n // 2, :], invc[q:q + 64, n // 2, :], float(w), None, ALU.min)
        own.step(last)
        own.last()
        own.step(v.reciprocal(invc[:, :, :], invc[:, :, :]))
        dve.wait_ge(sem("prep_mm"), 1)
        dve.wait_ge(sem("const_done"), 6)
        v.tensor_copy(seg(pext, LP, HP)[:, :, :, 0:HP],
                      banks[6][:, 0:240].rearrange("p (c b r) -> p c b r", c=CT, b=NB))
        v.tensor_copy(seg(zext, LS, HS)[:, :, :, 0:HS],
                      banks[6][:, 240:272].rearrange("p (c b r) -> p c b r", c=CT, b=NB))
        v.tensor_copy(prm[:, :, :], banks[6][:, 272:272 + CT * NPRM].rearrange("p (c r) -> p c r", c=CT)).then_inc(sem("prep_done"), 1)
        dve.wait_ge(sem("prep_mm"), 2)
        for h in range(2):
            last = v.tensor_copy(seg(cext, LC, HC)[:, :, 4 * h:4 * h + 4, 0:HC],
                                 banks[7][:, h * 240:(h + 1) * 240].rearrange("p (c b r) -> p c b r", c=CT, b=4))
        last.then_inc(sem("prep_done"), 1)
        dve.wait_ge(sem("prep_mm"), 3)
        v.tensor_copy(wsT[:, :, :], banks[4][:, :].rearrange("p (h t) -> p h t", h=4)).then_inc(sem("prep_done"), 1)

        dve.wait_ge(sem("pj_ev"), 2)
        v.tensor_copy(pext[:, :, HP:LP], proj[:, 0:2, 0:NPR])
        own.step(v.tensor_copy(seg(pext, LP, HP)[:, :, :, HP:], smp(proj[:, 0:2, :])))
        dve.wait_ge(sem("prep_done"), 1)
        own.last()
        own.step(v.tensor_tensor(sum2[:, :, 1:], pext[:, :, 1:], pext[:, :, :-1], ALU.add))
        own.last()
        own.step(v.tensor_tensor(sum4[:, :, 3:], sum2[:, :, 3:], sum2[:, :, 1:-2], ALU.add))
        own.last()
        own.step(v.tensor_tensor(sum8[:, 7:], sum4[:, 1, 7:], sum4[:, 1, 3:-4], ALU.add))
        own.last()
        own.step(v.tensor_tensor(sum16[64:128, 15:], sum8[64:128, 15:], sum8[64:128, 7:-8], ALU.add))
        own.last()
        for n, (w, sums) in enumerate(zip(WINDOWS, (sum2[:, 0, :], sum4[:, 0, :], sum8, sum16))):
            q, ct = slice(64 * (n % 2), 64 * (n % 2) + 64), n // 2
            v.tensor_tensor(vn[q, ct, 0:NPR], sums[q, HP:LP], invc[q, ct, :], ALU.mult)
            last = v.tensor_scalar(smp(vn[q, ct:ct + 1, :])[:, 0], sums[q, LP:].rearrange("p (b s) -> p b s", b=NB)[:, :, HP:],
                                   1.0 / w, None, ALU.mult)
        own.step(last)
        own.last()
        v.tensor_tensor(vn[:, :, :], vn[:, :, :], proj[:, 0:2, :], ALU.subtract).then_inc(sem("pool_ready"), 1)

        dve.wait_ge(sem("glu_gate"), 1)
        dve.wait_ge(sem("prep_done"), 2)
        own.step(v.tensor_tensor(proj[:, 2:4, :], proj[:, 2:4, :], proj[:, 4:6, :], ALU.mult))
        own.last()
        v.tensor_copy(cext[:, :, HC:LC], proj[:, 2:4, 0:NPR])
        own.step(v.tensor_copy(seg(cext, LC, HC)[:, :, :, HC:], smp(proj[:, 2:4, :])))
        own.last()
        conv_parts = [(ct, part) for ct in range(CT) for part in range(2)]

        def tap_view(ext, base, hist, ct, part, k):
            if part == 0:
                return ext[:, ct, bass.ds(k, NPR)]
            return seg(ext, base, hist)[:, ct, :, bass.ds(k, NS)]

        def acc_view(acc, ct, part):
            return acc[:, ct, 0:NPR] if part == 0 else smp(acc[:, :, :])[:, ct]

        conv = sem("conv_step")
        for ct, part in conv_parts:
            v.tensor_scalar(acc_view(cacc, ct, part), tap_view(cext, LC, HC, ct, part, 0),
                            prm[:, ct, PRM["dw"]:PRM["dw"] + 1], prm[:, ct, PRM["dwb"]:PRM["dwb"] + 1],
                            ALU.mult, ALU.add).then_inc(conv, 1)
        with dve.Fori(1, CW) as k:
            for n, (ct, part) in enumerate(conv_parts):
                dve.wait_ge(conv, k * 4 + (n - 3))
                acc = acc_view(cacc, ct, part)
                v.scalar_tensor_tensor(acc, tap_view(cext, LC, HC, ct, part, k), prm[:, ct, bass.ds(k, 1)], acc,
                                       ALU.mult, ALU.add).then_inc(conv, 1)

        def br_low(n, val):
            dve.wait_ge(sem("br_hi"), n + 1)
            v.tensor_tensor(brl[:, n * CT:(n + 1) * CT, :], val, brh[:, n * CT:(n + 1) * CT, :].bitcast(F32),
                            ALU.subtract).then_inc(sem("br_ready"), 1)

        dve.wait_ge(sem("br_hi"), 1)
        for ct in range(CT):
            last = v.scalar_tensor_tensor(brl[:, ct, :], banks[6 + ct][:, 0:T], prm[:, ct, PRM["ps"]:PRM["ps"] + 1],
                                          brh[:, ct, :].bitcast(F32), ALU.mult, ALU.subtract)
        last.then_inc(sem("br_ready"), 1)

        def merge(i, j):
            g = i * 8 + j
            dve.wait_ge(sem("gate_sg"), g + 1)
            dve.wait_ge(sem("br_mm"), g + 1)
            if not (isinstance(i, int) and g < 2):
                dve.wait_ge(sem("mg_add"), g - 1)
            v.tensor_tensor(prod[j % 2][:, :], sig[j % 2][:, :], banks[4 + j % 2][:, 0:T], ALU.mult).then_inc(sem("gp_done"), 1)
            dve.wait_ge(sem("gp_done"), g + 1)
            if isinstance(i, int) and g == 0:
                dve.wait_ge(sem("merged_zero"), 1)
            v.tensor_tensor(merged[:, j, :], merged[:, j, :], prod[j % 2][:, :], ALU.add).then_inc(sem("mg_add"), 1)

        def center(src, dst):
            mean = banks[6][:, 0:T].unsqueeze(1).to_broadcast([P, CT, T])
            v.tensor_tensor(dst, src, mean, ALU.subtract).then_inc(sem("ln_cent"), 1)

        def normalise(n, x, g, b, done):
            dve.wait_ge(sem("ln_root"), n)
            dve.wait_ge(sem("ln_sq"), n)
            own.step(v.reciprocal(lnr[:, :], lnr[:, :]))
            own.last()
            own.step(v.tensor_tensor(x, x, lnr[:, :].unsqueeze(1).to_broadcast([P, CT, T]), ALU.mult))
            own.last()
            for ct in range(CT):
                last = v.tensor_scalar(x[:, ct, :], x[:, ct, :], prm[:, ct, PRM[g]:PRM[g] + 1],
                                       prm[:, ct, PRM[b]:PRM[b] + 1], ALU.mult, ALU.add)
            last.then_inc(sem(done), 1)

        dve.wait_ge(sem("ln_mm"), 1)
        dve.wait_ge(sem("map_mm"), 1)
        center(proj[:, 14:16, :], vn[:, :, :])
        merge(0, 0)
        merge(0, 1)
        normalise(1, vn[:, :, :], "vg", "vb", "v_norm")
        merge(0, 2)
        dve.wait_ge(sem("ln_mm"), 3)
        center(cacc[:, :, :], cacc[:, :, :])
        merge(0, 3)
        dve.wait_ge(sem("pj_ev"), 12)
        v.tensor_tensor(proj[:, 8:10, :], proj[:, 8:10, :], proj[:, 10:12, :], ALU.mult).then_inc(sem("z_done"), 1)
        dve.wait_ge(sem("z_done"), 1)
        v.tensor_copy(zext[:, :, HS:LS], proj[:, 8:10, 0:NPR])
        own.step(v.tensor_copy(seg(zext, LS, HS)[:, :, :, HS:], smp(proj[:, 8:10, :])))
        normalise(2, cacc[:, :, :], "lng", "lnb", "b_norm")
        merge(0, 4)
        dve.wait_ge(sem("vT_mm"), 1)
        v.tensor_copy(v_tok[:, 0:2, :], banks[6][:, :].rearrange("p (t c) -> p t c", t=2)).then_inc(sem("v_tok_done"), 1)
        v.tensor_copy(v_tok[0:NSM, 2, :], banks[7][0:NSM, 0:BW]).then_inc(sem("v_tok_done"), 1)
        merge(0, 5)
        dve.wait_ge(sem("silu_gate"), 1)
        dve.wait_ge(sem("b_norm"), 1)
        v.tensor_tensor(cacc[:, :, :], cacc[:, :, :], sqb[:, :, :], ALU.mult).then_inc(sem("br_val"), 1)
        dve.wait_ge(sem("br_val"), 1)
        br_low(1, cacc[:, :, :])
        zc = Steps(dve, "sconv_step")
        for k in range(SW):
            for n, (ct, part) in enumerate(conv_parts):
                acc, row = acc_view(vn, ct, part), tap_view(zext, LS, HS, ct, part, k)
                w = prm[:, ct, PRM["sw"] + k:PRM["sw"] + k + 1]
                if k == 0:
                    zc.step(v.tensor_scalar(acc, row, w, None, ALU.mult))
                else:
                    dve.wait_ge(sem("sconv_step"), 4 * k + n - 3)
                    zc.step(v.scalar_tensor_tensor(acc, row, w, acc, ALU.mult, ALU.add))
        zc.last()
        merge(0, 6)
        v.tensor_tensor(vn[:, :, :], vn[:, :, :], proj[:, 6:8, :], ALU.mult).then_inc(sem("br_val"), 1)
        dve.wait_ge(sem("mix_mm"), 1)
        for ct in range(CT):
            v.tensor_tensor(proj[:, 14 + ct, 0:NPR].rearrange("p (n t) -> p n t", n=2),
                            banks[6 + ct][:, 0:NPR].rearrange("p (n t) -> p n t", n=2),
                            bS[:, ct, :].unsqueeze(1).to_broadcast([P, 2, P]), ALU.add)
            v.tensor_tensor(proj[:, 14 + ct, NPR:T].rearrange("p (b s) -> p b s", b=NB),
                            banks[6 + ct][:, NPR:T].rearrange("p (b s) -> p b s", b=NB),
                            bS[:, ct, 0:NS].unsqueeze(1).to_broadcast([P, NB, NS]), ALU.add).then_inc(sem("mix_read"), 1)
        dve.wait_ge(sem("mix_read"), 2)
        v.tensor_tensor(proj[:, 12:14, :], proj[:, 12:14, :], proj[:, 14:16, :], ALU.mult).then_inc(sem("br_val"), 1)
        merge(0, 7)
        br_low(2, vn[:, :, :])
        dve.wait_ge(sem("br_val"), 3)
        br_low(3, proj[:, 12:14, :])
        dve.wait_ge(sem("tail_mm"), 1)
        v.tensor_copy(tail_sb[:, 0:2, :], banks[6][0:TAIL, :].rearrange("p (x c) -> p x c", x=2)).then_inc(sem("tail_done"), 1)
        v.tensor_copy(tail_sb[:, 2, :], banks[7][0:TAIL, 0:BW]).then_inc(sem("tail_done"), 1)
        with dve.Fori(1, NBR) as i:
            for j in range(8):
                merge(i, j)
        for n in range(4):
            dve.wait_ge(sem("mg_hi"), n + 1)
            v.tensor_tensor(brl[:, 2 * n:2 * n + 2, :], merged[:, 2 * n:2 * n + 2, :],
                            brh[:, 2 * n:2 * n + 2, :].bitcast(F32), ALU.subtract).then_inc(sem("mg_lo"), 1)
        for c in range(N_OUT):
            for t, (_, n) in enumerate(TILES):
                dve.wait_ge(sem("wo_mm"), NT * c + t + 1)
                xc = x_tok[0:n, t, c * CH:(c + 1) * CH]
                v.tensor_tensor(xc, xc, banks[3 * (c % 2) + t][0:n, 0:CH], ALU.add).then_inc(sem("wo_add"), 1)

        mean_square("n2_sq", NT, "n2_ms")
        dve.wait_ge(sem("n2_root"), 1)
        own.step(v.reciprocal(rstd[:, :], root[:, :]))
        own.last()
        dve.wait_ge(sem("small2_in"), 16 * N_SMALL2)
        dve.wait_ge(sem("out_dma"), 16 * 7)
        dve.wait_ge(sem("tail_out"), 16)
        for t, (_, n) in enumerate(TILES):
            v.scalar_tensor_tensor(xn2[0:n, t, :], x_tok[0:n, t, :], rstd[0:n, t:t + 1], g2b[0:n, :],
                                   ALU.mult, ALU.mult).then_inc(sem("n2_done"), 1)
        for t, (t0, n) in enumerate(TILES):
            dve.wait_ge(sem("n2T_mm"), 2 * t + 2)
            v.tensor_copy(xn2T[:, 4:8, t0:t0 + n],
                          banks[2 * t + 1][:, :].rearrange("p (k c) -> p k c", c=P)[:, :, 0:n]).then_inc(sem("n2T_dve"), 1)

        def op(ins):
            own.step(ins)
            own.last()

        def wide(x, n):
            return x.unsqueeze(2).to_broadcast([P, NT, n])

        dve.wait_ge(sem("lg_mm"), 1)
        dve.wait_ge(sem("moe_const"), 1)
        logits = banks[6][:, 0:NT * 64].rearrange("p (t c) -> p t c", t=NT)[:, :, 0:NG + NE]
        v.tensor_tensor(lgt[:, 0:2, :], logits[:, 0:2, :], rb[:, :].unsqueeze(1).to_broadcast([P, 2, NG + NE]), ALU.add)
        op(v.tensor_tensor(lgt[0:NSM, 2, :], logits[0:NSM, 2, :], rb[0:NSM, :], ALU.add))
        op(v.tensor_reduce(gmax[:, :], lgt[:, :, 0:NG], axis=AX_X, op=ALU.max))
        v.tensor_tensor(gsh[:, :, :], lgt[:, :, 0:NG], wide(gmax[:, :], NG), ALU.subtract).then_inc(sem("gsh_done"), 1)
        dve.wait_ge(sem("gsh_done"), 1)
        op(v.scalar_tensor_tensor(geq[:, :, :], gsh[:, :, :], 0.0, iog[:, :, :], ALU.is_equal, ALU.mult))
        op(v.tensor_reduce(gidx[:, :], geq[:, :, :], axis=AX_X, op=ALU.min))
        op(v.tensor_tensor(geq[:, :, :], iog[:, :, :], wide(gidx[:, :], NG), ALU.is_equal))
        op(v.tensor_scalar(geq[:, :, :], geq[:, :, :], 1.0, 1.0e30, ALU.subtract, ALU.mult))
        for t in range(NT):
            last = v.tensor_tensor(lem[:, t, :].rearrange("p (g e) -> p g e", g=NG),
                                   lgt[:, t, NG:NG + NE].rearrange("p (g e) -> p g e", g=NG),
                                   geq[:, t, :].unsqueeze(2).to_broadcast([P, NG, EG]), ALU.add)
        op(last)
        for w in range(2):
            op(v.tensor_reduce(topv[w][:, :], lem[:, :, :], axis=AX_X, op=ALU.max))
            op(v.tensor_tensor(eqm[:, :, :], lem[:, :, :], wide(topv[w][:, :], NE), ALU.is_equal))
            op(v.tensor_tensor(eqm[:, :, :], eqm[:, :, :], ioe[:, :, :], ALU.mult))
            op(v.tensor_reduce(tidx[:, :], eqm[:, :, :], axis=AX_X, op=ALU.min))
            op(v.tensor_tensor(oh[w][:, :, :], ioe[:, :, :], wide(tidx[:, :], NE), ALU.is_equal))
            if w == 0:
                op(v.scalar_tensor_tensor(lem[:, :, :], oh[0][:, :, :], -1.0e38, lem[:, :, :], ALU.mult, ALU.add))
        v.memset(oh[0][64:128, 2, :], 0.0)
        op(v.memset(oh[1][64:128, 2, :], 0.0))
        v.tensor_tensor(both[:, :, :], oh[0][:, :, :], oh[1][:, :, :], ALU.add).then_inc(sem("both_done"), 1)
        v.tensor_tensor(tidx[:, :], topv[1][:, :], topv[0][:, :], ALU.subtract).then_inc(sem("tdiff_done"), 1)
        dve.wait_ge(sem("rt_exp"), 2)
        op(v.tensor_reduce(psel[:, :], gex[:, :, :], axis=AX_X, op=ALU.add))
        v.reciprocal(psel[:, :], psel[:, :])
        op(v.tensor_scalar(tw[0][:, :], ex[:, :], 1.0, None, ALU.add))
        op(v.reciprocal(tw[0][:, :], tw[0][:, :]))
        op(v.tensor_tensor(tw[0][:, :], tw[0][:, :], psel[:, :], ALU.mult))
        op(v.tensor_tensor(tw[1][:, :], tw[0][:, :], ex[:, :], ALU.mult))
        op(v.tensor_tensor(cwt[:, :, :], oh[0][:, :, :], wide(tw[0][:, :], NE), ALU.mult))
        op(v.tensor_tensor(rtmp[:, :, :], oh[1][:, :, :], wide(tw[1][:, :], NE), ALU.mult))
        v.tensor_tensor(cwt[:, :, :], cwt[:, :, :], rtmp[:, :, :], ALU.add).then_inc(sem("cwt_done"), 1)
        dve.wait_ge(sem("cum_mm"), 1)
        cum = banks[7][:, 0:NT * NE].rearrange("p (t e) -> p t e", t=NT)
        op(v.scalar_tensor_tensor(pos[:, :, :], cum, 1.0, both[:, :, :], ALU.add, ALU.mult))
        op(v.tensor_scalar(pos[:, :, :], pos[:, :, :], 1.0, None, ALU.subtract))

        def one_hot(out, i, done):
            v.tensor_tensor(out[:, :, :, :], pos[:, :, bass.ds(i * QE, QE)].unsqueeze(3).to_broadcast([P, NT, QE, CAP]),
                            slot_no[:, :].unsqueeze(1).unsqueeze(1).to_broadcast([P, NT, QE, CAP]),
                            ALU.is_equal).then_inc(sem(done), 1)

        one_hot(onehot, 0, "g_built")
        op(v.tensor_scalar(over[:, :, :], pos[:, :, :], float(CAP), None, ALU.is_ge))
        v.tensor_reduce(ovs[:, :], over[:, :, :].rearrange("p t e -> p (t e)"), axis=AX_X, op=ALU.add).then_inc(sem("ovs_done"), 1)
        dve.wait_ge(sem("cwt_done"), 1)
        op(v.tensor_tensor(cwo[:, :, :], cwt[:, :, :], over[:, :, :], ALU.mult))
        dve.wait_ge(sem("ovs_mm"), 1)
        v.tensor_copy(flag_i[0:1, :], banks[7][0:1, 256:257]).then_inc(sem("flag_ready"), 1)

        def weights_out(i):
            dve.wait_ge(sem("cw_mm"), i + 1)
            w2 = psT[:, 256:260].rearrange("p (m e) -> p m e", m=2)
            v.tensor_copy(slot_w[0:64, :], w2[0:64, :, 0])
            v.tensor_copy(slot_w[64:128, :], w2[64:128, :, 1]).then_inc(sem("cw_ev"), 1)

        def hidden(p, s):
            dve.wait_ge(sem("sg_done"), p + 1)
            if not (isinstance(p, int) and p < 2):
                dve.wait_ge(sem("ht_mm"), p - 1)
            v.scalar_tensor_tensor(hh[s][:, :], sg[s][:, :], slot_w[:, s:s + 1],
                                   psG[s][:, F:2 * F], ALU.mult, ALU.mult).then_inc(sem("h_done"), 1)

        def hidden_T(p, s):
            dve.wait_ge(sem("ht_mm"), p + 1)
            v.tensor_copy(hhT[s][:, :, :], psT[:, 0:FK * P].rearrange("p (k c) -> p k c", k=FK)).then_inc(sem("hte_done"), 1)

        def y_low(p, s):
            for half in range(2):
                dve.wait_ge(sem("yh_done"), p * 2 + (half + 1))
                cols = slice(half * 512, (half + 1) * 512)
                v.tensor_tensor(yl[:, s, cols], psY[half][:, :], yh[:, s, cols].bitcast(F32),
                                ALU.subtract).then_inc(sem("yl_done"), 1)

        def add_back(i, u):
            t, half = BACK[u]
            n = TILES[t][1]
            dve.wait_ge(sem("sc_mm"), i * 6 + (u + 1))
            xc = x_tok[0:n, t, half * 512:(half + 1) * 512]
            v.tensor_tensor(xc, xc, ring[BACK_BANK[u]][0:n, :], ALU.add).then_inc(sem("sc_add"), 1)

        def quad(i):
            first, end = isinstance(i, int) and i == 0, isinstance(i, int) and i == QUADS - 1
            if not first:
                hidden_T(i * 2 - 1, 1)
                dve.wait_ge(sem("st_mm"), i * 2)
            one_hot(onehot_s, i, "gs_built")
            if not end:
                dve.wait_ge(sem("cw_mm"), i + 1)
                one_hot(onehot, i + 1, "g_built")
            dve.wait_ge(sem("cw_ev"), i + 1)
            hidden(i * 2, 0)
            if not first:
                y_low(i * 2 - 1, 1)
            hidden(i * 2 + 1, 1)
            hidden_T(i * 2, 0)
            if not end:
                dve.wait_ge(sem("h_done"), i * 2 + 2)
                weights_out(i + 1)
            if not first:
                for u in range(6):
                    add_back(i - 1, u)
            y_low(i * 2, 0)

        weights_out(0)
        quad(0)
        with dve.Fori(1, QUADS - 1) as i:
            quad(i)
        quad(QUADS - 1)
        hidden_T(PAIRS - 1, 1)
        y_low(PAIRS - 1, 1)

        dve.wait_ge(sem("flag_ready"), 1)
        flag = dve.value_load(flag_i[0:1, 0:1], min_val=0, max_val=2 * T)
        with dve.If(flag > 0):
            v.memset(ovs[:, :], 0.0).then_inc(sem("ov_free"), 1)
            v.memset(ov_cw[:, :], 0.0).then_inc(sem("ov_acc"), 1)
            with dve.Fori(0, NE) as e:
                dve.wait_ge(sem("ov_acc"), e * NT + 1)
                v.tensor_copy(ov_cw[:, :], cwo[:, :, e]).then_inc(sem("ov_cw"), 1)
                dve.wait_ge(sem("ov_cw"), e + 1)
                for t, (_, n) in enumerate(TILES):
                    dve.wait_ge(sem("ov_sg"), e * NT + (t + 1))
                    v.scalar_tensor_tensor(hh[0][0:n, :], sg[0][0:n, :], ov_cw[0:n, t:t + 1],
                                           psG[0][0:n, F:2 * F], ALU.mult, ALU.mult).then_inc(sem("ov_h"), 1)
                    dve.wait_ge(sem("ov_ht"), e * NT + (t + 1))
                    v.tensor_copy(hhT[0][:, :, 0:n],
                                  psT[:, 0:FK * P].rearrange("p (k c) -> p k c", k=FK)[:, :, 0:n]).then_inc(sem("ov_hte"), 1)
                    dve.wait_ge(sem("ov_dn"), e * NT + (t + 1))
                    v.tensor_tensor(x_tok[0:n, t, 0:512], x_tok[0:n, t, 0:512], psY[0][0:n, :], ALU.add)
                    v.tensor_tensor(x_tok[0:n, t, 512:D], x_tok[0:n, t, 512:D], psY[1][0:n, :], ALU.add).then_inc(sem("ov_acc"), 1)
                v.memset(ovs[:, :], 0.0).then_inc(sem("ov_free"), 1)

        for u in range(6):
            add_back(QUADS - 1, u)
        for t, (_, n) in enumerate(TILES):
            dve.wait_ge(sem("f_sq"), t + 1)
            v.tensor_scalar(ms[:, t:t + 1], ss[:, t:t + 1], 1.0 / D, RMS_EPS, ALU.mult, ALU.add).then_inc(sem("f_ms"), 1)
            dve.wait_ge(sem("f_root"), t + 1)
            op(v.reciprocal(rstd[:, t:t + 1], root[:, t:t + 1]))
            v.scalar_tensor_tensor(x_tok[0:n, t, :], x_tok[0:n, t, :], rstd[0:n, t:t + 1], gfb[0:n, :],
                                   ALU.mult, ALU.mult).then_inc(sem("y_done"), 1)

    ctx.close()


_INS = ['x_prompt', 'x_sample', 'state_pool', 'state_conv', 'state_sconv', 'norm1_g', 'w_in', 'pool_w', 'pool_scale',
        'conf_dw', 'conf_dw_b', 'conf_ln_g', 'conf_ln_b', 'sconv_w', 'sgu_ln_g', 'sgu_ln_b', 'sgu_ws', 'sgu_b',
        'w_branch', 'w_out', 'norm2_g', 'router_g', 'router_g_b', 'router_e', 'router_e_b', 'w_gate', 'w_up',
        'w_down', 'final_g']
_OUTS = [('y_prompt', (1, 256, 1024)), ('y_sample', (8, 8, 1024)), ('pool_p', (1, 1, 15, 256)),
         ('conv_p', (1, 1, 30, 256)), ('sconv_p', (1, 1, 2, 256)), ('sguv_p', (1, 1, 128, 256)),
         ('pool_s', (1, 8, 15, 256)), ('conv_s', (1, 8, 30, 256)), ('sconv_s', (1, 8, 2, 256)),
         ('sguv_s', (1, 8, 8, 256))]


def kernel(**inputs):
    import numpy as _np
    import concourse.bacc as _bacc
    from concourse import mybir as _mybir
    from concourse.bass_utils import run_bass_kernel_spmd as _run

    nc = _bacc.Bacc("TRN2", target_bir_lowering=False, num_devices=1)
    arrays, ins, outs = {}, {}, {}
    for name in _INS:
        x = _np.ascontiguousarray(inputs[name])
        arrays["in_" + name] = x
        ins[name] = nc.dram_tensor("in_" + name, x.shape, _mybir.dt.from_np(x.dtype), kind="ExternalInput").ap()
    for name, shape in _OUTS:
        outs[name] = nc.dram_tensor("out_" + name, shape, _mybir.dt.float32, kind="ExternalOutput").ap()
    build(nc, ins, outs)
    r = _run(nc, [arrays], core_ids=[0])
    return tuple(r.results[0]["out_" + name] for name, _ in _OUTS)
```

```python
from contextlib import ExitStack

import concourse.bass as bass
from concourse import mybir

F32 = mybir.dt.float32
F32R = mybir.dt.float32r
I32 = mybir.dt.int32
ALU = mybir.AluOpType
ACT = mybir.ActivationFunctionType
AX_X = mybir.AxisListType.X

P = 128
D = 1024
KT = D // P
NPR, NB, NS = 256, 8, 8
NSM = NB * NS
T = NPR + NSM
TILES = ((0, 128), (128, 128), (256, 64))
NT = len(TILES)
BW = 256
CT = BW // P
NBR = 4
HP, HC, HS = 15, 30, 2
CW, SW = 31, 3
WINDOWS = (2, 4, 8, 16)
NG, EG = 4, 8
NE = NG * EG
PAIRS = NE // 2
QE = 4
QUADS = NE // QE
F = 256
FK = F // P
CAP = 64
QS = QE * CAP
CH = 256
N_PROJ = 2048 // CH
N_GATE = NBR * D // CH
N_OUT = D // CH
KH = KT // 2
ORDER = (0, 2, 3, 1)
TAPS_EARLY = 17
TAIL = 96
RMS_EPS, LN_EPS = 1e-6, 1e-5
LP = HP + NPR
LC = HC + NPR
LS = HS + NPR
EP, EC, ES = LP + NB * (HP + NS), LC + NB * (HC + NS), LS + NB * (HS + NS)
PRM = dict(dw=0, dwb=31, lng=32, lnb=33, sw=34, vg=37, vb=38, ps=39)
NPRM = 40


def build(nc, a, o):
    ctx = ExitStack()
    sems = {}

    def sb(name, shape, dt=F32, stack=ctx):
        return stack.enter_context(nc.sbuf_tensor(name, shape, dt))

    def sem(name):
        if name not in sems:
            sems[name] = ctx.enter_context(nc.semaphore(name))
        return sems[name]

    class Steps:

        def __init__(self, eng, name):
            self.eng, self.sem, self.n = eng, sem(name), 0

        def step(self, ins):
            self.n += 1
            ins.then_inc(self.sem, 1)

        def last(self):
            self.eng.wait_ge(self.sem, self.n)

    tail_dram = nc.dram_tensor("state_tail_rows", (3, NSM, BW), F32).ap()

    x_tok = sb("x_tok", [P, NT, D])
    ident = sb("ident", [P, P])
    mean_w = sb("mean_w", [P, P])
    before_r = sb("before_r", [P, P], F32R)
    ones_r = sb("ones_r", [P, P], F32R)
    gfb = sb("gfb", [P, D])
    rg = sb("rg", [P, KT, NG])
    re = sb("re", [P, KT, NE])
    rw = sb("rw", [P, KT, NG + NE])
    rb = sb("rb", [P, NG + NE])
    ss = sb("ss", [P, NT])
    ssc = sb("ssc", [P, NT, N_OUT])
    ms = sb("ms", [P, NT])
    root = sb("root", [P, NT])
    rstd = sb("rstd", [P, NT])
    epsb = sb("epsb", [P, 1])
    unread = sb("unread", [P, 4])
    banks = [ctx.enter_context(nc.psum_tensor(f"bank{i}", [P, 512], F32)) for i in range(8)]

    mixer = ExitStack()

    def pa(name, shape, dt=F32):
        return sb(name, shape, dt, mixer)

    xh = pa("xh", [P, KT, T], F32R)
    xl = pa("xl", [P, KT, T], F32R)
    proj = pa("proj", [P, 16, T])
    merged = pa("merged", [P, KT, T])
    before = pa("before", [P, P])
    ones = pa("ones", [P, P])
    g1b = pa("g1b", [P, D])
    prm_rows = pa("prm_rows", [NPRM, BW])
    pool_rows = pa("pool_rows", [NB * HP, BW])
    conv_rows = pa("conv_rows", [NB * HC // 2, 2, BW])
    sconv_rows = pa("sconv_rows", [NB * HS, BW])
    ws_rows = pa("ws_rows", [P, 4, P])
    invc = pa("invc", [P, CT, NPR])
    pext = pa("pext", [P, CT, EP])
    prm = pa("prm", [P, CT, NPRM])
    wsT = pa("wsT", [P, 4, P])
    wsS = pa("wsS", [NSM, 4, NSM])
    bS = pa("bS", [P, CT, P])
    pw = pa("pw", [P, CT, P])
    cext = pa("cext", [P, CT, EC])
    zext = pa("zext", [P, CT, ES])
    cacc = pa("cacc", [P, CT, T])
    vn = pa("vn", [P, CT, T])
    sqb = pa("sqb", [P, CT, T])
    lnr = pa("lnr", [P, T])
    v_tok = pa("v_tok", [P, NT, BW])
    tail_sb = pa("tail_sb", [TAIL, 3, BW])
    sig = [pa(f"sig{q}", [P, T]) for q in range(2)]
    prod = [pa(f"prod{q}", [P, T]) for q in range(2)]
    brh = pa("brh", [P, NBR * CT, T], F32R)
    brl = pa("brl", [P, NBR * CT, T], F32R)
    raw = [pa(f"raw{q}", [P, KT + CT, CH]) for q in range(2)]
    wh = [pa(f"wh{q}", [P, KT + CT, CH], F32R) for q in range(2)]
    wl = [pa(f"wl{q}", [P, KT + CT, CH], F32R) for q in range(2)]
    g2b = pa("g2b", [P, D])
    sq_out = pa("sq_out", [P, CH])
    proj_flat = proj[:, :, :].rearrange("p k t -> p (k t)")
    xs = proj_flat[:, 0:NT * D].rearrange("p (t d) -> p t d", t=NT)
    junk = proj_flat[:, 4 * D:5 * D]
    merged_flat = merged[:, :, :].rearrange("p k t -> p (k t)")
    sum2 = merged_flat[:, 0:CT * EP].rearrange("p (c e) -> p c e", c=CT)
    sum4 = merged_flat[:, CT * EP:2 * CT * EP].rearrange("p (c e) -> p c e", c=CT)
    sum8 = merged_flat[:, 2 * CT * EP:2 * CT * EP + EP]
    sum16 = sum2[:, 1, :]
    mixer.close()

    moe = ExitStack()

    def pb(name, shape, dt=F32):
        return sb(name, shape, dt, moe)

    with nc.sbuf_tensor("xn2", [P, NT, D], F32) as xn2:
        pass
    yh = pb("yh", [P, 2, D], F32R)
    yl = pb("yl", [P, 2, D], F32R)
    xn2T = pb("xn2T", [P, KT, T])
    xnh = pb("xnh", [P, NT, D], F32R)
    xnl = pb("xnl", [P, 2, D], F32R)
    lgt = pb("lgt", [P, NT, NG + NE])
    iog = pb("iog", [P, NT, NG])
    ioe = pb("ioe", [P, NT, NE])
    gsh = pb("gsh", [P, NT, NG])
    geq = pb("geq", [P, NT, NG])
    gex = pb("gex", [P, NT, NG])
    gmax = pb("gmax", [P, NT])
    gidx = pb("gidx", [P, NT])
    psel = pb("psel", [P, NT])
    lem = pb("lem", [P, NT, NE])
    eqm = pb("eqm", [P, NT, NE])
    oh = [pb(f"oh{w}", [P, NT, NE]) for w in range(2)]
    topv = [pb(f"topv{w}", [P, NT]) for w in range(2)]
    tidx = pb("tidx", [P, NT])
    tw = [pb(f"tw{w}", [P, NT]) for w in range(2)]
    both = pb("both", [P, NT, NE], F32R)
    pos = pb("pos", [P, NT, NE])
    over = pb("over", [P, NT, NE])
    cwt = pb("cwt", [P, NT, NE])
    cwr = pb("cwr", [P, NT, 2, NE], F32R)
    cwo = pb("cwo", [P, NT, NE])
    rtmp = pb("rtmp", [P, NT, NE])
    slot_no = pb("slot_no", [P, CAP])
    ovs = pb("ovs", [P, 1])
    flag_i = pb("flag_i", [P, 1], I32)
    ov_cw = pb("ov_cw", [P, NT])
    ex = pb("ex", [P, NT])
    wgu = [[pb(f"wgu0{j}", [P, 2, KT, F]) for j in range(2)]]
    onehot = pb("onehot", [P, NT, QE, CAP], F32R)
    onehot_s = pb("onehot_s", [P, NT, QE, CAP], F32R)
    slot_tok = pb("slot_tok", [P, 2, T], F32R)
    slot_w = pb("slot_w", [P, 2])
    sg = [pb(f"sg{s}", [P, F]) for s in range(2)]
    hh = [pb(f"hh{s}", [P, F]) for s in range(2)]
    hhT = [pb(f"hhT{s}", [P, FK, P]) for s in range(2)]
    xgT = pb("xgT", [P, KT, QS])
    wgu.append([pb(f"wgu1{j}", [P, 2, KT, F]) for j in range(2)])
    wd = [[pb(f"wd{s}{j}", [P, FK, D]) for j in range(2)] for s in range(2)]
    wd2 = [pb(f"wd2{j}", [P, FK, D]) for j in range(2)]
    junk2 = xgT[:, :, :].rearrange("p k t -> p (k t)")[:, 0:D]
    moe.close()

    w_in3 = a["w_in"][0].rearrange("(k p) n -> p k n", p=P)
    w_out3 = a["w_out"][0].rearrange("(k p) n -> p k n", p=P)
    w_br3 = a["w_branch"][0].rearrange("b (k p) n -> p (b k) n", p=P)
    x_rows = [a["x_prompt"][0, 0:128, :], a["x_prompt"][0, 128:256, :],
              a["x_sample"].rearrange("b s d -> (b s) d")]
    y_rows = [o["y_prompt"][0, 0:128, :], o["y_prompt"][0, 128:256, :],
              o["y_sample"].rearrange("b s d -> (b s) d")]
    w_gate4 = a["w_gate"][0].rearrange("e (p k) f -> e p k f", k=KT)
    w_up4 = a["w_up"][0].rearrange("e (p k) f -> e p k f", k=KT)
    w_down4 = a["w_down"][0].rearrange("e (p k) d -> e p k d", k=FK)

    def seg(ext, base, hist):
        return ext[:, :, base:base + NB * (hist + NS)].rearrange("p c (b s) -> p c b s", b=NB)

    def smp(ap):
        return ap[:, :, NPR:T].rearrange("p c (b s) -> p c b s", b=NB)

    N_SMALL = 8 + 3 + 1 + 4
    N_SMALL2 = 6
    raw_in = [sem("raw_in0"), sem("raw_in1")]
    wbr_in = [sem("wbr_in0"), sem("wbr_in1")]
    x_in = [sem(f"x_in{t}") for t in range(NT)]
    FIRST_OUT = N_PROJ + N_GATE

    ring = banks[0:3]
    psG = banks[3:5]
    psT = banks[5]
    psY = banks[6:8]
    BACK = [(t, half) for half in range(2) for t in range(NT)]
    IN_BANK = (0, 1, 2, 0)
    BACK_BANK = (1, 2, 0, 1, 2, 0)
    TURN_BANK = (1, 2)

    NORM_BANK = (banks[0], banks[1], banks[2], banks[6], banks[0], banks[1])

    block = ctx.enter_context(nc.Block())

    @block.sync
    def _(sp):
        for t, (_, n) in enumerate(TILES):
            sp.dma_start(x_tok[0:n, t, :], x_rows[t]).then_inc(x_in[t], 16)
            if t == 1:
                sp.dma_start(g1b[:, :], a["norm1_g"][0:1, :].to_broadcast([P, D])).then_inc(sem("g1_in"), 16)

        def load_plain(c):
            src, n0 = (w_in3, c * CH) if c < N_PROJ else (w_out3, (c - FIRST_OUT) * CH)
            if c == 0:
                sp.dma_start(raw[0][:, 0:KH, :], src[:, 0:KH, n0:n0 + CH]).then_inc(sem("raw_first"), 16)
                sp.dma_start(raw[0][:, KH:KT, :], src[:, KH:KT, n0:n0 + CH]).then_inc(raw_in[0], 16)
            else:
                sp.dma_start(raw[c % 2][:, 0:KT, :], src[:, :, n0:n0 + CH]).then_inc(raw_in[c % 2], 16)

        load_plain(0)
        load_plain(1)
        small = sem("small_in")
        sp.dma_start(prm_rows[0:31, :], a["conf_dw"][0]).then_inc(small, 16)
        sp.dma_start(prm_rows[31:32, :], a["conf_dw_b"]).then_inc(small, 16)
        sp.dma_start(prm_rows[32:33, :], a["conf_ln_g"]).then_inc(small, 16)
        sp.dma_start(prm_rows[33:34, :], a["conf_ln_b"]).then_inc(small, 16)
        sp.dma_start(prm_rows[34:37, :], a["sconv_w"][0]).then_inc(small, 16)
        sp.dma_start(prm_rows[37:38, :], a["sgu_ln_g"]).then_inc(small, 16)
        sp.dma_start(prm_rows[38:39, :], a["sgu_ln_b"]).then_inc(small, 16)
        sp.dma_start(prm_rows[39:40, :], a["pool_scale"]).then_inc(small, 16)
        sp.dma_start(pool_rows[:, :], a["state_pool"][0].rearrange("b r c -> (b r) c")).then_inc(small, 16)
        sp.dma_start(conv_rows[:, :, :],
                     a["state_conv"][0].rearrange("(h b) r c -> (b r) h c", h=2)).then_inc(small, 16)
        sp.dma_start(sconv_rows[:, :], a["state_sconv"][0].rearrange("b r c -> (b r) c")).then_inc(small, 16)
        sp.dma_start(ws_rows[:, :, :], a["sgu_ws"][0].rearrange("h t s -> t h s")).then_inc(small, 16)
        for h in range(4):
            q = 64 * (h % 2)
            sp.dma_start(bS[q:q + 64, h // 2, :],
                         a["sgu_b"][0, h:h + 1, :].to_broadcast([64, P])).then_inc(small, 16)
        sp.wait_ge(sem("const_done"), 3)
        for g in range(4):
            q = 64 * (g % 2)
            sp.dma_start(pw[q:q + 64, g // 2, q:q + 64], a["pool_w"][0, g]).then_inc(sem("pw_in"), 16)

        for c in range(2, N_PROJ):
            sp.wait_ge(sem("lo_done"), 2 * (c - 1))
            load_plain(c)
            if c == 3:
                s2 = sem("small2_in")
                sp.dma_start(g2b[:, :], a["norm2_g"][0:1, :].to_broadcast([P, D])).then_inc(s2, 16)
                sp.dma_start(gfb[:, :], a["final_g"].rearrange("(u d) -> u d", u=1).to_broadcast([P, D])).then_inc(s2, 16)
                sp.dma_start(rg[:, :, :], a["router_g"][0].rearrange("(p k) g -> p k g", k=KT)).then_inc(s2, 16)
                sp.dma_start(re[:, :, :], a["router_e"][0].rearrange("(p k) g -> p k g", k=KT)).then_inc(s2, 16)
                sp.dma_start(rb[:, 0:NG], a["router_g_b"][0:1, :].to_broadcast([P, NG])).then_inc(s2, 16)
                sp.dma_start(rb[:, NG:NG + NE], a["router_e_b"][0:1, :].to_broadcast([P, NE])).then_inc(s2, 16)
                sp.dma_start(o["pool_s"][0, :, 0:HP - NS, :],
                             a["state_pool"][0, :, NS:HP, :]).then_inc(sem("out_dma"), 16)
                sp.dma_start(o["conv_s"][0, :, 0:HC - NS, :],
                             a["state_conv"][0, :, NS:HC, :]).then_inc(sem("out_dma"), 16)
        def load_branch(i, branch):
            for m in range(4):
                q = m % 2
                sp.wait_ge(sem("lo_done"), i * 8 + 2 * (N_PROJ + m - 1))
                sp.dma_start(raw[q][:, 0:KT, :],
                             w_in3[:, :, bass.ds(branch * D + (N_PROJ + m) * CH, CH)]).then_inc(raw_in[q], 16)
                sp.dma_start(raw[q][:, KT:KT + CT, :],
                             w_br3[:, bass.ds(branch * CT, CT), m * CH:(m + 1) * CH]).then_inc(wbr_in[q], 16)

        load_branch(0, ORDER[0])
        with sp.Fori(1, NBR - 1) as i:
            load_branch(i, i + 1)
        load_branch(NBR - 1, ORDER[3])
        for c in range(FIRST_OUT, FIRST_OUT + N_OUT):
            sp.wait_ge(sem("lo_done"), 2 * (c - 1))
            load_plain(c)
            if c == FIRST_OUT:
                sp.wait_ge(sem("v_tok_done"), 2)
                sp.dma_start(o["sguv_p"][0, 0], v_tok[:, 1, :]).then_inc(sem("out_dma"), 16)
                sp.dma_start(o["sguv_s"][0].rearrange("b s c -> (b s) c"),
                             v_tok[0:NSM, 2, :]).then_inc(sem("out_dma"), 16)
                sp.wait_ge(sem("tail_done"), 2)
                sp.dma_start(o["pool_p"][0, 0], tail_sb[32 - HP:32, 0, :]).then_inc(sem("out_dma"), 16)
                sp.dma_start(o["conv_p"][0, 0], tail_sb[32 - HC:32, 1, :]).then_inc(sem("out_dma"), 16)
                sp.dma_start(o["sconv_p"][0, 0], tail_sb[32 - HS:32, 2, :]).then_inc(sem("out_dma"), 16)
                sp.dma_start(tail_dram.rearrange("x r c -> r x c"),
                             tail_sb[32:TAIL, :, :]).then_inc(sem("tail_out"), 16)

        def load_pair(p, s):
            for j in range(2):
                e = p * 2 + j
                sp.dma_start(wgu[s][j][:, 0, :, :], w_gate4[e]).then_inc(sem(f"wgu_in{s}"), 16)
                sp.dma_start(wgu[s][j][:, 1, :, :], w_up4[e]).then_inc(sem(f"wgu_in{s}"), 16)

        def load_down(p, s):
            for j in range(2):
                sp.dma_start(wd[s][j][:, :, :], w_down4[p * 2 + j]).then_inc(sem(f"wd_in{s}"), 16)

        sp.wait_ge(sem("mg_lo"), 4)
        sp.wait_ge(sem("out_dma"), 16 * 7)
        sp.wait_ge(sem("tail_out"), 16)
        sp.wait_ge(sem("wsS_in"), 16 * NB)
        load_pair(0, 0)
        sp.wait_ge(sem("wo_mm"), NT * N_OUT)
        load_pair(1, 1)
        load_down(0, 0)
        load_down(1, 1)
        sp.wait_ge(sem("n2_done"), NT)
        for j in range(2):
            sp.dma_start(wd2[j][:, :, :], w_down4[4 + j]).then_inc(sem("wd2_in"), 16)
        sp.dma_start(o["pool_s"][0, :, HP - NS:HP, :],
                     tail_dram[0].rearrange("(b s) c -> b s c", b=NB)).then_inc(sem("out_dma"), 16)
        sp.dma_start(o["conv_s"][0, :, HC - NS:HC, :],
                     tail_dram[1].rearrange("(b s) c -> b s c", b=NB)).then_inc(sem("out_dma"), 16)
        sp.dma_start(o["sconv_s"][0],
                     tail_dram[2].rearrange("(b s) c -> b s c", b=NB)[:, NS - HS:NS, :]).then_inc(sem("out_dma"), 16)

        def load_quad(i):
            sp.wait_ge(sem("gu_mm"), i * 2 + 1)
            load_pair(i * 2 + 2, 0)
            if not (isinstance(i, int) and i == 0):
                sp.wait_ge(sem("dn_mm"), i * 2)
                load_down(i * 2 + 1, 1)
            sp.wait_ge(sem("gu_mm"), i * 2 + 2)
            if isinstance(i, int) and i == QUADS - 2:
                sp.wait_ge(sem("dn_mm"), i * 2 + 1)
                load_down(i * 2 + 2, 0)
            load_pair(i * 2 + 3, 1)
            if not isinstance(i, int):
                sp.wait_ge(sem("dn_mm"), i * 2 + 1)
                load_down(i * 2 + 2, 0)

        load_quad(0)
        with sp.Fori(1, QUADS - 2) as i:
            load_quad(i)
        load_quad(QUADS - 2)
        sp.wait_ge(sem("dn_mm"), PAIRS - 2)
        load_down(PAIRS - 1, 1)

        sp.wait_ge(sem("flag_ready"), 1)
        flag = sp.value_load(flag_i[0:1, 0:1], min_val=0, max_val=2 * T)
        with sp.If(flag > 0):
            with sp.Fori(0, NE) as e:
                sp.wait_ge(sem("ov_free"), e + 1)
                sp.dma_start(wgu[0][0][:, 0, :, :], w_gate4[e]).then_inc(sem("ov_in"), 16)
                sp.dma_start(wgu[0][0][:, 1, :, :], w_up4[e]).then_inc(sem("ov_in"), 16)
                sp.dma_start(wd[0][0][:, :, :], w_down4[e]).then_inc(sem("ov_in"), 16)
            sp.wait_ge(sem("ov_free"), NE + 1)

        for t in range(NT):
            sp.wait_ge(sem("y_done"), t + 1)
            if t:
                sp.wait_ge(sem("y_pool"), t)
            sp.dma_start(y_rows[t], x_tok[0:TILES[t][1], t, :]).then_inc(sem("out_dma"), 16)
        sp.wait_ge(sem("out_dma"), 16 * (7 + 3 + NT))

    @block.gpsimd
    def _(pool):
        g = nc.gpsimd
        const = sem("const_done")
        g.memset(ss[:, :], 1.0)
        g.memset(ssc[:, :, :], 1.0)
        g.memset(epsb[:, :], LN_EPS)
        g.memset(pw[:, :, :], 0.0).then_inc(const, 1)
        g.memset(ident[:, :], 0.0).then_inc(const, 1)
        pool.wait_ge(const, 2)
        g.affine_select(out=ident[:, :], in_=ident[:, :], compare_op=ALU.not_equal, fill=1.0, base=0,
                        pattern=[[-1, P]], channel_multiplier=1).then_inc(const, 1)
        g.memset(before[:, :], 1.0).then_inc(const, 1)
        g.iota(invc[:, :, :], pattern=[[0, CT], [1, NPR]], base=1, channel_multiplier=0,
               allow_small_or_imprecise_dtypes=True)
        pool.wait_ge(const, 4)
        g.affine_select(out=before[:, :], in_=before[:, :], compare_op=ALU.is_gt, fill=0.0, base=0,
                        pattern=[[1, P]], channel_multiplier=-1).then_inc(const, 1)
        g.memset(ones[:, :], 1.0)
        g.memset(mean_w[:, :], 1.0 / BW)
        g.memset(wsS[:, :, :], 0.0)
        g.memset(pext[:, :, 0:HP], 0.0)
        g.memset(cext[:, :, 0:HC], 0.0)
        g.memset(zext[:, :, 0:HS], 0.0).then_inc(const, 1)

        def lo(c, q, kn):
            for h, rows in enumerate((slice(0, KH), slice(KH, kn))):
                pool.wait_ge(sem("hi_done"), c * 2 + (h + 1))
                g.tensor_tensor(wl[q][:, rows, :], raw[q][:, rows, :], wh[q][:, rows, :].bitcast(F32),
                                ALU.subtract).then_inc(sem("lo_done"), 1)

        lo(0, 0, KT)
        lo(1, 1, KT)
        pool.wait_ge(sem("small_in"), 16 * N_SMALL)
        g.affine_select(out=ws_rows[:, :, :], in_=ws_rows[:, :, :], compare_op=ALU.is_ge, fill=0.0, base=0,
                        pattern=[[0, 4], [-1, P]], channel_multiplier=1).then_inc(sem("ws_masked"), 1)
        with pool.Fori(1, N_PROJ // 2) as i:
            for q in range(2):
                lo(i * 2 + q, q, KT)
        pool.wait_ge(sem("pool_ready"), 1)
        g.memset(merged[:, :, :], 0.0).then_inc(sem("merged_zero"), 1)
        pool.wait_ge(sem("small2_in"), 16 * N_SMALL2)
        g.tensor_copy(rw[:, :, 0:NG], rg[:, :, :])
        g.tensor_copy(rw[:, :, NG:NG + NE], re[:, :, :]).then_inc(sem("rw_done"), 1)
        with pool.Fori(0, N_GATE // 2) as i:
            for q in range(2):
                lo(i * 2 + (N_PROJ + q), q, KT + CT)
        with pool.Fori(0, N_OUT // 2) as i:
            for q in range(2):
                lo(i * 2 + (FIRST_OUT + q), q, KT)

        pool.wait_ge(sem("wo_mm"), 1)
        g.iota(iog[:, :, :], pattern=[[0, NT], [1, NG]], base=-NG, channel_multiplier=0,
               allow_small_or_imprecise_dtypes=True)
        g.iota(ioe[:, :, :], pattern=[[0, NT], [1, NE]], base=-NE, channel_multiplier=0,
               allow_small_or_imprecise_dtypes=True)
        g.iota(slot_no[:, :], pattern=[[1, CAP]], base=1, channel_multiplier=0,
               allow_small_or_imprecise_dtypes=True)
        g.memset(lgt[:, :, :], 0.0).then_inc(sem("moe_const"), 1)
        for t in range(2):
            pool.wait_ge(sem("xn_hi"), t + 2)
            g.tensor_tensor(xnl[:, t, :], xn2[:, t, :], xnh[:, t, :].bitcast(F32), ALU.subtract).then_inc(sem("xn_lo"), 1)

        for m, t in enumerate((1, 2)):
            pool.wait_ge(sem("y_row"), m + 1)
            n = TILES[t][1]
            g.tensor_tensor(x_tok[0:n, t, 0:512], x_tok[0:n, t, 0:512], gfb[0:n, 0:512], ALU.mult).then_inc(sem("y_pool"), 1)

    @block.tensor
    def _(pe):
        mm, tr = nc.tensor.matmul, nc.tensor.transpose

        def keep_clock(n, bank):
            for _ in range(n):
                mm(bank[:, 0:4 * P].rearrange("p (u c) -> p u c", u=4), ident[:, :],
                   ident[:, :].unsqueeze(1).to_broadcast([P, 4, P]), start=True, stop=True)

        pe.wait_ge(sem("const_done"), 3)
        keep_clock(3, banks[7])
        for u in range(2 * NT):
            t, h = u // 2, u % 2
            n = TILES[t][1]
            pe.wait_ge(sem("xs_done"), t + 1)
            for m in range(4):
                k = 4 * h + m
                last = tr(banks[u][:, m * P:m * P + n], xs[0:n, t, k * P:(k + 1) * P], ident[0:n, 0:n])
            last.then_inc(sem("xT_mm"), 1)

        keep_clock(3, banks[7])

        def prepare():
            pe.wait_ge(sem("small_in"), 16 * N_SMALL)
            pe.wait_ge(sem("ws_masked"), 1)
            for ct in range(CT):
                cs = slice(ct * P, (ct + 1) * P)
                n = NB * HP
                tr(banks[6][:, ct * n:(ct + 1) * n], pool_rows[:, cs], ident[0:n, 0:n])
                tr(banks[6][:, 240 + ct * 16:256 + ct * 16], sconv_rows[:, cs], ident[0:16, 0:16])
                last = tr(banks[6][:, 272 + ct * NPRM:272 + (ct + 1) * NPRM], prm_rows[:, cs], ident[0:NPRM, 0:NPRM])
            last.then_inc(sem("prep_mm"), 1)
            n = NB * HC // 2
            for h in range(2):
                for ct in range(CT):
                    last = tr(banks[7][:, (2 * h + ct) * n:(2 * h + ct + 1) * n],
                              conv_rows[:, h, ct * P:(ct + 1) * P], ident[0:n, 0:n])
            last.then_inc(sem("prep_mm"), 1)
            for h in range(4):
                last = tr(banks[4][:, h * P:(h + 1) * P], ws_rows[:, h, :], ident[:, :])
            last.then_inc(sem("prep_mm"), 1)

        def split_product(out, wq, k0, kn, cols, mh, ml, m0, half=None):
            for k in range(kn):
                if k == KH and half is not None:
                    pe.wait_ge(sem("lo_done"), half)
                w_h, w_l = wh[wq][:, k0 + k, cols], wl[wq][:, k0 + k, cols]
                mm(out, w_h, mh(m0 + k), start=(k == 0), stop=False)
                mm(out, w_h, ml(m0 + k), start=False, stop=False)
                last = mm(out, w_l, mh(m0 + k), start=False, stop=(k == kn - 1))
            return last

        def proj_chunk(c, q, par, first):
            pe.wait_ge(sem("lo_done"), c * 2 + 1)
            for j in range(2):
                if not first:
                    pe.wait_ge(sem("pj_ev"), c * 2 + (j - 3))
                split_product(banks[2 * par + j][:, 0:T], q, 0, KT, slice(j * P, (j + 1) * P),
                              lambda k: xh[:, k, :], lambda k: xl[:, k, :], 0,
                              c * 2 + 2 if j == 0 else None).then_inc(sem("pj_mm"), 1)

        pe.wait_ge(sem("xT_lo"), 2 * NT)
        proj_chunk(0, 0, 0, True)
        prepare()
        proj_chunk(1, 1, 1, True)
        proj_chunk(2, 0, 0, False)
        pe.wait_ge(sem("pool_ready"), 1)
        pe.wait_ge(sem("pw_in"), 64)
        pe.wait_ge(sem("prep_done"), 3)
        for ct in range(CT):
            last = mm(banks[6 + ct][:, 0:T], pw[:, ct, :], vn[:, ct, :], start=True, stop=True)
        last.then_inc(sem("map_mm"), 1)
        proj_chunk(3, 1, 1, False)
        with pe.Fori(2, N_PROJ // 2) as i:
            for q in range(2):
                proj_chunk(i * 2 + q, q, q, False)

        def channel_mean(bank, src):
            for ct in range(CT):
                last = mm(bank[:, 0:T], mean_w[:, :], src[:, ct, :], start=(ct == 0), stop=(ct == CT - 1))
            last.then_inc(sem("ln_mm"), 1)

        def v_mean():
            pe.wait_ge(sem("pj_ev"), 16)
            pe.wait_ge(sem("br_ready"), 1)
            channel_mean(banks[6], proj[:, 14:16, :])

        def v_var():
            pe.wait_ge(sem("ln_sq"), 1)
            channel_mean(banks[7], sqb)

        def b_mean():
            pe.wait_ge(sem("conv_step"), 4 * CW)
            pe.wait_ge(sem("mix_read"), 2)
            channel_mean(banks[6], cacc)

        def b_var():
            pe.wait_ge(sem("ln_sq"), 2)
            channel_mean(banks[7], sqb)

        def v_rows():
            pe.wait_ge(sem("v_norm"), 1)
            for t, (t0, n) in enumerate(TILES):
                for ct in range(CT):
                    out = banks[6 + t // 2][0:n, (t % 2) * BW + ct * P:(t % 2) * BW + (ct + 1) * P]
                    last = tr(out, vn[:, ct, t0:t0 + n], ident[:, :])
            last.then_inc(sem("vT_mm"), 1)

        def v_mix():
            pe.wait_ge(sem("v_tok_done"), 2)
            pe.wait_ge(sem("wsS_in"), 16 * NB)
            for h in range(4):
                q, ct = 64 * (h % 2), h // 2
                hc = slice(h * 64, (h + 1) * 64)
                for n in range(2):
                    mm(banks[6 + ct][q:q + 64, n * P:(n + 1) * P], v_tok[:, n, hc], wsT[:, h, :],
                       start=True, stop=True, tile_position=(0, q))
                last = mm(banks[6 + ct][q:q + 64, NPR:T], v_tok[0:NSM, 2, hc], wsS[:, h, :],
                          start=True, stop=True, tile_position=(0, q))
            last.then_inc(sem("mix_mm"), 1)

        def tails():
            pe.wait_ge(sem("z_done"), 1)
            pe.wait_ge(sem("ln_cent"), 2)
            pe.wait_ge(sem("ln_root"), 2)
            for x, k0 in enumerate((0, 2, 8)):
                for ct in range(CT):
                    out = banks[6 + x // 2][0:TAIL, (x % 2) * BW + ct * P:(x % 2) * BW + (ct + 1) * P]
                    last = tr(out, proj[:, k0 + ct, T - TAIL:T], ident[:, :])
            last.then_inc(sem("tail_mm"), 1)

        def gate_tile(i, j, extra=None):
            q, cols = (j // 2) % 2, slice((j % 2) * P, (j % 2 + 1) * P)
            g = i * 8 + j
            if j % 2 == 0:
                pe.wait_ge(sem("lo_done"), i * 8 + (2 * (N_PROJ + j // 2) + 1))
            if isinstance(i, int) and g < 4:
                pe.wait_ge(sem("pj_ev"), 13 + g)
            else:
                pe.wait_ge(sem("gate_sg"), g - 3)
            split_product(banks[j % 4][:, 0:T], q, 0, KT, cols,
                          lambda k: xh[:, k, :], lambda k: xl[:, k, :], 0,
                          i * 8 + (2 * (N_PROJ + j // 2) + 2) if j % 2 == 0 else None).then_inc(sem("gate_mm"), 1)
            pe.wait_ge(sem("br_ready"), i + 1)
            if not (isinstance(i, int) and g < 2):
                pe.wait_ge(sem("gp_done"), g - 1)
            out = banks[4 + j % 2][:, 0:T]
            split_product(out, q, KT, CT, cols, lambda k: brh[:, i * CT + k, :],
                          lambda k: brl[:, i * CT + k, :], 0).then_inc(sem("br_mm"), 1)
            if extra:
                extra()

        beside_a = {0: v_mean, 1: v_var, 3: v_rows, 5: v_mix}
        beside_c = {4: b_mean, 5: b_var, 7: tails}
        for j in range(8):
            gate_tile(0, j, beside_a.get(j))
        for j in range(8):
            gate_tile(1, j, beside_c.get(j))
        with pe.Fori(2, NBR) as i:
            for j in range(8):
                gate_tile(i, j)

        def out_tile(c, t, k0=0, k1=KT):
            q = c % 2
            t0, n = TILES[t]
            out = banks[3 * q + t][0:n, 0:CH]
            if c >= 2:
                pe.wait_ge(sem("wo_add"), NT * (c - 2) + t + 1)
            for k in range(k0, k1):
                if c == 0 and t == 0 and k % 2 == 0:
                    pe.wait_ge(sem("mg_lo"), k // 2 + 1)
                if t == 0 and k % KH == 0:
                    pe.wait_ge(sem("lo_done"), 2 * (FIRST_OUT + c) + k // KH + 1)
                mh, ml = brh[:, k, t0:t0 + n], brl[:, k, t0:t0 + n]
                mm(out, mh, wh[q][:, k, :], start=(k == 0), stop=False)
                mm(out, mh, wl[q][:, k, :], start=False, stop=False)
                last = mm(out, ml, wh[q][:, k, :], start=False, stop=(k == KT - 1))
            if k1 == KT:
                last.then_inc(sem("wo_mm"), 1)

        def norm_rows(t):
            n = TILES[t][1]
            pe.wait_ge(sem("n2_done"), t + 1)
            for h in range(2):
                for m in range(4):
                    last = tr(NORM_BANK[2 * t + h][:, m * P:m * P + n], xn2[0:n, t, 4 * h + m:D:KT], ident[0:n, 0:n])
                last.then_inc(sem("n2T_mm"), 1)

        def logits(t):
            t0, n = TILES[t]
            pe.wait_ge(sem("n2T_act"), t + 1)
            pe.wait_ge(sem("n2T_dve"), t + 1)
            if t == 0:
                pe.wait_ge(sem("rw_done"), 1)
            for k in range(KT):
                last = mm(banks[7][0:n, t * 64:t * 64 + NG + NE], xn2T[:, k, t0:t0 + n], rw[:, k, :],
                          start=(k == 0), stop=(k == KT - 1))
            last.then_inc(sem("lg_mm"), 1)

        for t in range(NT):
            out_tile(0, t, 0, KT - 2)
        for t in range(NT):
            out_tile(0, t, KT - 2, KT)
        for c in range(1, N_OUT - 1):
            for t in range(NT):
                out_tile(c, t)
        out_tile(N_OUT - 1, 0)
        out_tile(N_OUT - 1, 1)
        pe.wait_ge(sem("wo_add"), NT * (N_OUT - 1))
        pe.wait_ge(sem("tail_done"), 2)
        norm_rows(0)
        out_tile(N_OUT - 1, 2)
        norm_rows(1)
        logits(0)
        norm_rows(2)
        logits(1)
        logits(2)
        keep_clock(6, banks[5])
        pe.wait_ge(sem("both_done"), 1)
        pe.wait_ge(sem("count_w"), 1)
        pe.wait_ge(sem("n2T_dve"), NT)
        for t in range(NT):
            for u in range(t + 1):
                n = TILES[u][1]
                last = mm(banks[6][:, t * NE:(t + 1) * NE], (before_r if u == t else ones_r)[0:n, :], both[0:n, u, :],
                          start=(u == 0), stop=(u == t))
        last.then_inc(sem("cum_mm"), 1)
        keep_clock(1, banks[5])

        def rows_in(i):
            pe.wait_ge(sem("g_built"), i + 1)
            if not (isinstance(i, int) and i < 3):
                pe.wait_ge(sem("sc_add"), i * 6 - 12)
            for u in range(4):
                if not (isinstance(i, int) and i == 0):
                    if u == 0:
                        pe.wait_ge(sem("xg_done"), i * 4)
                    elif u == 3:
                        pe.wait_ge(sem("xg_done"), i * 4 + 1)
                elif u == 3:
                    pe.wait_ge(sem("xg_done"), 1)
                for j in range(2):
                    k = 2 * u + j
                    out = ring[IN_BANK[u]][:, j * QS:(j + 1) * QS]
                    for t, rows in ((0, xnh), (0, xnl), (1, xnh), (1, xnl), (2, xnh)):
                        last = mm(out, rows[:, t, k:D:KT], onehot[:, t, :, :].rearrange("p e c -> p (e c)"),
                                  start=(t == 0 and rows is xnh), stop=(t == 2))
                last.then_inc(sem("ga_mm"), 1)

        def weights_in(i):
            pe.wait_ge(sem("cwr_done"), 2)
            for m in range(2):
                for t, (_, n) in enumerate(TILES):
                    slots = onehot[0:n, t, 2 * m:2 * m + 2, :].rearrange("p e c -> p (e c)")
                    last = mm(psT[:, 256 + 4 * m:260 + 4 * m].rearrange("p (w e) -> p w e", w=2), slots,
                              cwr[0:n, t, :, bass.ds(i * QE + 2 * m, 2)],
                              start=(t == 0), stop=(t == NT - 1))
            last.then_inc(sem("cw_mm"), 1)

        def gate_up(p, s, i):
            pe.wait_ge(sem("xg_done"), i * 4 + 4)
            pe.wait_ge(sem(f"wgu_in{s}"), i * 64 + 64)
            if not (isinstance(p, int) and p < 2):
                pe.wait_ge(sem("h_done"), p - 1)
            for k in range(KT):
                for j in range(2):
                    q = 64 * j
                    last = mm(psG[s][q:q + 64, :].rearrange("p (w f) -> p w f", w=2),
                              xgT[:, k, (2 * s + j) * CAP:(2 * s + j + 1) * CAP],
                              wgu[s][j][:, :, k, :], start=(k == 0), stop=(k == KT - 1), tile_position=(0, q))
            last.then_inc(sem("gu_mm"), 1)

        def turn_hidden(p, s, i):
            pe.wait_ge(sem("h_done"), p + 1)
            pe.wait_ge(sem("cw_ev"), i + 1)
            if not (isinstance(p, int) and p == 0):
                pe.wait_ge(sem("hte_done"), p)
            for k in range(FK):
                last = tr(psT[:, k * P:(k + 1) * P], hh[s][:, k:F:FK], ident[:, :])
            last.then_inc(sem("ht_mm"), 1)

        def down(p, s, i):
            pe.wait_ge(sem("hte_done"), p + 1)
            if isinstance(p, int) and p == 2:
                pe.wait_ge(sem("wd2_in"), 32)
            elif s == 1 or (isinstance(i, int) and i == 0):
                pe.wait_ge(sem(f"wd_in{s}"), i * 32 + 32)
            else:
                pe.wait_ge(sem("wd_in0"), i * 32)
            wdp = wd2 if isinstance(p, int) and p == 2 else wd[s]
            if not (isinstance(p, int) and p == 0):
                pe.wait_ge(sem("yl_done"), p * 2)
            for half in range(2):
                for k in range(FK):
                    for j in range(2):
                        q = 64 * j
                        last = mm(psY[half][q:q + 64, :], hhT[s][:, k, q:q + 64],
                                  wdp[j][:, k, half * 512:(half + 1) * 512],
                                  start=(k == 0), stop=(k == FK - 1), tile_position=(0, q))
                if isinstance(p, int) and p == PAIRS - 1 and half == 0:
                    last.then_inc(sem("dn_first"), 1)
            last.then_inc(sem("dn_mm"), 1)

        def back(i, after):
            pe.wait_ge(sem("yl_done"), i * 4 + 2)
            pe.wait_ge(sem("st_ev"), i * 2 + 2)

            def part(u, m):
                t, half = BACK[u]
                t0, n = TILES[t]
                for y, first in ((yh, True), (yl, False)):
                    last = mm(ring[BACK_BANK[u]][0:n, :], slot_tok[:, m, t0:t0 + n],
                              y[:, m, half * 512:(half + 1) * 512],
                              start=(m == 0 and first), stop=(m == 1 and not first))
                return last

            for u in range(3):
                if after == "rows":
                    pe.wait_ge(sem("xg_done"), i * 4 + (10 + u))
                part(u, 0)
            pe.wait_ge(sem("yl_done"), i * 4 + 4)
            for u in range(6):
                if u >= 3:
                    pe.wait_ge(sem("sc_add"), i * 6 + (u - 2))
                    part(u, 0)
                part(u, 1).then_inc(sem("sc_mm"), 1)

        def turn_slots(i):
            pe.wait_ge(sem("gs_built"), i + 1)
            for m in range(2):
                if isinstance(i, int) and i == 0:
                    pe.wait_ge(sem("xg_done"), 4 + 2 + m)
                else:
                    pe.wait_ge(sem("sc_add"), i * 6 + (m - 2))
                for t, (t0, n) in enumerate(TILES):
                    last = tr(ring[TURN_BANK[m]][:, t0:t0 + n],
                              onehot_s[0:n, t, 2 * m:2 * m + 2, :].rearrange("p e c -> p (e c)").bitcast(F32),
                              ident[0:n, 0:n])
                last.then_inc(sem("st_mm"), 1)

        def quad(i):
            first, end = isinstance(i, int) and i == 0, isinstance(i, int) and i == QUADS - 1
            if not first:
                turn_hidden(i * 2 - 1, 1, i)
            gate_up(i * 2, 0, i)
            if not first:
                down(i * 2 - 1, 1, i - 1)
            if not end:
                gate_up(i * 2 + 1, 1, i)
                turn_hidden(i * 2, 0, i)
                rows_in(i + 1)
                pe.wait_ge(sem("hte_done"), i * 2 + 1)
                weights_in(i + 1)
            else:
                turn_hidden(i * 2, 0, i)
            if not first:
                back(i - 1, None if end else "rows")
            if first:
                pe.wait_ge(sem("flag_ready"), 1)
            if end:
                turn_slots(i)
            down(i * 2, 0, i)
            if end:
                gate_up(i * 2 + 1, 1, i)
            if not end:
                turn_slots(i)

        pe.wait_ge(sem("xn_lo"), 2)
        pe.wait_ge(sem("xn_lo_s"), 1)
        rows_in(0)
        weights_in(0)
        pe.wait_ge(sem("ovs_done"), 1)
        mm(banks[6][:, 256:257], ones_r[:, :].bitcast(F32), ovs[:, :], start=True, stop=True).then_inc(sem("ovs_mm"), 1)
        quad(0)
        quad(1)
        with pe.Fori(2, QUADS - 1) as i:
            quad(i)
        quad(QUADS - 1)
        def back_part(u, m):
            t, half = BACK[u]
            t0, n = TILES[t]
            for y, first in ((yh, True), (yl, False)):
                last = mm(banks[u][0:n, :], slot_tok[:, m, t0:t0 + n], y[:, m, half * 512:(half + 1) * 512],
                          start=(m == 0 and first), stop=(m == 1 and not first))
            return last

        pe.wait_ge(sem("yl_done"), PAIRS * 2 - 2)
        pe.wait_ge(sem("st_ev"), QUADS * 2)
        pe.wait_ge(sem("sc_add"), 6 * (QUADS - 1))
        for u in range(3):
            back_part(u, 0)
        turn_hidden(PAIRS - 1, 1, QUADS - 1)

        flag = pe.value_load(flag_i[0:1, 0:1], min_val=0, max_val=2 * T)
        with pe.If(flag > 0):
            pe.wait_ge(sem("ov_free"), 1)
            with pe.Fori(0, NE) as e:
                pe.wait_ge(sem("ov_in"), e * 48 + 48)
                for t, (t0, n) in enumerate(TILES):
                    pe.wait_ge(sem("ov_acc"), e * NT + (t + 1))
                    for k in range(KT):
                        last = mm(psG[0][0:n, :].rearrange("p (w f) -> p w f", w=2), xn2T[:, k, t0:t0 + n],
                                  wgu[0][0][:, :, k, :], start=(k == 0), stop=(k == KT - 1))
                    last.then_inc(sem("ov_gu"), 1)
                    pe.wait_ge(sem("ov_h"), e * NT + (t + 1))
                    for k in range(FK):
                        last = tr(psT[:, k * P:(k + 1) * P], hh[0][:, k:F:FK], ident[:, :])
                    last.then_inc(sem("ov_ht"), 1)
                    pe.wait_ge(sem("ov_hte"), e * NT + (t + 1))
                    for half in range(2):
                        for k in range(FK):
                            last = mm(psY[half][0:n, :], hhT[0][:, k, 0:n],
                                      wd[0][0][:, k, half * 512:(half + 1) * 512],
                                      start=(k == 0), stop=(k == FK - 1))
                    last.then_inc(sem("ov_dn"), 1)
            pe.wait_ge(sem("ov_free"), NE + 1)
        for u in (3, 4):
            back_part(u, 0)
        down(PAIRS - 1, 1, QUADS - 1)

        for u in range(6):
            pe.wait_ge(sem("yl_done"), PAIRS * 2 - 1 + BACK[u][1])
            if u == 5:
                back_part(u, 0)
            back_part(u, 1).then_inc(sem("sc_mm"), 1)


    @block.scalar
    def _(act):
        f = nc.scalar.activation

        def load_table(n, func):
            f(unread[:, n:n + 1], epsb[:, :], func)

        act.wait_ge(sem("const_done"), 1)
        load_table(0, ACT.Sqrt)
        for t, (_, n) in enumerate(TILES):
            act.wait_ge(x_in[t], 16)
            if t:
                act.wait_ge(sem("x_sq"), t)
            f(junk[0:n, :], x_tok[0:n, t, :], ACT.Square, accum_out=ss[0:n, t:t + 1]).then_inc(sem("x_sq"), 1)
            act.wait_ge(sem("x_ms"), t + 1)
            f(root[:, t:t + 1], ms[:, t:t + 1], ACT.Sqrt).then_inc(sem("x_root"), 1)

        def hi(c, q, kn):
            if isinstance(c, int) and c == 0:
                act.wait_ge(sem("raw_first"), 16)
                f(wh[0][:, 0:KH, :], raw[0][:, 0:KH, :], ACT.Copy).then_inc(sem("hi_done"), 1)
            act.wait_ge(raw_in[q], (c - q) // 2 * 16 + 16 if isinstance(c, int) else c * 8 + (16 - 8 * q))
            if kn > KT:
                n = (c - N_PROJ - q) // 2 * 16 + 16 if isinstance(c, int) else c * 8 + (16 - 8 * q - 8 * N_PROJ)
                act.wait_ge(wbr_in[q], n)
            for rows in (slice(0, KH), slice(KH, kn))[1 if isinstance(c, int) and c == 0 else 0:]:
                f(wh[q][:, rows, :], raw[q][:, rows, :], ACT.Copy).then_inc(sem("hi_done"), 1)

        def rows_high(t):
            t0, n = TILES[t]
            for h in range(2):
                u = 2 * t + h
                act.wait_ge(sem("xT_mm"), u + 1)
                f(xh[:, 4 * h:4 * h + 4, t0:t0 + n],
                  banks[u][:, :].rearrange("p (k c) -> p k c", c=P)[:, :, 0:n], ACT.Copy).then_inc(sem("xT_hi"), 1)

        rows_high(0)
        hi(0, 0, KT)
        rows_high(1)
        rows_high(2)
        hi(1, 1, KT)
        FUNC = {4: ACT.Sigmoid, 5: ACT.Sigmoid, 12: ACT.Gelu_apprx_tanh, 13: ACT.Gelu_apprx_tanh,
                14: ACT.Gelu_apprx_tanh, 15: ACT.Gelu_apprx_tanh}
        load_table(1, ACT.Sigmoid)
        for c in range(N_PROJ):
            for tl in (2 * c, 2 * c + 1):
                act.wait_ge(sem("pj_mm"), tl + 1)
                f(proj[:, tl, :], banks[tl % 4][:, 0:T], FUNC.get(tl, ACT.Copy)).then_inc(sem("pj_ev"), 1)
            hi(c + 2, c % 2, KT if c + 2 < N_PROJ else KT + CT)
            if c == 1:
                act.wait_ge(sem("prep_done"), 3)
                act.wait_ge(sem("const_done"), 6)
                for b in range(NB):
                    act.dma_start(wsS[b * NS:(b + 1) * NS, :, b * NS:(b + 1) * NS],
                                  wsT[0:NS, :, 0:NS]).then_inc(sem("wsS_in"), 16)
            if c == 2:
                act.wait_ge(sem("map_mm"), 1)
                for ct in range(CT):
                    last = f(brh[:, ct, :], banks[6 + ct][:, 0:T], ACT.Copy, scale=prm[:, ct, PRM["ps"]:PRM["ps"] + 1])
                last.then_inc(sem("br_hi"), 1)

        def gate(i, j):
            g = i * 8 + j
            act.wait_ge(sem("gate_mm"), g + 1)
            if not (isinstance(i, int) and g < 2):
                act.wait_ge(sem("gp_done"), g - 1)
            f(sig[j % 2][:, :], banks[j % 4][:, 0:T], ACT.Sigmoid).then_inc(sem("gate_sg"), 1)

        def next_hi(i, j, kn=KT + CT):
            act.wait_ge(sem("br_mm"), i * 8 + (j + 1))
            hi(i * 4 + (N_PROJ + j // 2 + 2), (j // 2) % 2, kn)

        def norm_rows_out(t):
            t0, n = TILES[t]
            act.wait_ge(sem("n2T_mm"), 2 * t + 1)
            f(xn2T[:, 0:4, t0:t0 + n], NORM_BANK[2 * t][:, :].rearrange("p (k c) -> p k c", c=P)[:, :, 0:n],
              ACT.Copy).then_inc(sem("n2T_act"), 1)

        def square(n):
            act.wait_ge(sem("ln_cent"), n)
            f(sqb[:, :, :], (vn if n == 1 else cacc)[:, :, :], ACT.Square).then_inc(sem("ln_sq"), 1)

        def sqrt(n):
            act.wait_ge(sem("ln_mm"), 2 * n)
            if n == 2:
                act.wait_ge(sem("v_norm"), 1)
            f(lnr[:, :], banks[7][:, 0:T], ACT.Sqrt, bias=epsb[:, 0:1]).then_inc(sem("ln_root"), 1)

        def br_high(n, src):
            act.wait_ge(sem("br_val"), n)
            f(brh[:, n * CT:(n + 1) * CT, :], src, ACT.Copy).then_inc(sem("br_hi"), 1)

        gate(0, 0)
        square(1)
        gate(0, 1)
        next_hi(0, 1)
        sqrt(1)
        gate(0, 2)
        gate(0, 3)
        next_hi(0, 3)
        br_high(1, proj[:, 10:12, :])
        gate(0, 4)
        gate(0, 5)
        next_hi(0, 5)
        gate(0, 6)
        br_high(2, proj[:, 12:14, :])
        gate(0, 7)
        next_hi(0, 7)
        for j in range(8):
            gate(1, j)
            if j % 2:
                next_hi(1, j)
            if j == 4:
                square(2)
            if j == 5:
                sqrt(2)
            if j == 6:
                act.wait_ge(sem("b_norm"), 1)
                f(sqb[:, :, :], cacc[:, :, :], ACT.Sigmoid).then_inc(sem("silu_gate"), 1)
        br_high(3, cacc[:, :, :])
        with act.Fori(2, NBR - 1) as i:
            for j in range(8):
                gate(i, j)
                if j % 2:
                    next_hi(i, j)

        def merged_high(n):
            act.wait_ge(sem("mg_add"), 26 + 2 * n)
            f(brh[:, 2 * n:2 * n + 2, :], merged[:, 2 * n:2 * n + 2, :], ACT.Copy).then_inc(sem("mg_hi"), 1)

        for j in range(8):
            gate(NBR - 1, j)
            if j == 7:
                merged_high(2)
                merged_high(3)
            if j % 2:
                next_hi(NBR - 1, j, KT + CT if j < 4 else KT)
            if j in (3, 5):
                merged_high((j - 3) // 2)
        load_table(2, ACT.Sqrt)

        def part_square(c, t):
            n = TILES[t][1]
            act.wait_ge(sem("wo_add"), NT * c + t + 1)
            if c or t:
                act.wait_ge(sem("n2_sq"), NT * c + t)
            f(sq_out[0:n, :], x_tok[0:n, t, c * CH:(c + 1) * CH], ACT.Square,
              accum_out=ssc[0:n, t, c:c + 1]).then_inc(sem("n2_sq"), 1)

        for c in range(N_OUT - 1):
            for t in range(NT):
                part_square(c, t)
            if c < 2:
                hi(FIRST_OUT + 2 + c, c, KT)
        for t in range(NT):
            part_square(N_OUT - 1, t)
            act.wait_ge(sem("n2_ms"), t + 1)
            f(root[:, t:t + 1], ms[:, t:t + 1], ACT.Sqrt).then_inc(sem("n2_root"), 1)
            if t:
                norm_rows_out(t - 1)
        norm_rows_out(2)
        for t in (2, 0, 1):
            n = TILES[t][1]
            f(xnh[0:n, t, :], xn2[0:n, t, :], ACT.Copy).then_inc(sem("xn_hi"), 1)
        act.wait_ge(sem("gsh_done"), 1)
        f(gex[:, :, :], gsh[:, :, :], ACT.Exp).then_inc(sem("rt_exp"), 1)
        act.wait_ge(sem("tdiff_done"), 1)
        f(ex[:, :], tidx[:, :], ACT.Exp).then_inc(sem("rt_exp"), 1)

        def rows_out(i):
            for u in range(4):
                act.wait_ge(sem("ga_mm"), i * 4 + (u + 1))
                f(xgT[:, 2 * u:2 * u + 2, :], ring[IN_BANK[u]][:, :].rearrange("p (k c) -> p k c", k=2),
                  ACT.Copy).then_inc(sem("xg_done"), 1)

        def silu(p, s):
            act.wait_ge(sem("gu_mm"), p + 1)
            if not (isinstance(p, int) and p < 2):
                act.wait_ge(sem("h_done"), p - 1)
            f(sg[s][:, :], psG[s][:, 0:F], ACT.Silu).then_inc(sem("sg_done"), 1)

        def y_high(p, s):
            for half in range(2):
                if isinstance(p, int) and p == PAIRS - 1 and half == 0:
                    act.wait_ge(sem("dn_first"), 1)
                elif half == 0 or (isinstance(p, int) and p == PAIRS - 1):
                    act.wait_ge(sem("dn_mm"), p + 1)
                f(yh[:, s, half * 512:(half + 1) * 512], psY[half][:, :], ACT.Copy).then_inc(sem("yh_done"), 1)

        def slots_out(i):
            for m in range(2):
                act.wait_ge(sem("st_mm"), i * 2 + (m + 1))
                f(slot_tok[:, m, :], ring[TURN_BANK[m]][:, 0:T], ACT.Copy).then_inc(sem("st_ev"), 1)

        def quad(i):
            first, end = isinstance(i, int) and i == 0, isinstance(i, int) and i == QUADS - 1
            silu(i * 2, 0)
            if not first:
                y_high(i * 2 - 1, 1)
            if end:
                slots_out(i)
                y_high(i * 2, 0)
            silu(i * 2 + 1, 1)
            if not end:
                rows_out(i + 1)
                y_high(i * 2, 0)
                slots_out(i)

        rows_out(0)
        act.wait_ge(sem("xn_lo"), 2)
        act.wait_ge(sem("xn_lo_s"), 1)
        quad(0)
        with act.Fori(1, QUADS - 1) as i:
            quad(i)
        quad(QUADS - 1)

        act.wait_ge(sem("flag_ready"), 1)
        flag = act.value_load(flag_i[0:1, 0:1], min_val=0, max_val=2 * T)
        with act.If(flag > 0):
            with act.Fori(0, NE) as e:
                for t, (_, n) in enumerate(TILES):
                    act.wait_ge(sem("ov_gu"), e * NT + (t + 1))
                    f(sg[0][0:n, :], psG[0][0:n, 0:F], ACT.Silu).then_inc(sem("ov_sg"), 1)

        load_table(3, ACT.Sqrt)
        y_high(PAIRS - 1, 1)

        for u, (t, half) in enumerate(BACK):
            n = TILES[t][1]
            act.wait_ge(sem("sc_add"), 6 * (QUADS - 1) + u + 1)
            if u:
                act.wait_ge(sem("f_sq"), u)
            f(junk2[0:n, 0:512], x_tok[0:n, t, half * 512:(half + 1) * 512], ACT.Square,
              accum_out=ssc[0:n, t, half:half + 1]).then_inc(sem("f_sq"), 1)
        act.wait_ge(sem("f_ms"), 1)
        f(root[:, :], ms[:, :], ACT.Sqrt).then_inc(sem("f_root"), 1)
        act.wait_ge(sem("f_rstd"), 1)
        for t in (1, 2):
            n = TILES[t][1]
            f(x_tok[0:n, t, 0:512], x_tok[0:n, t, 0:512], ACT.Copy, scale=rstd[0:n, t:t + 1]).then_inc(sem("y_row"), 1)

    @block.vector
    def _(dve):
        v = nc.vector
        own = Steps(dve, "dve_step")

        def scale(t, sums, name):
            v.tensor_scalar(ms[:, t:t + 1], sums, 1.0 / D, RMS_EPS, ALU.mult, ALU.add).then_inc(sem(name + "_ms"), 1)
            dve.wait_ge(sem(name + "_root"), t + 1)
            own.step(v.reciprocal(rstd[:, t:t + 1], root[:, t:t + 1]))
            own.last()

        def scale_x(t):
            dve.wait_ge(sem("x_sq"), t + 1)
            scale(t, ss[:, t:t + 1], "x")

        scale_x(0)
        scale_x(1)
        dve.wait_ge(sem("g1_in"), 16)
        for t, (_, n) in enumerate(TILES):
            if t == 2:
                scale_x(2)
            v.scalar_tensor_tensor(xs[0:n, t, :], x_tok[0:n, t, :], rstd[0:n, t:t + 1], g1b[0:n, :],
                                   ALU.mult, ALU.mult).then_inc(sem("xs_done"), 1)
        for u in range(2 * NT):
            t, h = u // 2, u % 2
            t0, n = TILES[t]
            dve.wait_ge(sem("xT_hi"), u + 1)
            v.tensor_tensor(xl[:, 4 * h:4 * h + 4, t0:t0 + n],
                            banks[u][:, :].rearrange("p (k c) -> p k c", c=P)[:, :, 0:n],
                            xh[:, 4 * h:4 * h + 4, t0:t0 + n].bitcast(F32), ALU.subtract).then_inc(sem("xT_lo"), 1)

        dve.wait_ge(sem("const_done"), 6)
        for n, w in enumerate(WINDOWS):
            q = 64 * (n % 2)
            last = v.tensor_scalar(invc[q:q + 64, n // 2, :], invc[q:q + 64, n // 2, :], float(w), None, ALU.min)
        own.step(last)
        own.last()
        own.step(v.reciprocal(invc[:, :, :], invc[:, :, :]))
        dve.wait_ge(sem("prep_mm"), 1)
        dve.wait_ge(sem("const_done"), 6)
        v.tensor_copy(seg(pext, LP, HP)[:, :, :, 0:HP],
                      banks[6][:, 0:240].rearrange("p (c b r) -> p c b r", c=CT, b=NB))
        v.tensor_copy(seg(zext, LS, HS)[:, :, :, 0:HS],
                      banks[6][:, 240:272].rearrange("p (c b r) -> p c b r", c=CT, b=NB))
        v.tensor_copy(prm[:, :, :], banks[6][:, 272:272 + CT * NPRM].rearrange("p (c r) -> p c r", c=CT)).then_inc(sem("prep_done"), 1)
        dve.wait_ge(sem("prep_mm"), 2)
        for h in range(2):
            last = v.tensor_copy(seg(cext, LC, HC)[:, :, 4 * h:4 * h + 4, 0:HC],
                                 banks[7][:, h * 240:(h + 1) * 240].rearrange("p (c b r) -> p c b r", c=CT, b=4))
        last.then_inc(sem("prep_done"), 1)
        dve.wait_ge(sem("prep_mm"), 3)
        v.tensor_copy(wsT[:, :, :], banks[4][:, :].rearrange("p (h t) -> p h t", h=4)).then_inc(sem("prep_done"), 1)

        v.tensor_copy(before_r[:, :], before[:, :])
        v.tensor_copy(ones_r[:, :], ones[:, :]).then_inc(sem("count_w"), 1)

        dve.wait_ge(sem("pj_ev"), 2)
        v.tensor_copy(pext[:, :, HP:LP], proj[:, 0:2, 0:NPR])
        own.step(v.tensor_copy(seg(pext, LP, HP)[:, :, :, HP:], smp(proj[:, 0:2, :])))
        dve.wait_ge(sem("prep_done"), 1)
        own.last()
        own.step(v.tensor_tensor(sum2[:, :, 1:], pext[:, :, 1:], pext[:, :, :-1], ALU.add))
        own.last()
        own.step(v.tensor_tensor(sum4[:, :, 3:], sum2[:, :, 3:], sum2[:, :, 1:-2], ALU.add))
        own.last()
        own.step(v.tensor_tensor(sum8[:, 7:], sum4[:, 1, 7:], sum4[:, 1, 3:-4], ALU.add))
        own.last()
        own.step(v.tensor_tensor(sum16[64:128, 15:], sum8[64:128, 15:], sum8[64:128, 7:-8], ALU.add))
        own.last()
        for n, (w, sums) in enumerate(zip(WINDOWS, (sum2[:, 0, :], sum4[:, 0, :], sum8, sum16))):
            q, ct = slice(64 * (n % 2), 64 * (n % 2) + 64), n // 2
            v.tensor_tensor(vn[q, ct, 0:NPR], sums[q, HP:LP], invc[q, ct, :], ALU.mult)
            last = v.tensor_scalar(smp(vn[q, ct:ct + 1, :])[:, 0], sums[q, LP:].rearrange("p (b s) -> p b s", b=NB)[:, :, HP:],
                                   1.0 / w, None, ALU.mult)
        own.step(last)
        own.last()
        v.tensor_tensor(vn[:, :, :], vn[:, :, :], proj[:, 0:2, :], ALU.subtract).then_inc(sem("pool_ready"), 1)

        dve.wait_ge(sem("pj_ev"), 6)
        dve.wait_ge(sem("prep_done"), 2)
        own.step(v.tensor_tensor(proj[:, 2:4, :], proj[:, 2:4, :], proj[:, 4:6, :], ALU.mult))
        own.last()
        v.tensor_copy(cext[:, :, HC:LC], proj[:, 2:4, 0:NPR])
        own.step(v.tensor_copy(seg(cext, LC, HC)[:, :, :, HC:], smp(proj[:, 2:4, :])))
        own.last()
        conv_parts = [(ct, part) for ct in range(CT) for part in range(2)]

        def tap_view(ext, base, hist, ct, part, k):
            if part == 0:
                return ext[:, ct, bass.ds(k, NPR)]
            return seg(ext, base, hist)[:, ct, :, bass.ds(k, NS)]

        def acc_view(acc, ct, part):
            return acc[:, ct, 0:NPR] if part == 0 else smp(acc[:, :, :])[:, ct]

        conv = sem("conv_step")
        for ct, part in conv_parts:
            v.tensor_scalar(acc_view(cacc, ct, part), tap_view(cext, LC, HC, ct, part, 0),
                            prm[:, ct, PRM["dw"]:PRM["dw"] + 1], prm[:, ct, PRM["dwb"]:PRM["dwb"] + 1],
                            ALU.mult, ALU.add).then_inc(conv, 1)

        def tap(k):
            for n, (ct, part) in enumerate(conv_parts):
                dve.wait_ge(conv, k * 4 + (n - 3))
                acc = acc_view(cacc, ct, part)
                v.scalar_tensor_tensor(acc, tap_view(cext, LC, HC, ct, part, k), prm[:, ct, bass.ds(k, 1)], acc,
                                       ALU.mult, ALU.add).then_inc(conv, 1)

        def br_low(n, val):
            dve.wait_ge(sem("br_hi"), n + 1)
            v.tensor_tensor(brl[:, n * CT:(n + 1) * CT, :], val, brh[:, n * CT:(n + 1) * CT, :].bitcast(F32),
                            ALU.subtract).then_inc(sem("br_ready"), 1)

        dve.wait_ge(sem("br_hi"), 1)
        for ct in range(CT):
            last = v.scalar_tensor_tensor(brl[:, ct, :], banks[6 + ct][:, 0:T], prm[:, ct, PRM["ps"]:PRM["ps"] + 1],
                                          brh[:, ct, :].bitcast(F32), ALU.mult, ALU.subtract)
        last.then_inc(sem("br_ready"), 1)
        with dve.Fori(1, TAPS_EARLY) as k:
            tap(k)

        def merge(i, j):
            g = i * 8 + j
            dve.wait_ge(sem("gate_sg"), g + 1)
            dve.wait_ge(sem("br_mm"), g + 1)
            if not (isinstance(i, int) and g < 2):
                dve.wait_ge(sem("mg_add"), g - 1)
            v.tensor_tensor(prod[j % 2][:, :], sig[j % 2][:, :], banks[4 + j % 2][:, 0:T], ALU.mult).then_inc(sem("gp_done"), 1)
            dve.wait_ge(sem("gp_done"), g + 1)
            if isinstance(i, int) and g == 0:
                dve.wait_ge(sem("merged_zero"), 1)
            v.tensor_tensor(merged[:, j, :], merged[:, j, :], prod[j % 2][:, :], ALU.add).then_inc(sem("mg_add"), 1)

        def center(src, dst):
            mean = banks[6][:, 0:T].unsqueeze(1).to_broadcast([P, CT, T])
            v.tensor_tensor(dst, src, mean, ALU.subtract).then_inc(sem("ln_cent"), 1)

        def normalise(n, x, g, b, done):
            dve.wait_ge(sem("ln_root"), n)
            dve.wait_ge(sem("ln_sq"), n)
            own.step(v.reciprocal(lnr[:, :], lnr[:, :]))
            own.last()
            own.step(v.tensor_tensor(x, x, lnr[:, :].unsqueeze(1).to_broadcast([P, CT, T]), ALU.mult))
            own.last()
            for ct in range(CT):
                last = v.tensor_scalar(x[:, ct, :], x[:, ct, :], prm[:, ct, PRM[g]:PRM[g] + 1],
                                       prm[:, ct, PRM[b]:PRM[b] + 1], ALU.mult, ALU.add)
            last.then_inc(sem(done), 1)

        def taps(k, n):
            for m in range(n):
                tap(k + m)

        dve.wait_ge(sem("ln_mm"), 1)
        dve.wait_ge(sem("map_mm"), 1)
        center(proj[:, 14:16, :], vn[:, :, :])
        merge(0, 0)
        dve.wait_ge(sem("pj_ev"), 12)
        v.tensor_tensor(proj[:, 8:10, :], proj[:, 8:10, :], proj[:, 10:12, :], ALU.mult).then_inc(sem("z_done"), 1)
        dve.wait_ge(sem("z_done"), 1)
        v.tensor_copy(zext[:, :, HS:LS], proj[:, 8:10, 0:NPR])
        own.step(v.tensor_copy(seg(zext, LS, HS)[:, :, :, HS:], smp(proj[:, 8:10, :])))
        own.last()
        merge(0, 1)
        zc = Steps(dve, "sconv_step")
        for k in range(SW):
            for n, (ct, part) in enumerate(conv_parts):
                acc, row = acc_view(proj[:, 10:12, :], ct, part), tap_view(zext, LS, HS, ct, part, k)
                w = prm[:, ct, PRM["sw"] + k:PRM["sw"] + k + 1]
                if k == 0:
                    zc.step(v.tensor_scalar(acc, row, w, None, ALU.mult))
                else:
                    dve.wait_ge(sem("sconv_step"), 4 * k + n - 3)
                    zc.step(v.scalar_tensor_tensor(acc, row, w, acc, ALU.mult, ALU.add))
        zc.last()
        v.tensor_tensor(proj[:, 10:12, :], proj[:, 10:12, :], proj[:, 6:8, :], ALU.mult).then_inc(sem("br_val"), 1)
        normalise(1, vn[:, :, :], "vg", "vb", "v_norm")
        merge(0, 2)
        merge(0, 3)
        dve.wait_ge(sem("vT_mm"), 1)
        v.tensor_copy(v_tok[:, 0:2, :], banks[6][:, :].rearrange("p (t c) -> p t c", t=2)).then_inc(sem("v_tok_done"), 1)
        v.tensor_copy(v_tok[0:NSM, 2, :], banks[7][0:NSM, 0:BW]).then_inc(sem("v_tok_done"), 1)
        br_low(1, proj[:, 10:12, :])
        merge(0, 4)
        taps(TAPS_EARLY, 2)
        merge(0, 5)
        dve.wait_ge(sem("mix_mm"), 1)
        for ct in range(CT):
            v.tensor_tensor(proj[:, 14 + ct, 0:NPR].rearrange("p (n t) -> p n t", n=2),
                            banks[6 + ct][:, 0:NPR].rearrange("p (n t) -> p n t", n=2),
                            bS[:, ct, :].unsqueeze(1).to_broadcast([P, 2, P]), ALU.add)
            v.tensor_tensor(proj[:, 14 + ct, NPR:T].rearrange("p (b s) -> p b s", b=NB),
                            banks[6 + ct][:, NPR:T].rearrange("p (b s) -> p b s", b=NB),
                            bS[:, ct, 0:NS].unsqueeze(1).to_broadcast([P, NB, NS]), ALU.add).then_inc(sem("mix_read"), 1)
        dve.wait_ge(sem("mix_read"), 2)
        v.tensor_tensor(proj[:, 12:14, :], proj[:, 12:14, :], proj[:, 14:16, :], ALU.mult).then_inc(sem("br_val"), 1)
        merge(0, 6)
        taps(TAPS_EARLY + 2, 2)
        merge(0, 7)
        br_low(2, proj[:, 12:14, :])
        taps(TAPS_EARLY + 4, 2)

        left = CW - TAPS_EARLY - 6
        for j in range(8):
            merge(1, j)
            if j < 4:
                taps(TAPS_EARLY + 6 + left * j // 4, left * (j + 1) // 4 - left * j // 4)
            if j == 4:
                dve.wait_ge(sem("ln_mm"), 3)
                center(cacc[:, :, :], cacc[:, :, :])
            if j == 5:
                normalise(2, cacc[:, :, :], "lng", "lnb", "b_norm")
        dve.wait_ge(sem("silu_gate"), 1)
        v.tensor_tensor(cacc[:, :, :], cacc[:, :, :], sqb[:, :, :], ALU.mult).then_inc(sem("br_val"), 1)
        dve.wait_ge(sem("tail_mm"), 1)
        v.tensor_copy(tail_sb[:, 0:2, :], banks[6][0:TAIL, :].rearrange("p (x c) -> p x c", x=2)).then_inc(sem("tail_done"), 1)
        v.tensor_copy(tail_sb[:, 2, :], banks[7][0:TAIL, 0:BW]).then_inc(sem("tail_done"), 1)
        dve.wait_ge(sem("br_val"), 3)
        br_low(3, cacc[:, :, :])
        with dve.Fori(2, NBR - 1) as i:
            for j in range(8):
                merge(i, j)

        def merged_low(n):
            dve.wait_ge(sem("mg_hi"), n + 1)
            v.tensor_tensor(brl[:, 2 * n:2 * n + 2, :], merged[:, 2 * n:2 * n + 2, :],
                            brh[:, 2 * n:2 * n + 2, :].bitcast(F32), ALU.subtract).then_inc(sem("mg_lo"), 1)

        for j in range(8):
            merge(NBR - 1, j)
            if j > 3 and j % 2 == 0:
                merged_low((j - 4) // 2)
        merged_low(2)
        merged_low(3)
        def norm_rows_out(t):
            t0, n = TILES[t]
            dve.wait_ge(sem("n2T_mm"), 2 * t + 2)
            v.tensor_copy(xn2T[:, 4:8, t0:t0 + n],
                          NORM_BANK[2 * t + 1][:, :].rearrange("p (k c) -> p k c", c=P)[:, :, 0:n]).then_inc(sem("n2T_dve"), 1)

        for c in range(N_OUT):
            for t, (_, n) in enumerate(TILES):
                dve.wait_ge(sem("wo_mm"), NT * c + t + 1)
                xc = x_tok[0:n, t, c * CH:(c + 1) * CH]
                v.tensor_tensor(xc, xc, banks[3 * (c % 2) + t][0:n, 0:CH], ALU.add).then_inc(sem("wo_add"), 1)
                if c == N_OUT - 1:
                    dve.wait_ge(sem("n2_sq"), NT * c + t + 1)
                    own.step(v.tensor_reduce(ss[0:n, t:t + 1], ssc[0:n, t, :], axis=AX_X, op=ALU.add))
                    own.last()
                    scale(t, ss[:, t:t + 1], "n2")
                    if t == 0:
                        dve.wait_ge(sem("small2_in"), 16 * N_SMALL2)
                    v.scalar_tensor_tensor(xn2[0:n, t, :], x_tok[0:n, t, :], rstd[0:n, t:t + 1], g2b[0:n, :],
                                           ALU.mult, ALU.mult).then_inc(sem("n2_done"), 1)
                    if t:
                        norm_rows_out(t - 1)
        norm_rows_out(2)
        dve.wait_ge(sem("xn_hi"), 1)
        v.tensor_tensor(xnh[64:128, 2, :], xn2[0:64, 2, :], xnh[0:64, 2, :].bitcast(F32), ALU.subtract).then_inc(sem("xn_lo_s"), 1)

        def op(ins):
            own.step(ins)
            own.last()

        def wide(x, n):
            return x.unsqueeze(2).to_broadcast([P, NT, n])

        dve.wait_ge(sem("lg_mm"), NT)
        dve.wait_ge(sem("moe_const"), 1)
        logits = banks[7][:, 0:NT * 64].rearrange("p (t c) -> p t c", t=NT)[:, :, 0:NG + NE]
        v.tensor_tensor(lgt[:, 0:2, :], logits[:, 0:2, :], rb[:, :].unsqueeze(1).to_broadcast([P, 2, NG + NE]), ALU.add)
        op(v.tensor_tensor(lgt[0:NSM, 2, :], logits[0:NSM, 2, :], rb[0:NSM, :], ALU.add))
        op(v.tensor_reduce(gmax[:, :], lgt[:, :, 0:NG], axis=AX_X, op=ALU.max))
        v.tensor_tensor(gsh[:, :, :], lgt[:, :, 0:NG], wide(gmax[:, :], NG), ALU.subtract).then_inc(sem("gsh_done"), 1)
        dve.wait_ge(sem("gsh_done"), 1)
        op(v.scalar_tensor_tensor(geq[:, :, :], gsh[:, :, :], 0.0, iog[:, :, :], ALU.is_equal, ALU.mult))
        op(v.tensor_reduce(gidx[:, :], geq[:, :, :], axis=AX_X, op=ALU.min))
        op(v.tensor_tensor(geq[:, :, :], iog[:, :, :], wide(gidx[:, :], NG), ALU.not_equal))
        for t in range(NT):
            last = v.scalar_tensor_tensor(lem[:, t, :].rearrange("p (g e) -> p g e", g=NG),
                                          geq[:, t, :].unsqueeze(2).to_broadcast([P, NG, EG]), -1.0e30,
                                          lgt[:, t, NG:NG + NE].rearrange("p (g e) -> p g e", g=NG),
                                          ALU.mult, ALU.add)
        op(last)
        for w in range(2):
            op(v.tensor_reduce(topv[w][:, :], lem[:, :, :], axis=AX_X, op=ALU.max))
            for t in range(NT):
                last = v.scalar_tensor_tensor(eqm[:, t, :], lem[:, t, :], topv[w][:, t:t + 1], ioe[:, t, :],
                                              ALU.is_equal, ALU.mult)
            op(last)
            op(v.tensor_reduce(tidx[:, :], eqm[:, :, :], axis=AX_X, op=ALU.min))
            op(v.tensor_tensor(oh[w][:, :, :], ioe[:, :, :], wide(tidx[:, :], NE), ALU.is_equal))
            if w == 0:
                op(v.scalar_tensor_tensor(lem[:, :, :], oh[0][:, :, :], -1.0e38, lem[:, :, :], ALU.mult, ALU.add))
        v.tensor_tensor(both[:, 0:2, :], oh[0][:, 0:2, :], oh[1][:, 0:2, :], ALU.add)
        v.tensor_tensor(both[0:64, 2, :], oh[0][0:64, 2, :], oh[1][0:64, 2, :], ALU.add).then_inc(sem("both_done"), 1)
        v.tensor_tensor(tidx[:, :], topv[1][:, :], topv[0][:, :], ALU.subtract).then_inc(sem("tdiff_done"), 1)
        dve.wait_ge(sem("rt_exp"), 2)
        op(v.tensor_reduce(psel[:, :], gex[:, :, :], axis=AX_X, op=ALU.add))
        v.reciprocal(psel[:, :], psel[:, :])
        op(v.tensor_scalar(tw[0][:, :], ex[:, :], 1.0, None, ALU.add))
        op(v.reciprocal(tw[0][:, :], tw[0][:, :]))
        op(v.tensor_tensor(tw[0][:, :], tw[0][:, :], psel[:, :], ALU.mult))
        op(v.tensor_tensor(tw[1][:, :], tw[0][:, :], ex[:, :], ALU.mult))
        op(v.tensor_tensor(cwt[:, :, :], oh[0][:, :, :], wide(tw[0][:, :], NE), ALU.mult))
        op(v.tensor_tensor(rtmp[:, :, :], oh[1][:, :, :], wide(tw[1][:, :], NE), ALU.mult))
        v.tensor_tensor(cwt[:, :, :], cwt[:, :, :], rtmp[:, :, :], ALU.add).then_inc(sem("cwt_done"), 1)

        def weight_halves():
            dve.wait_ge(sem("cwt_done"), 1)
            v.tensor_copy(cwr[:, :, 0, :], cwt[:, :, :]).then_inc(sem("cwr_done"), 1)
            dve.wait_ge(sem("cwr_done"), 1)
            v.tensor_tensor(cwr[:, :, 1, :], cwt[:, :, :], cwr[:, :, 0, :].bitcast(F32), ALU.subtract).then_inc(sem("cwr_done"), 1)

        dve.wait_ge(sem("cum_mm"), 1)
        dve.wait_ge(sem("both_done"), 1)
        cum = banks[6][:, 0:NT * NE].rearrange("p (t e) -> p t e", t=NT)
        v.scalar_tensor_tensor(pos[:, 0:2, :], cum[:, 0:2, :], 1.0, both[:, 0:2, :].bitcast(F32), ALU.add, ALU.mult)
        v.scalar_tensor_tensor(pos[0:64, 2, :], cum[0:64, 2, :], 1.0, both[0:64, 2, :].bitcast(F32), ALU.add, ALU.mult)
        op(v.scalar_tensor_tensor(pos[64:128, 2, :], cum[0:64, 2, :], 1.0, both[0:64, 2, :].bitcast(F32), ALU.add, ALU.mult))

        def one_hot(out, i, done):
            v.tensor_tensor(out[:, :, :, :], pos[:, :, bass.ds(i * QE, QE)].unsqueeze(3).to_broadcast([P, NT, QE, CAP]),
                            slot_no[:, :].unsqueeze(1).unsqueeze(1).to_broadcast([P, NT, QE, CAP]),
                            ALU.is_equal).then_inc(sem(done), 1)

        one_hot(onehot, 0, "g_built")
        weight_halves()
        v.memset(over[64:128, 2, :], 0.0)
        v.tensor_scalar(over[:, 0:2, :], pos[:, 0:2, :], float(CAP), None, ALU.is_gt)
        op(v.tensor_scalar(over[0:64, 2, :], pos[0:64, 2, :], float(CAP), None, ALU.is_gt))
        v.tensor_reduce(ovs[:, :], over[:, :, :].rearrange("p t e -> p (t e)"), axis=AX_X, op=ALU.add).then_inc(sem("ovs_done"), 1)
        dve.wait_ge(sem("cwt_done"), 1)
        op(v.tensor_tensor(cwo[:, :, :], cwt[:, :, :], over[:, :, :], ALU.mult))
        dve.wait_ge(sem("ovs_mm"), 1)
        v.tensor_copy(flag_i[0:1, :], banks[6][0:1, 256:257]).then_inc(sem("flag_ready"), 1)

        def weights_out(i):
            dve.wait_ge(sem("cw_mm"), i + 1)
            w2 = psT[:, 256:264].rearrange("p (m w e) -> p m w e", m=2, w=2)
            v.tensor_reduce(slot_w[0:64, :], w2[0:64, :, :, 0], axis=AX_X, op=ALU.add)
            v.tensor_reduce(slot_w[64:128, :], w2[64:128, :, :, 1], axis=AX_X, op=ALU.add).then_inc(sem("cw_ev"), 1)

        def hidden(p, s):
            dve.wait_ge(sem("sg_done"), p + 1)
            if not (isinstance(p, int) and p < 2):
                dve.wait_ge(sem("ht_mm"), p - 1)
            v.scalar_tensor_tensor(hh[s][:, :], sg[s][:, :], slot_w[:, s:s + 1],
                                   psG[s][:, F:2 * F], ALU.mult, ALU.mult).then_inc(sem("h_done"), 1)

        def hidden_T(p, s):
            dve.wait_ge(sem("ht_mm"), p + 1)
            v.tensor_copy(hhT[s][:, :, :], psT[:, 0:FK * P].rearrange("p (k c) -> p k c", k=FK)).then_inc(sem("hte_done"), 1)

        def y_low(p, s):
            for half in range(2):
                dve.wait_ge(sem("yh_done"), p * 2 + (half + 1))
                cols = slice(half * 512, (half + 1) * 512)
                v.tensor_tensor(yl[:, s, cols], psY[half][:, :], yh[:, s, cols].bitcast(F32),
                                ALU.subtract).then_inc(sem("yl_done"), 1)

        def add_back(i, u):
            t, half = BACK[u]
            n = TILES[t][1]
            dve.wait_ge(sem("sc_mm"), i * 6 + (u + 1))
            xc = x_tok[0:n, t, half * 512:(half + 1) * 512]
            bank = banks[u] if isinstance(i, int) and i == QUADS - 1 else ring[BACK_BANK[u]]
            v.tensor_tensor(xc, xc, bank[0:n, :], ALU.add).then_inc(sem("sc_add"), 1)

        def quad(i):
            first, end = isinstance(i, int) and i == 0, isinstance(i, int) and i == QUADS - 1
            if not first:
                hidden_T(i * 2 - 1, 1)
                dve.wait_ge(sem("st_mm"), i * 2)
            one_hot(onehot_s, i, "gs_built")
            if not end:
                dve.wait_ge(sem("cw_mm"), i + 1)
                one_hot(onehot, i + 1, "g_built")
            dve.wait_ge(sem("cw_ev"), i + 1)
            hidden(i * 2, 0)
            if not first:
                y_low(i * 2 - 1, 1)
            if not end:
                hidden(i * 2 + 1, 1)
            hidden_T(i * 2, 0)
            if not end:
                dve.wait_ge(sem("h_done"), i * 2 + 2)
                weights_out(i + 1)
            if not first:
                for u in range(6):
                    add_back(i - 1, u)
            y_low(i * 2, 0)
            if end:
                hidden(i * 2 + 1, 1)

        weights_out(0)
        quad(0)
        with dve.Fori(1, QUADS - 1) as i:
            quad(i)
        quad(QUADS - 1)
        hidden_T(PAIRS - 1, 1)

        dve.wait_ge(sem("flag_ready"), 1)
        flag = dve.value_load(flag_i[0:1, 0:1], min_val=0, max_val=2 * T)
        with dve.If(flag > 0):
            dve.wait_ge(sem("sc_add"), 6 * (QUADS - 1))
            v.memset(ovs[:, :], 0.0).then_inc(sem("ov_free"), 1)
            v.memset(ov_cw[:, :], 0.0).then_inc(sem("ov_acc"), 1)
            with dve.Fori(0, NE) as e:
                dve.wait_ge(sem("ov_acc"), e * NT + 1)
                v.tensor_copy(ov_cw[:, :], cwo[:, :, e]).then_inc(sem("ov_cw"), 1)
                dve.wait_ge(sem("ov_cw"), e + 1)
                for t, (_, n) in enumerate(TILES):
                    dve.wait_ge(sem("ov_sg"), e * NT + (t + 1))
                    v.scalar_tensor_tensor(hh[0][0:n, :], sg[0][0:n, :], ov_cw[0:n, t:t + 1],
                                           psG[0][0:n, F:2 * F], ALU.mult, ALU.mult).then_inc(sem("ov_h"), 1)
                    dve.wait_ge(sem("ov_ht"), e * NT + (t + 1))
                    v.tensor_copy(hhT[0][:, :, 0:n],
                                  psT[:, 0:FK * P].rearrange("p (k c) -> p k c", k=FK)[:, :, 0:n]).then_inc(sem("ov_hte"), 1)
                    dve.wait_ge(sem("ov_dn"), e * NT + (t + 1))
                    v.tensor_tensor(x_tok[0:n, t, 0:512], x_tok[0:n, t, 0:512], psY[0][0:n, :], ALU.add)
                    v.tensor_tensor(x_tok[0:n, t, 512:D], x_tok[0:n, t, 512:D], psY[1][0:n, :], ALU.add).then_inc(sem("ov_acc"), 1)
                v.memset(ovs[:, :], 0.0).then_inc(sem("ov_free"), 1)

        y_low(PAIRS - 1, 1)
        for u in range(NT):
            add_back(QUADS - 1, u)
        for u in range(NT, 2 * NT):
            add_back(QUADS - 1, u)
        dve.wait_ge(sem("f_sq"), 2 * NT)
        op(v.tensor_tensor(ss[:, :], ssc[:, :, 0], ssc[:, :, 1], ALU.add))
        v.tensor_scalar(ms[:, :], ss[:, :], 1.0 / D, RMS_EPS, ALU.mult, ALU.add).then_inc(sem("f_ms"), 1)
        dve.wait_ge(sem("f_root"), 1)
        v.reciprocal(rstd[:, :], root[:, :]).then_inc(sem("f_rstd"), 1)
        dve.wait_ge(sem("f_rstd"), 1)
        for t, c0 in ((0, 0), (1, 512), (2, 512)):
            n = TILES[t][1]
            v.scalar_tensor_tensor(x_tok[0:n, t, c0:D], x_tok[0:n, t, c0:D], rstd[0:n, t:t + 1], gfb[0:n, c0:D],
                                   ALU.mult, ALU.mult).then_inc(sem("y_done"), 1)

    ctx.close()


_INS = ['x_prompt', 'x_sample', 'state_pool', 'state_conv', 'state_sconv', 'norm1_g', 'w_in', 'pool_w', 'pool_scale',
        'conf_dw', 'conf_dw_b', 'conf_ln_g', 'conf_ln_b', 'sconv_w', 'sgu_ln_g', 'sgu_ln_b', 'sgu_ws', 'sgu_b',
        'w_branch', 'w_out', 'norm2_g', 'router_g', 'router_g_b', 'router_e', 'router_e_b', 'w_gate', 'w_up',
        'w_down', 'final_g']
_OUTS = [('y_prompt', (1, 256, 1024)), ('y_sample', (8, 8, 1024)), ('pool_p', (1, 1, 15, 256)),
         ('conv_p', (1, 1, 30, 256)), ('sconv_p', (1, 1, 2, 256)), ('sguv_p', (1, 1, 128, 256)),
         ('pool_s', (1, 8, 15, 256)), ('conv_s', (1, 8, 30, 256)), ('sconv_s', (1, 8, 2, 256)),
         ('sguv_s', (1, 8, 8, 256))]


def kernel(**inputs):
    import numpy as _np
    import concourse.bacc as _bacc
    from concourse import mybir as _mybir
    from concourse.bass_utils import run_bass_kernel_spmd as _run

    nc = _bacc.Bacc("TRN2", target_bir_lowering=False, num_devices=1)
    arrays, ins, outs = {}, {}, {}
    for name in _INS:
        x = _np.ascontiguousarray(inputs[name])
        arrays["in_" + name] = x
        ins[name] = nc.dram_tensor("in_" + name, x.shape, _mybir.dt.from_np(x.dtype), kind="ExternalInput").ap()
    for name, shape in _OUTS:
        outs[name] = nc.dram_tensor("out_" + name, shape, _mybir.dt.float32, kind="ExternalOutput").ap()
    build(nc, ins, outs)
    r = _run(nc, [arrays], core_ids=[0])
    return tuple(r.results[0]["out_" + name] for name, _ in _OUTS)
```
